# Optimizing a Trainium2 kernel written in Bass

```python
import math
import jax, jax.numpy as jnp
from jax import lax
import numpy as np

D_MODEL = 1024
BATCH = 1
SEQ = 256
DEPTH = 2

CHUNK = 64
N_HEADS = 8
N_KV_HEADS = 2
HEAD_DIM = 64
ATTN_WIDTH = N_HEADS * HEAD_DIM
ROPE_DIM = HEAD_DIM // 4
ROPE_THETA = 500000.0
N_IDX_HEADS = 4
IDX_DIM = 64
TOPK_MAX = 256
Q_BLOCK = 128
SGU_CHUNK = 128
SGU_GROUPS = 8
SGU_WIDTH = D_MODEL - ATTN_WIDTH
SGU_GROUP_DIM = SGU_WIDTH // SGU_GROUPS
D_FF = -(-(8 * D_MODEL) // (3 * 256)) * 256
PLE_DIM = 256
ALPHA = (2 * DEPTH) ** 0.25
BETA = (8 * DEPTH) ** -0.25
LN_EPS = 1e-5

Q_COLS = N_HEADS * HEAD_DIM
KV_COLS = N_KV_HEADS * HEAD_DIM
IQ_COLS = N_IDX_HEADS * IDX_DIM
IK_COLS = IDX_DIM
IW_COLS = N_IDX_HEADS
IN_SPLITS = (Q_COLS, KV_COLS, KV_COLS, IQ_COLS, IK_COLS, IW_COLS, SGU_WIDTH, SGU_WIDTH)
IN_COLS = Q_COLS + 2 * KV_COLS + IQ_COLS + IK_COLS + IW_COLS + 2 * SGU_WIDTH


def layer_norm(x, g, b):
    xf = x.astype(jnp.float32)
    mu = jnp.mean(xf, axis=-1, keepdims=True)
    var = jnp.mean(jnp.square(xf - mu), axis=-1, keepdims=True)
    y = (xf - mu) * lax.rsqrt(var + LN_EPS)
    return (y * g.astype(jnp.float32) + b.astype(jnp.float32)).astype(x.dtype)

def partial_rope(x, pos):
    half = ROPE_DIM // 2
    inv = ROPE_THETA ** (-2.0 * jnp.arange(half, dtype=jnp.float32) / ROPE_DIM)
    ang = pos.astype(jnp.float32)[..., None] * inv
    cos = jnp.cos(ang)[:, :, None, :]
    sin = jnp.sin(ang)[:, :, None, :]
    xr = x[..., :ROPE_DIM].astype(jnp.float32)
    x1, x2 = xr[..., :half], xr[..., half:]
    rot = jnp.concatenate([x1 * cos - x2 * sin, x2 * cos + x1 * sin], axis=-1)
    return jnp.concatenate([rot.astype(x.dtype), x[..., ROPE_DIM:]], axis=-1)

def dsa_attention(q, k, v, qi, ki, wi):
    B, S = q.shape[0], q.shape[1]
    topk = min(TOPK_MAX, S // 4)
    nb = S // Q_BLOCK
    G = N_KV_HEADS
    R = N_HEADS // N_KV_HEADS
    key_chunk = jnp.arange(S) // CHUNK

    def to_blocks(a):
        return jnp.moveaxis(a.reshape((B, nb, Q_BLOCK) + a.shape[2:]), 1, 0)

    q_b = to_blocks(q.reshape(B, S, G, R, HEAD_DIM))
    qi_b = to_blocks(qi)
    wi_b = to_blocks(wi)
    t_b = jnp.arange(S).reshape(nb, Q_BLOCK)

    def block(args):
        qb, qib, wib, tb = args
        q_chunk = tb // CHUNK
        allowed = key_chunk[None, :] <= q_chunk[:, None]
        logits = jnp.einsum('bqhd,bsd->bqhs', qib, ki)
        score = jnp.einsum('bqhs,bqh->bqs', jax.nn.relu(logits), wib).astype(jnp.float32)
        score = jnp.where(allowed[None], score, -jnp.inf)
        _, idx = lax.top_k(score, topk)
        k_sel = jax.vmap(lambda kb, ib: kb[ib])(k, idx)
        v_sel = jax.vmap(lambda vb, ib: vb[ib])(v, idx)
        valid = key_chunk[idx] <= q_chunk[None, :, None]
        s = jnp.einsum('bqgrd,bqkgd->bqgrk', qb, k_sel).astype(jnp.float32) * (HEAD_DIM ** -0.5)
        s = jnp.where(valid[:, :, None, None, :], s, -jnp.inf)
        pr = jax.nn.softmax(s, axis=-1).astype(v.dtype)
        return jnp.einsum('bqgrk,bqkgd->bqgrd', pr, v_sel)

    out = lax.map(block, (q_b, qi_b, wi_b, t_b))
    return jnp.moveaxis(out, 0, 1).reshape(B, S, ATTN_WIDTH)

def spatial_gating(u, v, w_s, b_s, g, bta):
    B, S = u.shape[0], u.shape[1]
    v = layer_norm(v, g, bta)
    nc = S // SGU_CHUNK
    vb = v.reshape(B, nc, SGU_CHUNK, SGU_GROUPS, SGU_GROUP_DIM)
    tri = jnp.tril(jnp.ones((SGU_CHUNK, SGU_CHUNK), dtype=bool))
    w = jnp.where(tri[None], w_s, jnp.zeros_like(w_s))
    mixed = jnp.einsum('gts,bcsgd->bctgd', w, vb) + jnp.swapaxes(b_s, 0, 1)[None, None, :, :, None]
    return u * mixed.reshape(B, S, SGU_WIDTH)

def first_inputs(seed: int = 0) -> dict:
    key = jax.random.key(seed)
    ks = jax.random.split(key, 20)

    def nrm(k, shape, scale):
        return jax.random.normal(k, shape, jnp.float32) * scale

    x = nrm(ks[0], (BATCH, SEQ, D_MODEL), 1.0)
    p = nrm(ks[1], (DEPTH, BATCH, SEQ, PLE_DIM), 1.0)
    start = jax.random.randint(ks[2], (BATCH, 1), 0, 64, dtype=jnp.int32) * CHUNK
    positions = (start + jnp.arange(SEQ, dtype=jnp.int32)[None, :]).astype(jnp.int32)
    return {
        "x": x,
        "p": p,
        "positions": positions,
        "w_in": nrm(ks[3], (DEPTH, D_MODEL, IN_COLS), D_MODEL ** -0.5),
        "w_o": nrm(ks[4], (DEPTH, D_MODEL, D_MODEL), BETA * D_MODEL ** -0.5),
        "ln1_g": 1.0 + nrm(ks[5], (DEPTH, D_MODEL), 0.02),
        "ln1_b": nrm(ks[6], (DEPTH, D_MODEL), 0.02),
        "ln2_g": 1.0 + nrm(ks[7], (DEPTH, D_MODEL), 0.02),
        "ln2_b": nrm(ks[8], (DEPTH, D_MODEL), 0.02),
        "sgu_w": nrm(ks[9], (DEPTH, SGU_GROUPS, SGU_CHUNK, SGU_CHUNK), SGU_CHUNK ** -0.5),
        "sgu_b": 1.0 + nrm(ks[10], (DEPTH, SGU_GROUPS, SGU_CHUNK), 0.02),
        "sgu_ln_g": 1.0 + nrm(ks[11], (DEPTH, SGU_WIDTH), 0.02),
        "sgu_ln_b": nrm(ks[12], (DEPTH, SGU_WIDTH), 0.02),
        "w_ffn_in": nrm(ks[13], (DEPTH, D_MODEL, 2 * D_FF), D_MODEL ** -0.5),
        "w_ffn_out": nrm(ks[14], (DEPTH, D_FF, D_MODEL), BETA * D_FF ** -0.5),
        "w_ple": nrm(ks[15], (DEPTH, PLE_DIM, D_MODEL), PLE_DIM ** -0.5),
        "w_ple_gate": nrm(ks[16], (DEPTH, D_MODEL, D_MODEL), D_MODEL ** -0.5),
    }

def first_block(x, p, positions, w_in, w_o, ln1_g, ln1_b, ln2_g, ln2_b, sgu_w, sgu_b,
              sgu_ln_g, sgu_ln_b, w_ffn_in, w_ffn_out, w_ple, w_ple_gate):
    B, S = x.shape[0], x.shape[1]
    split_points = [int(o) for o in np.cumsum(IN_SPLITS)[:-1]]
    for i in range(DEPTH):
        h = x @ w_in[i]
        q, k, v, qi, ki, wi, u, vs = jnp.split(h, split_points, axis=-1)
        q = partial_rope(q.reshape(B, S, N_HEADS, HEAD_DIM), positions)
        k = partial_rope(k.reshape(B, S, N_KV_HEADS, HEAD_DIM), positions)
        v = v.reshape(B, S, N_KV_HEADS, HEAD_DIM)
        qi = partial_rope(qi.reshape(B, S, N_IDX_HEADS, IDX_DIM), positions)
        ki = partial_rope(ki.reshape(B, S, 1, IDX_DIM), positions)[:, :, 0]
        wi = wi * ((N_IDX_HEADS * IDX_DIM) ** -0.5)
        a_out = dsa_attention(q, k, v, qi, ki, wi)
        b_out = spatial_gating(jax.nn.gelu(u), jax.nn.gelu(vs), sgu_w[i], sgu_b[i],
                               sgu_ln_g[i], sgu_ln_b[i])
        mix = jnp.concatenate([a_out, b_out], axis=-1) @ w_o[i]
        x = layer_norm(ALPHA * x + mix, ln1_g[i], ln1_b[i])
        gate, up = jnp.split(x @ w_ffn_in[i], 2, axis=-1)
        ffn = (jax.nn.silu(gate) * up) @ w_ffn_out[i]
        ple = (p[i] @ w_ple[i]) * jax.nn.sigmoid(x @ w_ple_gate[i])
        x = layer_norm(ALPHA * x + ffn + ple, ln2_g[i], ln2_b[i])
    return x


ROPE_THETA_2 = 10000.0
NORM_EPS = 1e-6
NEG_INF = -1e30
D_FF_2 = 4 * D_MODEL
MAX_POS_OFFSET = 4096

MLA_HEADS = 8
MLA_Q_RANK = 384
MLA_KV_RANK = 256
MLA_NOPE = 64
MLA_ROPE = 32
MLA_V = 64

DIL_CONFIGS = ((128, 1), (512, 4), (2048, 16))
DIL_GROUPS = len(DIL_CONFIGS)
DIL_HEADS = 4

DIFF_HEADS = 4
DIFF_DIM = 64

MOBA_HEADS = 8
MOBA_BLOCK = 256
MOBA_TOPK = 3
MOBA_Q_CHUNK = 32

N_EVEN = (DEPTH + 1) // 2
N_ODD = DEPTH // 2

EVEN_IN = MLA_Q_RANK + MLA_KV_RANK + MLA_ROPE + 3 * DIL_GROUPS * DIL_HEADS * HEAD_DIM
EVEN_OUT = MLA_HEADS * MLA_V + DIL_HEADS * HEAD_DIM
ODD_IN = 3 * DIFF_HEADS * 2 * DIFF_DIM + 3 * MOBA_HEADS * HEAD_DIM
ODD_OUT = DIFF_HEADS * 2 * DIFF_DIM + MOBA_HEADS * HEAD_DIM


def rms_norm(x, w):
    xf = x.astype(jnp.float32)
    y = xf * lax.rsqrt(jnp.mean(xf * xf, axis=-1, keepdims=True) + NORM_EPS)
    return (y * w.astype(jnp.float32)).astype(x.dtype)

def apply_rope(x, positions):
    half = x.shape[-1] // 2
    inv_freq = ROPE_THETA_2 ** (-jnp.arange(half, dtype=jnp.float32) / half)
    ang = positions.astype(jnp.float32)[:, :, None] * inv_freq
    bshape = ang.shape[:2] + (1,) * (x.ndim - 3) + (half,)
    cos = jnp.cos(ang).reshape(bshape)
    sin = jnp.sin(ang).reshape(bshape)
    xf = x.astype(jnp.float32)
    x1, x2 = xf[..., :half], xf[..., half:]
    return jnp.concatenate([x1 * cos - x2 * sin, x2 * cos + x1 * sin], axis=-1).astype(x.dtype)

def dense_causal_attention(q, k, v):
    b, s, h, dk = q.shape
    nq = s // Q_BLOCK
    scale = dk ** -0.5
    qb = q.reshape(b, nq, Q_BLOCK, h, dk).transpose(1, 0, 2, 3, 4)
    kpos = jnp.arange(s)

    def one_block(args):
        i, qi = args
        sc = jnp.einsum('bqhd,bkhd->bhqk', qi, k, preferred_element_type=jnp.float32) * scale
        qpos = i * Q_BLOCK + jnp.arange(Q_BLOCK)
        sc = jnp.where(qpos[:, None] >= kpos[None, :], sc, NEG_INF)
        p = jax.nn.softmax(sc, axis=-1)
        return jnp.einsum('bhqk,bkhe->bqhe', p.astype(v.dtype), v)

    out = lax.map(one_block, (jnp.arange(nq), qb))
    return out.transpose(1, 0, 2, 3, 4).reshape(b, s, h, v.shape[-1])

def diff_causal_attention(q, k, v, lam):
    b, s, h, _, d = q.shape
    nq = s // Q_BLOCK
    scale = d ** -0.5
    qb = q.reshape(b, nq, Q_BLOCK, h, 2, d).transpose(1, 0, 2, 3, 4, 5)
    kpos = jnp.arange(s)

    def one_block(args):
        i, qi = args
        sc = jnp.einsum('bqhmd,bkhmd->bmhqk', qi, k, preferred_element_type=jnp.float32) * scale
        qpos = i * Q_BLOCK + jnp.arange(Q_BLOCK)
        sc = jnp.where(qpos[:, None] >= kpos[None, :], sc, NEG_INF)
        p = jax.nn.softmax(sc, axis=-1)
        pd = p[:, 0] - lam * p[:, 1]
        return jnp.einsum('bhqk,bkhe->bqhe', pd.astype(v.dtype), v)

    out = lax.map(one_block, (jnp.arange(nq), qb))
    return out.transpose(1, 0, 2, 3, 4).reshape(b, s, h, v.shape[-1])

def sliding_window_lse(q, k, v, window):
    n, l, h, d = q.shape
    blk = window
    lp = -(-l // blk) * blk
    pad = ((0, 0), (0, lp - l), (0, 0), (0, 0))
    q, k, v = jnp.pad(q, pad), jnp.pad(k, pad), jnp.pad(v, pad)
    nb = lp // blk
    qb = q.reshape(n, nb, blk, h, d)
    kb = k.reshape(n, nb, blk, h, d)
    vb = v.reshape(n, nb, blk, h, d)
    prev_pad = ((0, 0), (1, 0), (0, 0), (0, 0), (0, 0))
    kk = jnp.concatenate([jnp.pad(kb[:, :-1], prev_pad), kb], axis=2)
    vv = jnp.concatenate([jnp.pad(vb[:, :-1], prev_pad), vb], axis=2)
    sc = jnp.einsum('nbqhd,nbkhd->nbhqk', qb, kk, preferred_element_type=jnp.float32) * d ** -0.5
    qloc = jnp.arange(blk) + blk
    kloc = jnp.arange(2 * blk)
    rel = qloc[:, None] - kloc[None, :]
    band = (rel >= 0) & (rel <= window)
    kabs = jnp.arange(nb)[:, None, None] * blk + kloc[None, None, :] - blk
    mask = band[None] & (kabs >= 0)
    sc = jnp.where(mask[None, :, None], sc, NEG_INF)
    lse = jax.nn.logsumexp(sc, axis=-1)
    p = jnp.exp(sc - lse[..., None])
    out = jnp.einsum('nbhqk,nbkhd->nbqhd', p.astype(v.dtype), vv).reshape(n, lp, h, d)[:, :l]
    lse = lse.transpose(0, 1, 3, 2).reshape(n, lp, h)[:, :l]
    return out, lse

def dilated_group(q, k, v, window, dilation):
    b, s, h, d = q.shape
    m = s // dilation

    def split(t):
        return t.reshape(b, m, dilation, h, d).transpose(0, 2, 1, 3, 4).reshape(b * dilation, m, h, d)

    out, lse = sliding_window_lse(split(q), split(k), split(v), window // dilation)
    out = out.reshape(b, dilation, m, h, d).transpose(0, 2, 1, 3, 4).reshape(b, s, h, d)
    lse = lse.reshape(b, dilation, m, h).transpose(0, 2, 1, 3).reshape(b, s, h)
    return out, lse

def dilated_mixture(q, k, v):
    outs, lses = [], []
    for g, (w, r) in enumerate(DIL_CONFIGS):
        o, l = dilated_group(q[:, :, g], k[:, :, g], v[:, :, g], w, r)
        outs.append(o)
        lses.append(l)
    alpha = jax.nn.softmax(jnp.stack(lses), axis=0)
    out = jnp.sum(alpha[..., None] * jnp.stack(outs).astype(jnp.float32), axis=0)
    return out.astype(q.dtype)

def moba_attention(q, k, v):
    b, s, h, d = q.shape
    blk = MOBA_BLOCK
    sp = -(-s // blk) * blk
    nb = sp // blk
    scale = d ** -0.5
    pad = ((0, 0), (0, sp - s), (0, 0), (0, 0))
    qp, kp, vp = jnp.pad(q, pad), jnp.pad(k, pad), jnp.pad(v, pad)
    qb = qp.reshape(b, nb, blk, h, d)
    kb = kp.reshape(b, nb, blk, h, d)
    vb = vp.reshape(b, nb, blk, h, d)

    s_own = jnp.einsum('bnqhd,bnkhd->bnhqk', qb, kb, preferred_element_type=jnp.float32) * scale
    s_own = jnp.where(jnp.tril(jnp.ones((blk, blk), dtype=bool)), s_own, NEG_INF)
    lse_own = jax.nn.logsumexp(s_own, axis=-1)
    o_own = jnp.einsum('bnhqk,bnkhd->bnqhd', jnp.exp(s_own - lse_own[..., None]).astype(v.dtype), vb)
    o_own = o_own.reshape(b, sp, h, d)[:, :s].astype(jnp.float32)
    lse_own = lse_own.transpose(0, 1, 3, 2).reshape(b, sp, h)[:, :s]

    kmean = jnp.mean(kb.astype(jnp.float32), axis=2)
    gate = jnp.einsum('bshd,bnhd->bhsn', q.astype(jnp.float32), kmean)
    qblk = jnp.arange(s) // blk
    past = jnp.arange(nb)[None, :] < qblk[:, None]
    gate = jnp.where(past, gate, NEG_INF)
    n_sel = min(MOBA_TOPK, nb)
    _, idx = lax.top_k(gate, n_sel)
    valid = idx < qblk[None, None, :, None]

    kbh = kb.transpose(0, 3, 1, 2, 4)
    vbh = vb.transpose(0, 3, 1, 2, 4)
    nc = s // MOBA_Q_CHUNK
    qc_all = q.transpose(0, 2, 1, 3).reshape(b, h, nc, MOBA_Q_CHUNK, d).transpose(2, 0, 1, 3, 4)
    ic_all = idx.reshape(b, h, nc, MOBA_Q_CHUNK, n_sel).transpose(2, 0, 1, 3, 4)
    vc_all = valid.reshape(b, h, nc, MOBA_Q_CHUNK, n_sel).transpose(2, 0, 1, 3, 4)
    bidx = jnp.arange(b)[:, None, None, None]
    hidx = jnp.arange(h)[None, :, None, None]

    def chunk(args):
        qc, ic, vc = args
        kg = kbh[bidx, hidx, ic]
        vg = vbh[bidx, hidx, ic]
        sc = jnp.einsum('bhqd,bhqjkd->bhqjk', qc, kg, preferred_element_type=jnp.float32) * scale
        sc = jnp.where(vc[..., None], sc, NEG_INF).reshape(b, h, MOBA_Q_CHUNK, n_sel * blk)
        lse = jax.nn.logsumexp(sc, axis=-1)
        p = jnp.exp(sc - lse[..., None]).reshape(b, h, MOBA_Q_CHUNK, n_sel, blk)
        o = jnp.einsum('bhqjk,bhqjkd->bhqd', p.astype(vg.dtype), vg)
        return o, lse

    o_sel, lse_sel = lax.map(chunk, (qc_all, ic_all, vc_all))
    o_sel = o_sel.transpose(1, 0, 3, 2, 4).reshape(b, s, h, d).astype(jnp.float32)
    lse_sel = lse_sel.transpose(1, 0, 3, 2).reshape(b, s, h)

    lse_tot = jnp.logaddexp(lse_own, lse_sel)
    out = (jnp.exp(lse_own - lse_tot)[..., None] * o_own
           + jnp.exp(lse_sel - lse_tot)[..., None] * o_sel)
    return out.astype(q.dtype)

def even_mixer(h, positions, w_in, w_out, q_lat_norm, kv_lat_norm, w_uq, w_ukv,
               mla_qn, mla_kn, dil_qn, dil_kn):
    b, s, _ = h.shape
    u = h @ w_in
    o1 = MLA_Q_RANK
    o2 = o1 + MLA_KV_RANK
    o3 = o2 + MLA_ROPE
    c_q, c_kv, k_r, u_dil = u[..., :o1], u[..., o1:o2], u[..., o2:o3], u[..., o3:]

    q = jnp.einsum('bsr,rhd->bshd', rms_norm(c_q, q_lat_norm), w_uq)
    kv = jnp.einsum('bsr,rhd->bshd', rms_norm(c_kv, kv_lat_norm), w_ukv)
    k_nope, v_a = kv[..., :MLA_NOPE], kv[..., MLA_NOPE:]
    k_rope = jnp.broadcast_to(k_r[:, :, None, :], (b, s, MLA_HEADS, MLA_ROPE))
    k = jnp.concatenate([k_nope, k_rope], axis=-1)
    q, k = rms_norm(q, mla_qn), rms_norm(k, mla_kn)
    q = jnp.concatenate([q[..., :MLA_NOPE], apply_rope(q[..., MLA_NOPE:], positions)], axis=-1)
    k = jnp.concatenate([k[..., :MLA_NOPE], apply_rope(k[..., MLA_NOPE:], positions)], axis=-1)
    o_a = dense_causal_attention(q, k, v_a)

    qkv = u_dil.reshape(b, s, 3, DIL_GROUPS, DIL_HEADS, HEAD_DIM)
    qd = apply_rope(rms_norm(qkv[:, :, 0], dil_qn), positions)
    kd = apply_rope(rms_norm(qkv[:, :, 1], dil_kn), positions)
    o_b = dilated_mixture(qd, kd, qkv[:, :, 2])

    o = jnp.concatenate([o_a.reshape(b, s, -1), o_b.reshape(b, s, -1)], axis=-1)
    return o @ w_out

def odd_mixer(h, positions, w_in, w_out, diff_qn, diff_kn, diff_lambda, diff_subln,
              moba_qn, moba_kn, lam_init):
    b, s, _ = h.shape
    u = h @ w_in
    nqk = DIFF_HEADS * 2 * DIFF_DIM

    qc = u[..., :nqk].reshape(b, s, DIFF_HEADS, 2, DIFF_DIM)
    kc = u[..., nqk:2 * nqk].reshape(b, s, DIFF_HEADS, 2, DIFF_DIM)
    vc = u[..., 2 * nqk:3 * nqk].reshape(b, s, DIFF_HEADS, 2 * DIFF_DIM)
    qc = apply_rope(rms_norm(qc, diff_qn), positions)
    kc = apply_rope(rms_norm(kc, diff_kn), positions)
    lv = diff_lambda.astype(jnp.float32)
    lam = jnp.exp(jnp.sum(lv[0] * lv[1])) - jnp.exp(jnp.sum(lv[2] * lv[3])) + lam_init
    o_c = diff_causal_attention(qc, kc, vc, lam)
    o_c = rms_norm(o_c, diff_subln) * (1.0 - lam_init)

    m = u[..., 3 * nqk:].reshape(b, s, 3, MOBA_HEADS, HEAD_DIM)
    qm = apply_rope(rms_norm(m[:, :, 0], moba_qn), positions)
    km = apply_rope(rms_norm(m[:, :, 1], moba_kn), positions)
    o_d = moba_attention(qm, km, m[:, :, 2])

    o = jnp.concatenate([o_c.reshape(b, s, -1), o_d.reshape(b, s, -1)], axis=-1)
    return o @ w_out

def squared_relu_mlp(h, w1, w2):
    a = jax.nn.relu(h @ w1)
    return (a * a) @ w2

def modulate(xn, shift, scale):
    return xn * (1.0 + scale[:, None, :]) + shift[:, None, :]

def second_inputs(seed: int = 0) -> dict:
    key = jax.random.key(seed)
    ks = jax.random.split(key, 27)
    f32 = jnp.float32

    def nrm(k, shape, scale):
        return jax.random.normal(k, shape, f32) * scale

    def gain(k, shape):
        return 1.0 + 0.1 * jax.random.normal(k, shape, f32)

    offset = jax.random.randint(ks[2], (BATCH, 1), 0, MAX_POS_OFFSET, dtype=jnp.int32)
    positions = offset + jnp.arange(SEQ, dtype=jnp.int32)[None, :]
    return {
        "x": nrm(ks[0], (BATCH, SEQ, D_MODEL), 1.0),
        "c": nrm(ks[1], (BATCH, D_MODEL), 1.0),
        "positions": positions,
        "ada_w": nrm(ks[3], (DEPTH, D_MODEL, 6 * D_MODEL), 0.5 * D_MODEL ** -0.5),
        "ada_b": nrm(ks[4], (DEPTH, 6 * D_MODEL), 0.02),
        "norm_mix": gain(ks[5], (DEPTH, D_MODEL)),
        "norm_mlp": gain(ks[6], (DEPTH, D_MODEL)),
        "mlp_w1": nrm(ks[7], (DEPTH, D_MODEL, D_FF_2), D_MODEL ** -0.5),
        "mlp_w2": nrm(ks[8], (DEPTH, D_FF_2, D_MODEL), D_FF_2 ** -0.5),
        "even_w_in": nrm(ks[9], (N_EVEN, D_MODEL, EVEN_IN), D_MODEL ** -0.5),
        "even_w_out": nrm(ks[10], (N_EVEN, EVEN_OUT, D_MODEL), EVEN_OUT ** -0.5),
        "mla_q_lat_norm": gain(ks[11], (N_EVEN, MLA_Q_RANK)),
        "mla_kv_lat_norm": gain(ks[12], (N_EVEN, MLA_KV_RANK)),
        "mla_w_uq": nrm(ks[13], (N_EVEN, MLA_Q_RANK, MLA_HEADS, MLA_NOPE + MLA_ROPE), MLA_Q_RANK ** -0.5),
        "mla_w_ukv": nrm(ks[14], (N_EVEN, MLA_KV_RANK, MLA_HEADS, MLA_NOPE + MLA_V), MLA_KV_RANK ** -0.5),
        "mla_q_norm": gain(ks[15], (N_EVEN, MLA_NOPE + MLA_ROPE)),
        "mla_k_norm": gain(ks[16], (N_EVEN, MLA_NOPE + MLA_ROPE)),
        "dil_q_norm": gain(ks[17], (N_EVEN, HEAD_DIM)),
        "dil_k_norm": gain(ks[18], (N_EVEN, HEAD_DIM)),
        "odd_w_in": nrm(ks[19], (N_ODD, D_MODEL, ODD_IN), D_MODEL ** -0.5),
        "odd_w_out": nrm(ks[20], (N_ODD, ODD_OUT, D_MODEL), ODD_OUT ** -0.5),
        "diff_q_norm": gain(ks[21], (N_ODD, DIFF_DIM)),
        "diff_k_norm": gain(ks[22], (N_ODD, DIFF_DIM)),
        "diff_lambda": nrm(ks[23], (N_ODD, 4, DIFF_DIM), 0.1),
        "diff_subln": gain(ks[24], (N_ODD, 2 * DIFF_DIM)),
        "moba_q_norm": gain(ks[25], (N_ODD, HEAD_DIM)),
        "moba_k_norm": gain(ks[26], (N_ODD, HEAD_DIM)),
    }

def second_block(x, c, positions, ada_w, ada_b, norm_mix, norm_mlp, mlp_w1, mlp_w2,
              even_w_in, even_w_out, mla_q_lat_norm, mla_kv_lat_norm, mla_w_uq, mla_w_ukv,
              mla_q_norm, mla_k_norm, dil_q_norm, dil_k_norm,
              odd_w_in, odd_w_out, diff_q_norm, diff_k_norm, diff_lambda, diff_subln,
              moba_q_norm, moba_k_norm):
    cond = jax.nn.silu(c.astype(jnp.float32)).astype(x.dtype)
    for layer in range(DEPTH):
        mod = cond @ ada_w[layer] + ada_b[layer]
        sh1, sc1, g1, sh2, sc2, g2 = jnp.split(mod, 6, axis=-1)
        h = modulate(rms_norm(x, norm_mix[layer]), sh1, sc1)
        i = layer // 2
        if layer % 2 == 0:
            y = even_mixer(h, positions, even_w_in[i], even_w_out[i], mla_q_lat_norm[i],
                           mla_kv_lat_norm[i], mla_w_uq[i], mla_w_ukv[i], mla_q_norm[i],
                           mla_k_norm[i], dil_q_norm[i], dil_k_norm[i])
        else:
            lam_init = 0.8 - 0.6 * math.exp(-0.3 * layer)
            y = odd_mixer(h, positions, odd_w_in[i], odd_w_out[i], diff_q_norm[i], diff_k_norm[i],
                          diff_lambda[i], diff_subln[i], moba_q_norm[i], moba_k_norm[i], lam_init)
        x = x + g1[:, None, :] * y
        h = modulate(rms_norm(x, norm_mlp[layer]), sh2, sc2)
        x = x + g2[:, None, :] * squared_relu_mlp(h, mlp_w1[layer], mlp_w2[layer])
    return x


def setup_inputs(seed=0):
    out = dict(first_inputs(seed))
    for name, value in second_inputs(seed + 1).items():
        if name != "x":
            out[name + "_2"] = value
    return out


def reference(
    x, p, positions, w_in, w_o, ln1_g, ln1_b, ln2_g, ln2_b, sgu_w, sgu_b, sgu_ln_g, sgu_ln_b,
    w_ffn_in, w_ffn_out, w_ple, w_ple_gate, c_2, positions_2, ada_w_2, ada_b_2, norm_mix_2,
    norm_mlp_2, mlp_w1_2, mlp_w2_2, even_w_in_2, even_w_out_2, mla_q_lat_norm_2,
    mla_kv_lat_norm_2, mla_w_uq_2, mla_w_ukv_2, mla_q_norm_2, mla_k_norm_2, dil_q_norm_2,
    dil_k_norm_2, odd_w_in_2, odd_w_out_2, diff_q_norm_2, diff_k_norm_2, diff_lambda_2,
    diff_subln_2, moba_q_norm_2, moba_k_norm_2,
):
    x = first_block(
        x, p, positions, w_in, w_o, ln1_g, ln1_b, ln2_g, ln2_b, sgu_w, sgu_b, sgu_ln_g,
        sgu_ln_b, w_ffn_in, w_ffn_out, w_ple, w_ple_gate,
    )
    return second_block(
        x, c_2, positions_2, ada_w_2, ada_b_2, norm_mix_2, norm_mlp_2, mlp_w1_2, mlp_w2_2,
        even_w_in_2, even_w_out_2, mla_q_lat_norm_2, mla_kv_lat_norm_2, mla_w_uq_2, mla_w_ukv_2,
        mla_q_norm_2, mla_k_norm_2, dil_q_norm_2, dil_k_norm_2, odd_w_in_2, odd_w_out_2,
        diff_q_norm_2, diff_k_norm_2, diff_lambda_2, diff_subln_2, moba_q_norm_2, moba_k_norm_2,
    )


_drawn_inputs = setup_inputs


def setup_inputs(seed=0):
    import zlib

    import numpy as np

    out = dict(_drawn_inputs(seed))
    spreads = {}
    factors = {'sgu_b': 8.0,
     'sgu_ln_g': 8.0,
     'sgu_ln_b': 8.0,
     'norm_mix_2': 3.071,
     'mla_q_lat_norm_2': 8.0,
     'mla_kv_lat_norm_2': 5.66,
     'mla_q_norm_2': 8.0,
     'mla_k_norm_2': 8.0,
     'dil_q_norm_2': 8.0,
     'dil_k_norm_2': 8.0,
     'diff_q_norm_2': 8.0,
     'diff_k_norm_2': 8.0,
     'diff_lambda_2': 8.0,
     'diff_subln_2': 5.016,
     'moba_q_norm_2': 8.0,
     'moba_k_norm_2': 8.0}
    for name, (base, spread) in spreads.items():
        noise = np.random.default_rng([zlib.crc32(name.encode()), seed]).standard_normal(out[name].shape)
        drawn = base * np.exp(spread * noise) if base else spread * noise
        out[name] = __import__('jax').numpy.asarray(drawn.astype(out[name].dtype))
    for name, factor in factors.items():
        out[name] = (out[name] * factor).astype(out[name].dtype)
    return out
```

```python
import math
from contextlib import ExitStack

import numpy as np

import concourse.bass as bass
from concourse import mybir

F32 = mybir.dt.float32
BF16 = mybir.dt.bfloat16
I32 = mybir.dt.int32
ALU = mybir.AluOpType
ACT = mybir.ActivationFunctionType
X_ = mybir.AxisListType.X

S, D = 256, 1024
SLOT = 2048
NSLOT = 6
DFF = 2816
ALPHA = 4 ** 0.25
BIG = 1e30
LAM = 0.8 - 0.6 * math.exp(-0.3)

C_ID, C_CM, C_TRI, C_INV, C_HPI, C_MH, C_END = 0, 128, 256, 384, 424, 425, 426
B_ID, B_TRI, B_UP, B_TRI4, B_M4, B_TRI16, B_M16 = range(7)
SMALL = [("mla_q_lat_norm_2", 384), ("mla_kv_lat_norm_2", 256), ("mla_q_norm_2", 96), ("mla_k_norm_2", 96),
         ("dil_q_norm_2", 64), ("dil_k_norm_2", 64), ("diff_q_norm_2", 64), ("diff_k_norm_2", 64),
         ("diff_subln_2", 128), ("moba_q_norm_2", 64), ("moba_k_norm_2", 64), ("diff_lambda_2", 256)]
NSMALL = sum(n for _, n in SMALL)


def plan():
    out = []
    for i in range(2):
        for a, b in ((0, 512), (512, 1024), (1024, 1092), (1092, 1604), (1604, 2116)):
            out.append(("w_in", i, 1024, [(a, b)]))
        out.append(("sgu_w", i, 128, [(0, 1024)]))
        for c in range(2):
            out.append(("w_o", i, 1024, [(c * 512, c * 512 + 512)]))
        for c in range(2):
            out.append(("w_ple_gate", i, 1024, [(c * 512, c * 512 + 512)]))
            out.append(("w_ple", i, 256, [(c * 512, c * 512 + 512)]))
        for c in range(11):
            out.append(("w_ffn_in", i, 1024, [(c * 256, c * 256 + 256), (DFF + c * 256, DFF + c * 256 + 256)]))
        out.append(("w_ffn_out", i, DFF, [(0, 1024)]))
    for i in range(2):
        for c in range(12):
            out.append(("ada_w_2", i, 1024, [(c * 512, c * 512 + 512)]))
        if i == 0:
            for a, b in ((0, 384), (384, 672), (672, 1056), (1056, 1440), (1440, 1824), (1824, 2208)):
                out.append(("even_w_in_2", 0, 1024, [(a, b)]))
            out.append(("mla_w_uq_2", 0, 384, [(0, 384)]))
            out.append(("mla_w_uq_2", 0, 384, [(384, 768)]))
            out.append(("mla_w_ukv_2", 0, 256, [(h * 128, h * 128 + 64) for h in range(8)]))
            out.append(("mla_w_ukv_2", 0, 256, [(h * 128 + 64, h * 128 + 128) for h in range(8)]))
            for a, b in ((2208, 2592), (2592, 2976)):
                out.append(("even_w_in_2", 0, 1024, [(a, b)]))
            for c in range(2):
                out.append(("even_w_out_2", 0, 768, [(c * 512, c * 512 + 512)]))
        else:
            for c in range(6):
                out.append(("odd_w_in_2", 0, 1024, [(c * 512, c * 512 + 512)]))
            for c in range(2):
                out.append(("odd_w_out_2", 0, 1024, [(c * 512, c * 512 + 512)]))
        for c in range(8):
            out.append(("mlp_w1_2", i, 1024, [(c * 512, c * 512 + 512)]))
        out.append(("mlp_w2_2", i, 4096, [(0, 1024)]))
    return out


def pieces(k, w):
    per = SLOT // w
    kt = k // 128
    return [(a, min(per, kt - a)) for a in range(0, kt, per)]


def width(cols):
    return sum(b - a for a, b in cols)


def total():
    return sum(k * width(cols) for _, _, k, cols in plan())


class Op:
    def __init__(self, eng, f, waits, a, k):
        self.eng, self.f, self.waits, self.a, self.k = eng, f, waits, a, k
        self.used, self.sem, self.val = False, None, 0


class Queue:

    def __init__(self, nc, sem):
        self.nc, self.sem = nc, sem
        self.q = {"pe": [], "dve": [], "act": [], "pool": [], "sp": []}
        self.esem = {e: sem("s_" + e) for e in self.q}
        self.dcount = {}
        self.stores = []

    def add(self, eng, f, waits, *a, **k):
        flat = []
        for w in waits:
            flat.extend(w if isinstance(w, (list, tuple)) else [w])
        op = Op(eng, f, flat, a, k)
        for w in flat:
            w.used = True
        self.q[eng].append(op)
        return op

    def dma(self, eng, name, f, waits, dst, src):
        op = self.add(eng, f, waits, dst, src)
        if name not in self.dcount:
            self.dcount[name] = [self.sem("d_" + name), 0]
        c = self.dcount[name]
        c[1] += 16
        op.sem, op.val = c[0], c[1]
        return op

    def finish(self):
        for e, ops in self.q.items():
            n = 0
            for op in ops:
                if op.sem is None and op.used:
                    n += 1
                    op.val = n

    def emit(self, e, eng):
        seen = {}
        for op in self.q[e]:
            need = {}
            for w in op.waits:
                s = w.sem if w.sem is not None else self.esem[w.eng]
                need[id(s)] = (s, max(w.val, need.get(id(s), (s, 0))[1]))
            for i, (s, v) in need.items():
                if seen.get(i, 0) < v:
                    eng.wait_ge(s, v)
                    seen[i] = v
            ins = op.f(*op.a, **op.k)
            if op.sem is not None:
                ins.then_inc(op.sem, 16)
            elif op.used:
                ins.then_inc(self.esem[e], 1)
        for op in self.stores:
            if op.eng == e:
                eng.wait_ge(op.sem, op.val)


def program(nc, W, xd, xTd, pTd, posd, pos2d, cTd, cstd, cstbd, vecd, sgbd, nrmd, adabd, smalld, out):
    with ExitStack() as ctx:
        def sb(name, shape, dt=F32):
            return ctx.enter_context(nc.sbuf_tensor(name, shape, dt))

        def sem(name):
            return ctx.enter_context(nc.semaphore(name))

        Q = Queue(nc, sem)
        V, A, G, M, Y = nc.vector, nc.scalar, nc.gpsimd, nc.tensor, nc.sync

        def v(f, waits, *a, **k):
            return Q.add("dve", f, waits, *a, **k)

        def s(f, waits, *a, **k):
            return Q.add("act", f, waits, *a, **k)

        def g(f, waits, *a, **k):
            return Q.add("pool", f, waits, *a, **k)

        def m(waits, *a, **k):
            return Q.add("pe", M.matmul, waits, *a, **k)

        ring = sb("ring", [128, NSLOT, SLOT])
        X = sb("X", [128, 2, 1024])
        XT = sb("XT", [128, 8, 256])
        MIX = sb("MIX", [128, 2, 1024])
        H = sb("H", [128, 2, 3072])
        T = sb("T", [128, 32, 256])
        GB = sb("GB", [128, 2, 1024])
        MOD = sb("MOD", [128, 6, 1024])
        MV = sb("MV", [128, 2, 512])
        E = sb("E", [128, 2, 1024])
        PET = sb("PET", [128, 2, 768])
        SCR = sb("SCR", [128, 1024])
        CB = sb("CB", [128, 8, 128])
        NW = sb("NW", [128, 1024])
        PT = sb("PT", [128, 2, 256])
        cst = sb("cst", [128, C_END])
        cstb = sb("cstb", [128, 7 * 128], BF16)
        selb = sb("selb", [128, 2, 256], BF16)
        small = sb("small", [128, NSMALL])
        sgb = sb("sgb", [128, 2, 8])
        posi = sb("posi", [128, 4], I32)
        posf = sb("posf", [128, 4])
        trig = sb("trig", [128, 4, 2, 40])
        COS = sb("COS", [128, 2, 40])
        SIN = sb("SIN", [128, 2, 40])
        cT = sb("cT", [128, 8])
        st = sb("st", [128, 256])
        banks = [ctx.enter_context(nc.psum_tensor(f"ps{i}", [128, 512], F32)) for i in range(8)]

        free = [(b, []) for b in banks]

        def take():
            return free.pop(0)

        def give(bank, ops):
            free.append((bank, list(ops)))

        chunks = plan()
        cur = {"chunk": 0, "slot": 0, "off": 0}
        left = [[] for _ in range(NSLOT)]

        def stream(name):
            nm, _, k, cols = chunks[cur["chunk"]]
            assert nm == name, (nm, name)
            cur["chunk"] += 1
            w = width(cols)
            for a, n in pieces(k, w):
                sl = cur["slot"] % NSLOT
                cur["slot"] += 1
                dst = ring[:, sl, 0:n * w]
                src = W[cur["off"]:cur["off"] + 128 * n * w].rearrange("(p w) -> p w", p=128)
                cur["off"] += 128 * n * w
                ld = Q.dma("sp", f"w{sl}", Y.dma_start, left[sl], dst, src)
                yield a, dst.rearrange("p (k w) -> p k w", k=n), ld, sl

        def linear(name, lhs, deps, w, kt_total):
            ps = [take(), take()]
            last = [None, None]
            for a, view, ld, sl in stream(name):
                for t in range(2):
                    for j in range(view.shape[1]):
                        kt = a + j
                        last[t] = m([ld] + (deps if kt == 0 else []) + (ps[t][1] if kt == 0 else []),
                                    ps[t][0][:, 0:w], lhs(kt, t), view[:, j, :],
                                    start=(kt == 0), stop=(kt == kt_total - 1))
                left[sl] = [last[1]]
            return [(ps[t][0], last[t]) for t in range(2)]

        def linear_long(name, lhs, deps, kt_total):
            ps = [[take(), take()], [take(), take()]]
            last = [[None, None], [None, None]]
            for a, view, ld, sl in stream(name):
                for j in range(view.shape[1]):
                    kt = a + j
                    for t in range(2):
                        for c in range(2):
                            dd = deps(kt) + (ps[t][c][1] if kt == 0 else [])
                            last[t][c] = m([ld] + dd, ps[t][c][0][:, :], lhs(kt, t),
                                           view[:, j, c * 512:c * 512 + 512],
                                           start=(kt == 0), stop=(kt == kt_total - 1))
                left[sl] = [last[1][1]]
            return [[(ps[t][c][0], last[t][c]) for c in range(2)] for t in range(2)]

        ident = cst[:, C_ID:C_ID + 128]
        identb = cstb[:, 0:128]

        def maskb(b):
            return cstb[:, b * 128:b * 128 + 128]

        def pld(name, dst, src, waits=()):
            return Q.dma("pool", name, G.dma_start, list(waits), dst, src)

        l_cst = pld("cst", cst[:, :], cstd[:, :])
        l_pos = pld("pos", posi[:, 0:2], posd)
        l_pos2 = pld("pos2", posi[:, 2:4], pos2d)
        l_xT = Q.dma("act", "xT", A.dma_start, [], XT[:, :, :], xTd.rearrange("p (k n) -> p k n", k=8))
        l_x = Q.dma("act", "x", A.dma_start, [], X[:, :, :], xd[0].rearrange("(t p) d -> p t d", p=128))
        l_cb = pld("cstb", SCR[:, 0:896], cstbd[:, :])
        l_cstb = v(V.tensor_copy, [l_cb], cstb[:, :], SCR[:, 0:896])
        VEC = MOD[:, :, :].rearrange("p a b -> p (a b)")

        def bc(src):
            return src.rearrange("(a n) -> a n", a=1).to_broadcast([128, src.shape[0]])

        l_sgb = pld("sgb", sgb[:, :, :], sgbd.rearrange("p (i g) -> p i g", i=2))
        l_small = pld("small", small[:, :], bc(smalld))
        l_c = pld("c", cT[:, :], cTd[:, :])
        sm = {}
        at = 0
        for nm, n in SMALL:
            sm[nm] = small[:, at:at + n]
            at += n

        w_pf = v(V.tensor_copy, [l_pos, l_pos2], posf[:, :], posi[:, :])
        ang, kk, rr, ab = (trig[:, n, :, :] for n in range(4))
        for t in range(2):
            v(V.tensor_scalar, [w_pf, l_cst], ang[:, t, 0:8], cst[:, C_INV:C_INV + 8], posf[:, t:t + 1], None, ALU.mult)
            w_a = v(V.tensor_scalar, [w_pf], ang[:, t, 8:40], cst[:, C_INV + 8:C_INV + 40], posf[:, 2 + t:3 + t], None,
                    ALU.mult)
        MAGIC = 12582912.0
        C1 = 6.28125
        c2 = 2 * math.pi - C1
        C2 = round(c2 * 2 ** 20) / 2.0 ** 20
        C3 = 2 * math.pi - C1 - C2
        o = v(V.tensor_scalar, [w_a], kk, ang, 1 / (2 * math.pi), MAGIC, ALU.mult, ALU.add)
        o = v(V.tensor_scalar, [o], kk, kk, -MAGIC, None, ALU.add)
        o = v(V.scalar_tensor_tensor, [o], out=rr, in0=kk, scalar=-C1, in1=ang, op0=ALU.mult, op1=ALU.add)
        o = v(V.scalar_tensor_tensor, [o], out=ab, in0=kk, scalar=-C2, in1=rr, op0=ALU.mult, op1=ALU.add)
        o = v(V.scalar_tensor_tensor, [o], out=rr, in0=kk, scalar=-C3, in1=ab, op0=ALU.mult, op1=ALU.add)
        PI = 3.1415925
        w_r = v(V.tensor_scalar, [o], rr, rr, PI, -PI, ALU.min, ALU.max)
        w_ab = v(V.scalar_tensor_tensor, [w_r], out=ab, in0=rr, scalar=-1.0, in1=rr, op0=ALU.mult, op1=ALU.max)
        s(A.activation, [w_r], SIN[:, :, :], rr, ACT.Sin)
        w_trig = s(A.activation, [w_ab], COS[:, :, :], ab, ACT.Sin, bias=cst[:, C_HPI:C_HPI + 1], scale=-1.0)

        def copy(eng, waits, dst, src):
            if eng == "act":
                return s(A.activation, waits, dst, src, ACT.Copy)
            if eng == "dve":
                return v(V.tensor_copy, waits, dst, src)
            return g(G.tensor_copy, waits, dst, src)

        flip = {"n": 0}

        def alt():
            flip["n"] += 1
            return "act" if flip["n"] % 2 else "dve"

        def turn(srcs, deps, dst, rows=128, eng=None):
            out_ops = []
            for a in range(0, len(srcs), 4):
                part = srcs[a:a + 4]
                b, bw = take()
                for j, src in enumerate(part):
                    op = Q.add("pe", M.transpose, (deps + bw) if j == 0 else [],
                               b[0:rows, j * 128:j * 128 + 128], src, ident)
                cp = copy(eng or alt(), [op], dst(a, len(part)),
                          b[0:rows, 0:128 * len(part)].rearrange("p (n q) -> p n q", n=len(part)))
                give(b, [cp])
                out_ops.append(cp)
            return out_ops

        def to_XT(src, n, deps, eng=None):
            ops = []
            for t in range(2):
                ops += turn([src[:, t, k * 128:k * 128 + 128] for k in range(n)], deps[t],
                            lambda a, c, t=t: XT[:, a:a + c, t * 128:t * 128 + 128], eng=eng)
            return ops

        def xt(kt, t):
            return XT[:, kt, t * 128:t * 128 + 128]

        tick = {"n": 0}

        def col(n):
            if tick["n"] + n > 256:
                tick["n"] = 0
            c = tick["n"]
            tick["n"] += n
            return st[:, c:c + n]

        MH = cst[:, C_MH:C_MH + 1]

        def rsqrt(src, waits, scale, eps):
            o1 = g(G.tensor_scalar, waits + [l_cst], src, src, scale, eps, ALU.mult, ALU.add)
            return g(G.tensor_tensor, [o1], src, src, MH.to_broadcast([128, src.shape[1]]), ALU.pow)

        def layer_norm(src, dst, n, gam, bet, waits, vw):
            c = n // 512
            sts = col(6 * c)
            mv = col(2)
            for j in range(c):
                o = v(V.bn_stats, waits, sts[:, 6 * j:6 * j + 6], src[:, j * 512:j * 512 + 512])
            o = v(V.bn_aggr, [o], mv, sts.rearrange("p (c k) -> p c k", k=6))
            r = rsqrt(mv[:, 1:2], [o], 1.0, 1e-5)
            o = v(V.scalar_tensor_tensor, [r] + vw, out=dst, in0=src, scalar=mv[:, 0:1], in1=gam,
                  op0=ALU.subtract, op1=ALU.mult)
            return v(V.scalar_tensor_tensor, [o], out=dst, in0=dst, scalar=mv[:, 1:2], in1=bet,
                     op0=ALU.mult, op1=ALU.add)

        scr_rd = []

        def rope(x, cos, sin, nh, hf, waits, tmp_deps):
            x4 = x.rearrange("p h (a f) -> p h a f", a=2)
            cb = cos.unsqueeze(1).unsqueeze(1).broadcast_to([128, nh, 2, hf])
            sb_ = sin.unsqueeze(1).unsqueeze(1).broadcast_to([128, nh, 2, hf])
            n = nh * 2 * hf
            P4 = SCR[:, 0:n].rearrange("p (h a f) -> p h a f", h=nh, a=2)
            Q4 = SCR[:, 512:512 + n].rearrange("p (h a f) -> p h a f", h=nh, a=2) if n <= 512 else None
            if n > 512:
                raise ValueError("rope too wide")
            o1 = v(V.tensor_tensor, waits + tmp_deps + [w_trig], P4, x4, cb, ALU.mult)
            o2 = v(V.tensor_tensor, [], Q4, x4, sb_, ALU.mult)
            o3 = v(V.tensor_tensor, [o1, o2], x4[:, :, 0, :], P4[:, :, 0, :], Q4[:, :, 1, :], ALU.subtract)
            return v(V.tensor_tensor, [], x4[:, :, 1, :], P4[:, :, 1, :], Q4[:, :, 0, :], ALU.add)

        scr = {"last": [l_cstb]}

        def rope_at(x, cos, sin, nh, hf, waits):
            o = rope(x, cos, sin, nh, hf, waits, scr["last"])
            scr["last"] = [o]
            return o

        def head_rms(x, nh, hd, w, waits, engw="dve"):
            n = nh * hd
            o = s(A.activation, waits + scr["last"], SCR[:, 0:n], x, ACT.Square)
            r = col(nh)
            o = v(V.tensor_reduce, [o], r, SCR[:, 0:n].rearrange("p (h d) -> p h d", h=nh), X_, ALU.add)
            scr["last"] = [o]
            rq = rsqrt(r, [o], 1.0 / hd, 1e-6)
            x3 = x.rearrange("p (h d) -> p h d", h=nh)
            o = v(V.tensor_tensor, [rq], x3, x3, r.unsqueeze(2).broadcast_to([128, nh, hd]), ALU.mult)
            return v(V.tensor_tensor, [o, l_small], x3, x3, w.unsqueeze(1).broadcast_to([128, nh, hd]), ALU.mult)

        buf = {"n": 0}
        e_free = [[], []]
        p_free = [[], []]

        def attention(units, scale):
            n = len(units)

            def scores(u):
                u["ps"] = []
                u["off"] = []
                off = 0
                for segs in u["banks"]:
                    b, bw = take()
                    c = 0
                    cols = []
                    first = True
                    for lhsT, rhs, nk, masks in segs:
                        op = m((u["deps"] + bw) if first else [], b[:, c:c + nk], lhsT, rhs,
                               start=True, stop=True)
                        first = False
                        for j, (c0, w, mk) in enumerate(masks):
                            op = m([l_cstb] + u.get("mdeps", []), b[:, c + c0:c + c0 + w], identb, mk, start=False,
                                   stop=True, skip_group_check=True)
                        cols.append((c, nk, off))
                        c += nk
                        off += nk
                    u["ps"].append((b, cols, op))

            def maxes(u):
                nseg = sum(len(c) for _, c, _ in u["ps"])
                mx = col(nseg)
                k = 0
                for b, cols, op in u["ps"]:
                    nk = cols[0][1]
                    o = v(V.tensor_reduce, [op], mx[:, k:k + len(cols)],
                          b[:, 0:nk * len(cols)].rearrange("p (n k) -> p n k", k=nk), X_, ALU.max)
                    k += len(cols)
                if u["joint"] and nseg > 1:
                    m1 = col(1)
                    o = v(V.tensor_reduce, [o], m1, mx, X_, ALU.max)
                    mx = m1
                nb = col(mx.shape[1])
                o = v(V.tensor_scalar, [o], nb, mx, -scale, None, ALU.mult)
                i = buf["n"] % 2
                buf["n"] += 1
                u["i"] = i
                k = 0
                if u["joint"]:
                    sums = col(nseg)
                else:
                    sums = u["sums"]
                for b, cols, op in u["ps"]:
                    for c, nk, off in cols:
                        bi = nb[:, 0:1] if u["joint"] else nb[:, k:k + 1]
                        so = sums[:, k:k + 1] if u["joint"] else sums[k]
                        x = s(A.activation, [o] + (e_free[i] if k == 0 else []), E[:, i, off:off + nk],
                              b[:, c:c + nk], ACT.Exp, bias=bi, scale=scale, accum_out=so)
                        k += 1
                    give(b, [x])
                u["x"] = x
                if u["joint"]:
                    u["x2"] = v(V.tensor_reduce, [x], u["sums"][0], sums, X_, ALU.add)
                if u["diff"]:
                    u["diff"](u)

            def turns(u):
                i = u["i"]
                tb = u["blocks"]
                ops = turn([E[:, i, c:c + 128] for c in tb], [u["x"]] + p_free[i],
                           lambda a, c: PET[:, i, a * 128:(a + c) * 128].rearrange("p (n q) -> p n q", n=c))
                u["t"] = ops
                e_free[i] = [ops[-1]]

            def values(u):
                i = u["i"]
                for okey, c0, dv, lst in u["outs"]:
                    ob, ow = okey["bank"]
                    for j, (blk, vap) in enumerate(lst):
                        op = m(u["t"] + ow + u["vdeps"], ob[:, c0:c0 + dv], PET[:, i, blk * 128:blk * 128 + 128], vap,
                               start=(j == 0), stop=(j == len(lst) - 1))
                    okey["op"] = op
                    okey["left"] -= 1
                    if okey["left"] == 0:
                        okey["done"]()
                p_free[i] = [op]

            for k in range(n + 2):
                if k < n:
                    for okey, *_ in units[k]["outs"]:
                        if "bank" not in okey:
                            okey["bank"] = take()
                    scores(units[k])
                    maxes(units[k])
                if 1 <= k <= n:
                    turns(units[k - 1])
                if k >= 2:
                    values(units[k - 2])

        def okey(n, done):
            return {"left": n, "done": done}

        def normalise(ob, dst, sums, nh, dv, key):
            def done():
                r = col(nh)
                sdeps = key["sdeps"]() if "sdeps" in key else []
                o = v(V.reciprocal, [key["op"]] + sdeps, r, sums)
                o = v(V.tensor_tensor, [o], dst, key["bank"][0][:, 0:nh * dv].rearrange("p (h d) -> p h d", h=nh),
                      r.unsqueeze(2).broadcast_to([128, nh, dv]), ALU.mult)
                give(key["bank"][0], [o])
                key["out"] = o
            return done

        def residual(ps, c, t, waits):
            xs = X[:, t, c * 512:c * 512 + 512]
            o = v(V.scalar_tensor_tensor, [ps[1]] + waits, out=xs, in0=xs, scalar=ALPHA, in1=ps[0][:, :],
                  op0=ALU.mult, op1=ALU.add)
            give(ps[0], [o])
            return o

        vec_rd = [[], []]
        x_w = [[l_x], [l_x]]
        xt_w = [l_xT]
        t_pe = []
        for i in range(2):
            ldv = [pld("vec0", VEC[:, 0:1024], bc(vecd[i * 5120:i * 5120 + 1024]), vec_rd[0]),
                   pld("vec1", VEC[:, 1024:2048], bc(vecd[i * 5120 + 1024:i * 5120 + 2048]), vec_rd[0]),
                   pld("vec4", VEC[:, 4096:5120], bc(vecd[i * 5120 + 4096:i * 5120 + 5120]), vec_rd[0]),
                   pld("vec2", VEC[:, 2048:3072], bc(vecd[i * 5120 + 2048:i * 5120 + 3072]), vec_rd[1]),
                   pld("vec3", VEC[:, 3072:4096], bc(vecd[i * 5120 + 3072:i * 5120 + 4096]), vec_rd[1])]
            l_pT = pld("pT", PT[:, :, :], pTd[i].rearrange("p (k n) -> p k n", k=2), vec_rd[1])
            hw = [[], []]
            for c, (a, b) in enumerate(((0, 512), (512, 1024), (1024, 1092))):
                r = linear("w_in", xt, xt_w, b - a, 8)
                for t in range(2):
                    o = copy("act", [r[t][1]], H[:, t, a:b], r[t][0][:, 0:b - a])
                    give(r[t][0], [o])
                    hw[t].append(o)
            gw = [[], []]
            r2 = [linear("w_in", xt, xt_w, 512, 8) for _ in range(2)]
            for c in range(2):
                for t in range(2):
                    o = s(A.activation, [r2[c][t][1]], GB[:, t, c * 512:c * 512 + 512], r2[c][t][0][:, :],
                          ACT.Gelu_apprx_tanh)
                    give(r2[c][t][0], [o])
                    gw[t].append(o)
            kd = [None, None]
            KD = MIX[:, :, 0:384].rearrange("p t (a b d) -> p t a b d", a=3, b=2)
            tw = []
            for t in range(2):
                cs, sn = COS[:, t, 0:8], SIN[:, t, 0:8]
                o1 = rope_at(H[:, t, 0:640].rearrange("p (h d) -> p h d", d=64)[:, :, 0:16], cs, sn, 10, 8, hw[t])
                o2 = rope_at(H[:, t, 768:1088].rearrange("p (h d) -> p h d", d=64)[:, :, 0:16], cs, sn, 5, 8, hw[t])
                k1 = v(V.tensor_copy, [o1], KD[:, t, 0:2, :, :], H[:, t, 512:640].rearrange("p (a d) -> p a d", a=2)
                       .unsqueeze(2).broadcast_to([128, 2, 2, 64]))
                k2 = v(V.tensor_copy, [o2], KD[:, t, 2, :, :], H[:, t, 1024:1088].unsqueeze(1)
                       .broadcast_to([128, 2, 64]))
                src = ([H[:, t, j * 128:j * 128 + 128] for j in range(4)]
                       + [MIX[:, t, j * 128:j * 128 + 128] for j in range(2)]
                       + [H[:, t, 768 + j * 128:896 + j * 128] for j in range(2)] + [MIX[:, t, 256:384]])
                tw += turn(src, [k1, k2] + t_pe, lambda a, c, t=t: T[:, a:a + c, t * 128:t * 128 + 128])
                wi = H[:, t, 1088:1092]
                kd[t] = v(V.tensor_scalar, [o2], wi, wi, 1.0 / 16.0, None, ALU.mult)

            sel_w = [None, None]
            for t in range(2):
                nk = 128 * (t + 1)
                SC = SCR[:, 0:nk]
                WK = [SCR[:, 256:256 + nk], SCR[:, 512:512 + nk]]
                RL = GB
                ops = []
                o = v(V.memset, scr["last"], SCR[:, 0:256], 0.0)
                o = v(V.tensor_copy, [o], SCR[:, nk - 128:nk], cst[:, C_CM:C_CM + 128])
                acc = [o]
                for par in range(2):
                    b, bw = take()
                    for n_, h in enumerate((par, par + 2)):
                        mm = m(tw + bw, b[:, n_ * nk:n_ * nk + nk],
                               T[64 * par:64 * par + 64, 6 + h // 2, t * 128:t * 128 + 128],
                               T[64 * par:64 * par + 64, 8, 0:nk], start=True, stop=True)
                    rl = s(A.activation, [mm] + e_free[par], E[:, par, 0:2 * nk], b[:, 0:2 * nk], ACT.Relu)
                    give(b, [rl])
                    for n_, h in enumerate((par, par + 2)):
                        o = v(V.scalar_tensor_tensor, [rl, kd[t]] + acc, out=SC, in0=E[:, par, n_ * nk:n_ * nk + nk],
                              scalar=H[:, t, 1088 + h:1089 + h], in1=SC, op0=ALU.mult, op1=ALU.add)
                        acc = [o]
                    e_free[par] = [o]
                src, prev = SC, o
                for rnd in range(8):
                    mx8 = col(8)
                    o = v(V.max, [prev], mx8, src)
                    o = v(V.match_replace, [o], WK[rnd % 2], mx8, src, -3e38)
                    src, prev = WK[rnd % 2], o
                sel_w[t] = v(V.tensor_scalar, [prev] + t_pe, selb[:, t, 0:nk], src, -2e38, -BIG, ALU.is_gt, ALU.mult)
                scr["last"] = [sel_w[t]]

            SM = [col(8), col(8)]
            keys_, units = [], []
            for t in range(2):
                nk = 128 * (t + 1)
                ok = okey(8, None)
                ok["done"] = normalise(None, MIX[:, t, 0:512].rearrange("p (h d) -> p h d", h=8), SM[t], 8, 64, ok)
                keys_.append(ok)
                per = 4 // (t + 1)
                for par in range(2):
                    hs = [par + 2 * j for j in range(4)]
                    for a in range(0, 4, per):
                        hh = hs[a:a + per]
                        segs = [(T[64 * par:64 * par + 64, h // 2, t * 128:t * 128 + 128],
                                 T[64 * par:64 * par + 64, 4 + h // 4, 0:nk], nk, [(0, nk, selb[:, t, 0:nk])])
                                for h in hh]
                        outs = [(ok, h * 64, 64, [(n_ * (t + 1) + kb, H[:, kb, 640 + (h // 4) * 64:704 + (h // 4) * 64])
                                                  for kb in range(t + 1)]) for n_, h in enumerate(hh)]
                        units.append(dict(banks=[segs], joint=False, diff=None, deps=tw, mdeps=[sel_w[t]],
                                          vdeps=[hw[0][1], hw[1][1]],
                                          sums=[SM[t][:, h:h + 1] for h in hh], outs=outs,
                                          blocks=[c * 128 for c in range(per * (t + 1))]))
            attention(units, 0.125)
            t_pe = [keys_[1]["op"]]

            vsw = [layer_norm(GB[:, t, 512:1024], GB[:, t, 512:1024], 512, VEC[:, 4096:4608], VEC[:, 4608:5120],
                              gw[t], ldv) for t in range(2)]
            (_, sv, ld, sl), = list(stream("sgu_w"))
            sv3 = sv[:, 0, :].rearrange("p (g t) -> p g t", g=8)
            wm = v(V.tensor_tensor, [ld, l_cst], sv3, sv3,
                   cst[:, C_TRI:C_TRI + 128].unsqueeze(1).broadcast_to([128, 8, 128]), ALU.mult)
            bo = []
            for gh in range(2):
                b, bw = take()
                for gg in range(4):
                    gr = gh * 4 + gg
                    mm = m([wm] + vsw + bw, b[:, gg * 128:gg * 128 + 128], sv3[:, gr, :],
                           GB[:, :, 512 + gr * 64:576 + gr * 64], start=True, stop=True)
                for gg in range(4):
                    gr = gh * 4 + gg
                    o = v(V.scalar_tensor_tensor, [mm, l_sgb], out=MIX[:, :, 512 + gr * 64:576 + gr * 64],
                          in0=b[:, gg * 128:gg * 128 + 128].rearrange("p (t d) -> p t d", t=2),
                          scalar=sgb[:, i, gr:gr + 1], in1=GB[:, :, gr * 64:gr * 64 + 64], op0=ALU.add, op1=ALU.mult)
                give(b, [o])
            left[sl] = [mm]

            xt_w = to_XT(MIX, 8, [[keys_[t]["out"], o] for t in range(2)])
            rw = [[], []]
            for c in range(2):
                r = linear("w_o", xt, xt_w, 512, 8)
                for t in range(2):
                    rw[t].append(residual(r[t], c, t, x_w[t]))
            x_w = [[layer_norm(X[:, t, :], X[:, t, :], 1024, VEC[:, 0:1024], VEC[:, 1024:2048], rw[t], ldv)]
                   for t in range(2)]
            vec_rd[0] = [x_w[1][0]]
            xt_w = to_XT(X, 8, x_w)

            for c in range(2):
                r = linear("w_ple_gate", xt, xt_w, 512, 8)
                sg = []
                for t in range(2):
                    o = s(A.activation, [r[t][1]], MIX[:, t, c * 512:c * 512 + 512], r[t][0][:, :], ACT.Sigmoid)
                    give(r[t][0], [o])
                    sg.append(o)
                r = linear("w_ple", lambda kt, t: PT[:, kt, t * 128:t * 128 + 128], [l_pT], 512, 2)
                for t in range(2):
                    ms = MIX[:, t, c * 512:c * 512 + 512]
                    o = v(V.tensor_tensor, [r[t][1], sg[t]], ms, ms, r[t][0][:, :], ALU.mult)
                    give(r[t][0], [o])
                    xs = X[:, t, c * 512:c * 512 + 512]
                    o = v(V.scalar_tensor_tensor, [o] + xt_w, out=xs, in0=xs, scalar=ALPHA, in1=ms,
                          op0=ALU.mult, op1=ALU.add)
                    x_w[t] = [o]
            ht = {}

            def ffn_turn(c):
                b, bw = take()
                for q in range(4):
                    kt, t = q // 2, q % 2
                    op = Q.add("pe", M.transpose, fw[c] + bw + t_pe, b[:, q * 128:q * 128 + 128],
                               GB[:, t, (c % 2) * 256 + kt * 128:(c % 2) * 256 + kt * 128 + 128], ident)
                cp = copy(alt(), [op], T[:, 2 * c:2 * c + 2, :], b[:, :].rearrange("p (n q) -> p n q", n=2))
                give(b, [cp])
                ht[2 * c] = ht[2 * c + 1] = cp
                f_free[c % 2] = [op]

            fw = {}
            f_free = [[o], [o]]
            for c in range(11):
                r = linear("w_ffn_in", xt, xt_w, 512, 8)
                fw[c] = []
                for t in range(2):
                    gs = GB[:, t, 512 + (c % 2) * 256:768 + (c % 2) * 256]
                    fs = GB[:, t, (c % 2) * 256:(c % 2) * 256 + 256]
                    a1 = s(A.activation, [r[t][1]] + f_free[c % 2] + fw.get(c - 2, []), gs, r[t][0][:, 0:256], ACT.Silu)
                    a2 = v(V.tensor_tensor, [a1] + f_free[c % 2], fs, gs, r[t][0][:, 256:512], ALU.mult)
                    give(r[t][0], [a2])
                    fw[c].append(a2)
                if c:
                    ffn_turn(c - 1)
            ffn_turn(10)
            r = linear_long("w_ffn_out", lambda kt, t: T[:, kt, t * 128:t * 128 + 128], lambda kt: [ht[kt]], 22)
            t_pe = [r[1][1][1]]
            rw = [[], []]
            for t in range(2):
                for c in range(2):
                    xs = X[:, t, c * 512:c * 512 + 512]
                    o = v(V.tensor_tensor, [r[t][c][1]] + x_w[t], xs, xs, r[t][c][0][:, :], ALU.add)
                    give(r[t][c][0], [o])
                    rw[t].append(o)
            x_w = [[layer_norm(X[:, t, :], X[:, t, :], 1024, VEC[:, 2048:3072], VEC[:, 3072:4096], rw[t], ldv)]
                   for t in range(2)]
            vec_rd[1] = [x_w[1][0]]
            if i == 0:
                xt_w = to_XT(X, 8, x_w)

        o = s(A.activation, [l_c], cT[:, :], cT[:, :], ACT.Silu)
        cbw = v(V.tensor_copy, [o], CB[:, :, :], cT[:, :].unsqueeze(2).broadcast_to([128, 8, 128]))
        lv = sm["diff_lambda_2"].rearrange("p (a b d) -> p a b d", a=2, b=2)
        lt = col(2)
        o = v(V.tensor_tensor, [l_small] + scr["last"], SCR[:, 0:128].rearrange("p (a d) -> p a d", a=2), lv[:, :, 0, :],
              lv[:, :, 1, :], ALU.mult)
        o = v(V.tensor_reduce, [o], lt, SCR[:, 0:128].rearrange("p (a d) -> p a d", a=2), X_, ALU.add)
        scr["last"] = [o]
        lam = sb("lam", [128, 2])
        o = s(A.activation, [o], lt, lt, ACT.Exp)
        o = v(V.tensor_tensor, [o], lam[:, 0:1], lt[:, 0:1], lt[:, 1:2], ALU.subtract)
        w_lam = v(V.tensor_scalar, [o], lam[:, 1:2], lam[:, 0:1], LAM, -1.0, ALU.add, ALU.mult)
        subl = sm["diff_subln_2"]
        w_sub = v(V.tensor_scalar, [l_small], subl, subl, 1.0 - LAM, None, ALU.mult)

        mod_rd = [x_w[0][0], x_w[1][0]]
        nw_rd = []

        def norm_mod(ssh, ssc, waits, wdeps):
            hw_ = []
            for t in range(2):
                ss = col(1)
                o = s(A.activation, x_w[t] + waits, MIX[:, t, :], X[:, t, :], ACT.Square, accum_out=ss)
                o = rsqrt(ss, [o], 1.0 / D, 1e-6)
                o = v(V.scalar_tensor_tensor, [o] + wdeps, out=MIX[:, t, :], in0=X[:, t, :], scalar=ss,
                      in1=MOD[:, ssc, :], op0=ALU.mult, op1=ALU.mult)
                hw_.append([v(V.tensor_tensor, [o], MIX[:, t, :], MIX[:, t, :], MOD[:, ssh, :], ALU.add)])
            return to_XT(MIX, 8, hw_)

        def gated(r, c, gi, wdeps):
            for t in range(2):
                ms = MIX[:, t, c * 512:c * 512 + 512]
                o = v(V.tensor_tensor, [r[t][1]] + wdeps, ms, r[t][0][:, :], MOD[:, gi, c * 512:c * 512 + 512], ALU.mult)
                give(r[t][0], [o])
                xs = X[:, t, c * 512:c * 512 + 512]
                o = v(V.tensor_tensor, [o] + x_w[t], xs, xs, ms, ALU.add)
                xg[t].append(o)

        mix_rd = list(xt_w)
        for i in range(2):
            l_mod = pld("mod", MOD[:, :, :].rearrange("p a b -> p (a b)"), bc(adabd[i * 6144:i * 6144 + 6144]), mod_rd)
            l_n1 = pld("n1", NW[:, :], bc(nrmd[i * 2048:i * 2048 + 1024]), nw_rd)
            mw = []
            for c in range(12):
                ps = take()
                for a, view, ld, sl in stream("ada_w_2"):
                    for j in range(view.shape[1]):
                        kt = a + j
                        op = m([ld, cbw] + ps[1], ps[0][:, :], CB[:, kt, :], view[:, j, :], start=(kt == 0),
                               stop=(kt == 7))
                    left[sl] = [op]
                ms = MOD[:, c // 2, (c % 2) * 512:(c % 2) * 512 + 512]
                o = v(V.tensor_tensor, [op, l_mod], ms, ms, ps[0][:, :], ALU.add)
                give(ps[0], [o])
                mw.append(o)
            o = v(V.scalar_tensor_tensor, [mw[3], l_n1], out=MOD[:, 1, :], in0=MOD[:, 1, :], scalar=1.0, in1=NW[:, :],
                  op0=ALU.add, op1=ALU.mult)
            l_n2 = pld("n2", NW[:, :], bc(nrmd[i * 2048 + 1024:i * 2048 + 2048]), [o])
            o2 = v(V.scalar_tensor_tensor, [mw[9], l_n2], out=MOD[:, 4, :], in0=MOD[:, 4, :], scalar=1.0, in1=NW[:, :],
                   op0=ALU.add, op1=ALU.mult)
            nw_rd = [o2]
            xt_w = norm_mod(0, 1, mix_rd, [o, mw[1]])
            if i == 0:
                LT_ = MIX
                MQ = H[:, :, 2304:3072]
                MK = GB[:, :, 0:768]
                lw = [[], []]
                for a, b in ((0, 384), (384, 672)):
                    r = linear("even_w_in_2", xt, xt_w, b - a, 8)
                    for t in range(2):
                        o = copy("act", [r[t][1]] + xt_w, MIX[:, t, a:b], r[t][0][:, 0:b - a])
                        give(r[t][0], [o])
                        lw[t].append(o)
                dw = [[[], []] for _ in range(3)]

                def dil_in(c):
                    r = linear("even_w_in_2", xt, xt_w, 384, 8)
                    for t in range(2):
                        o = copy("act", [r[t][1]], H[:, t, c * 384:c * 384 + 384], r[t][0][:, 0:384])
                        give(r[t][0], [o])
                        dw[c // 2][t].append(o)

                for c in range(4):
                    dil_in(c)
                lnw = [[], []]
                for t in range(2):
                    for a, n_, nm in ((0, 384, "mla_q_lat_norm_2"), (384, 256, "mla_kv_lat_norm_2")):
                        xs = MIX[:, t, a:a + n_]
                        ss = col(1)
                        o = s(A.activation, lw[t] + scr["last"], SCR[:, 0:n_], xs, ACT.Square, accum_out=ss)
                        scr["last"] = [o]
                        o = rsqrt(ss, [o], 1.0 / n_, 1e-6)
                        lnw[t].append(v(V.scalar_tensor_tensor, [o, l_small], out=xs, in0=xs, scalar=ss, in1=sm[nm],
                                        op0=ALU.mult, op1=ALU.mult))
                LTT = PET[:, :, :].rearrange("p a b -> p (a b)")[:, 0:1280].rearrange("p (k n) -> p k n", k=5)
                ltw = []
                for t in range(2):
                    ltw += turn([MIX[:, t, k * 128:k * 128 + 128] for k in range(5)], lnw[t] + p_free[0] + p_free[1],
                                lambda a, c, t=t: LTT[:, a:a + c, t * 128:t * 128 + 128])
                qw = [[], []]
                for c in range(2):
                    r = linear("mla_w_uq_2", lambda kt, t: LTT[:, kt, t * 128:t * 128 + 128], ltw, 384, 3)
                    for t in range(2):
                        o = copy("act", [r[t][1]], MQ[:, t, c * 384:c * 384 + 384], r[t][0][:, 0:384])
                        give(r[t][0], [o])
                        qw[t].append(o)
                kw = [[], []]
                r = linear("mla_w_ukv_2", lambda kt, t: LTT[:, 3 + kt, t * 128:t * 128 + 128], ltw, 512, 2)
                for t in range(2):
                    k3 = MK[:, t, :].rearrange("p (h d) -> p h d", h=8)
                    o = copy("act", [r[t][1]] + mod_rd, k3[:, :, 0:64], r[t][0][:, :].rearrange("p (h d) -> p h d", h=8))
                    give(r[t][0], [o])
                    o3 = copy("dve", lw[t] + mod_rd, k3[:, :, 64:96],
                              MIX[:, t, 640:672].unsqueeze(1).broadcast_to([128, 8, 32]))
                    kw[t] = [o, o3]
                r = linear("mla_w_ukv_2", lambda kt, t: LTT[:, 3 + kt, t * 128:t * 128 + 128], ltw, 512, 2)
                mvw = []
                for t in range(2):
                    o = copy("act", [r[t][1]], MV[:, t, :], r[t][0][:, :])
                    give(r[t][0], [o])
                    mvw.append(o)
                p_free = [[r[1][1]], [r[1][1]]]
                for c in range(4, 6):
                    dil_in(c)
                tw = []
                for t in range(2):
                    cs, sn = COS[:, t, 8:40:2], SIN[:, t, 8:40:2]
                    for x_, ww, nm, base in ((MQ, qw, "mla_q_norm_2", 0), (MK, kw, "mla_k_norm_2", 8)):
                        o = head_rms(x_[:, t, :], 8, 96, sm[nm], ww[t])
                        o = rope_at(x_[:, t, :].rearrange("p (h d) -> p h d", h=8)[:, :, 64:96], cs, sn, 8, 16, [o])
                        tw += turn([x_[:, t, h * 96:h * 96 + 96] for h in range(8)], [o] + t_pe,
                                   lambda a, c, t=t, base=base: T[0:96, base + a:base + a + c, t * 128:t * 128 + 128],
                                   rows=96)
                SMm = [col(8), col(8)]
                keys_, units = [], []
                mla_scale = 96 ** -0.5
                for t in range(2):
                    nk = 128 * (t + 1)
                    ok = okey(8, None)
                    ok["done"] = normalise(None, MIX[:, t, 0:512].rearrange("p (h d) -> p h d", h=8), SMm[t], 8, 64, ok)
                    keys_.append(ok)
                    per = 4 // (t + 1)
                    for a in range(0, 8, per):
                        hh = list(range(a, a + per))
                        segs = [(T[0:96, h, t * 128:t * 128 + 128], T[0:96, 8 + h, 0:nk], nk,
                                 [(nk - 128, 128, maskb(B_TRI))]) for h in hh]
                        outs = [(ok, h * 64, 64, [(n_ * (t + 1) + kb, MV[:, kb, h * 64:h * 64 + 64])
                                                  for kb in range(t + 1)]) for n_, h in enumerate(hh)]
                        units.append(dict(banks=[segs], joint=False, diff=None, deps=tw,
                                          vdeps=mvw, sums=[SMm[t][:, h:h + 1] for h in hh], outs=outs,
                                          blocks=[c * 128 for c in range(per * (t + 1))]))
                attention(units, mla_scale)
                tw2 = []
                for t in range(2):
                    for x0, ww, nm, base in ((0, dw[0], "dil_q_norm_2", 16), (768, dw[1], "dil_k_norm_2", 22)):
                        xs = H[:, t, x0:x0 + 768]
                        o = head_rms(xs, 12, 64, sm[nm], ww[t])
                        x3 = xs.rearrange("p (h d) -> p h d", h=12)
                        o = rope_at(x3[:, 0:6, :], COS[:, t, 8:40], SIN[:, t, 8:40], 6, 32, [o])
                        o = rope_at(x3[:, 6:12, :], COS[:, t, 8:40], SIN[:, t, 8:40], 6, 32, [o])
                        tw2 += turn([xs[:, h * 128:h * 128 + 128] for h in range(6)], [o] + t_pe,
                                    lambda a, c, t=t, base=base: T[:, base + a:base + a + c, t * 128:t * 128 + 128])
                SMd = [col(4), col(4)]
                units = []
                for t in range(2):
                    nk = 128 * (t + 1)
                    ok = okey(4, None)
                    ok["done"] = normalise(None, MIX[:, t, 512:768].rearrange("p (h d) -> p h d", h=4), SMd[t], 4, 64, ok)
                    keys_.append(ok)
                    for h in range(4):
                        segs = []
                        for gp in range(3):
                            hd = gp * 4 + h
                            bs = 64 * (hd % 2)
                            mk = [(nk - 128, 128, maskb((B_TRI, B_TRI4, B_TRI16)[gp]))]
                            if t:
                                mk.append((0, 128, maskb((B_UP, B_M4, B_M16)[gp])))
                            segs.append((T[bs:bs + 64, 16 + hd // 2, t * 128:t * 128 + 128],
                                         T[bs:bs + 64, 22 + hd // 2, 0:nk], nk, mk))
                        outs = [(ok, h * 64, 64, [(gp * (t + 1) + kb,
                                                   H[:, kb, 1536 + (gp * 4 + h) * 64:1600 + (gp * 4 + h) * 64])
                                                  for gp in range(3) for kb in range(t + 1)])]
                        units.append(dict(banks=[segs[0:2], segs[2:3]], joint=True, diff=None, deps=tw2,
                                          vdeps=dw[2][0] + dw[2][1], sums=[SMd[t][:, h:h + 1]], outs=outs,
                                          blocks=[c * 128 for c in range(3 * (t + 1))]))
                attention(units, 0.125)
                t_pe = [keys_[3]["op"]]
                ao_w = [[keys_[0]["out"], keys_[2]["out"]], [keys_[1]["out"], keys_[3]["out"]]]
                xt_w = to_XT(MIX, 6, ao_w)
                xg = [[], []]
                for c in range(2):
                    gated(linear("even_w_out_2", xt, xt_w, 512, 6), c, 2, [mw[5]] + xt_w)
            else:
                dw = []
                for c in range(6):
                    r = linear("odd_w_in_2", xt, xt_w, 512, 8)
                    dw.append([])
                    for t in range(2):
                        o = copy("act", [r[t][1]] + xt_w, H[:, t, c * 512:c * 512 + 512], r[t][0][:, :])
                        give(r[t][0], [o])
                        dw[c].append(o)

                def qk(c, nm, base):
                    ops = []
                    for t in range(2):
                        xs = H[:, t, c * 512:c * 512 + 512]
                        o = head_rms(xs, 8, 64, sm[nm], [dw[c][t]])
                        o = rope_at(xs.rearrange("p (h d) -> p h d", h=8), COS[:, t, 8:40], SIN[:, t, 8:40], 8, 32, [o])
                        ops += turn([xs[:, h * 128:h * 128 + 128] for h in range(4)], [o] + t_pe,
                                    lambda a, c, t=t: T[:, base + a:base + a + c, t * 128:t * 128 + 128])
                    return ops

                tw = qk(0, "diff_q_norm_2", 0) + qk(1, "diff_k_norm_2", 4)
                units, keys_ = [], []

                def differ(u):
                    i_, t, nk = u["i"], u["tt"], u["nk"]
                    r4 = col(4)
                    o = v(V.reciprocal, [u["x"]], r4, u["s4"])
                    c2_ = col(2)
                    o = v(V.tensor_scalar, [o, w_lam], c2_, r4[:, 2:4], lam[:, 1:2], None, ALU.mult)
                    for n_ in range(2):
                        e1 = E[:, i_, (2 + n_) * nk:(3 + n_) * nk]
                        o1 = v(V.tensor_scalar, [o], e1, e1, c2_[:, n_:n_ + 1], None, ALU.mult)
                    for n_ in range(2):
                        e0 = E[:, i_, n_ * nk:n_ * nk + nk]
                        e1 = E[:, i_, (2 + n_) * nk:(3 + n_) * nk]
                        o1 = v(V.scalar_tensor_tensor, [o1], out=e0, in0=e0, scalar=r4[:, n_:n_ + 1], in1=e1,
                               op0=ALU.mult, op1=ALU.add)
                    u["x"] = o1

                def diff_done(t, ok):
                    def done():
                        dst = MIX[:, t, 0:512]
                        b = ok["bank"][0]
                        o = s(A.activation, [ok["op"]], dst, b[:, :], ACT.Copy)
                        give(b, [o])
                        ok["out"] = head_rms(dst, 4, 128, subl, [o, w_sub])
                    return done

                for t in range(2):
                    nk = 128 * (t + 1)
                    ok = okey(4, None)
                    ok["done"] = diff_done(t, ok)
                    keys_.append(ok)
                    for a in (0, 2):
                        bks = []
                        for mp in range(2):
                            bks.append([(T[64 * mp:64 * mp + 64, h, t * 128:t * 128 + 128],
                                         T[64 * mp:64 * mp + 64, 4 + h, 0:nk], nk, [(nk - 128, 128, maskb(B_TRI))])
                                        for h in (a, a + 1)])
                        s4 = col(4)
                        outs = [(ok, h * 128, 128, [(n_ * (t + 1) + kb, H[:, kb, 1024 + h * 128:1152 + h * 128])
                                                    for kb in range(t + 1)]) for n_, h in enumerate((a, a + 1))]
                        units.append(dict(banks=bks, joint=False, diff=differ, deps=tw, vdeps=dw[2], s4=s4, tt=t, nk=nk,
                                          sums=[s4[:, j:j + 1] for j in range(4)], outs=outs,
                                          blocks=[c * 128 for c in range(2 * (t + 1))]))
                attention(units, 0.125)
                tw = qk(3, "moba_q_norm_2", 8) + qk(4, "moba_k_norm_2", 12)
                SMb = [col(8), col(8)]
                units = []
                for t in range(2):
                    nk = 128 * (t + 1)
                    ok = okey(8, None)
                    ok["done"] = normalise(None, MIX[:, t, 512:1024].rearrange("p (h d) -> p h d", h=8), SMb[t], 8, 64,
                                           ok)
                    keys_.append(ok)
                    per = 4 // (t + 1)
                    for par in range(2):
                        hs = [par + 2 * j for j in range(4)]
                        for a in range(0, 4, per):
                            hh = hs[a:a + per]
                            segs = [(T[64 * par:64 * par + 64, 8 + h // 2, t * 128:t * 128 + 128],
                                     T[64 * par:64 * par + 64, 12 + h // 2, 0:nk], nk,
                                     [(nk - 128, 128, maskb(B_TRI))]) for h in hh]
                            outs = [(ok, h * 64, 64, [(n_ * (t + 1) + kb, H[:, kb, 2560 + h * 64:2624 + h * 64])
                                                      for kb in range(t + 1)]) for n_, h in enumerate(hh)]
                            units.append(dict(banks=[segs], joint=False, diff=None, deps=tw, vdeps=dw[5],
                                              sums=[SMb[t][:, h:h + 1] for h in hh], outs=outs,
                                              blocks=[c * 128 for c in range(per * (t + 1))]))
                attention(units, 0.125)
                t_pe = [keys_[3]["op"]]
                ao_w = [[keys_[0]["out"], keys_[2]["out"]], [keys_[1]["out"], keys_[3]["out"]]]
                xt_w = to_XT(MIX, 8, ao_w)
                xg = [[], []]
                for c in range(2):
                    gated(linear("odd_w_out_2", xt, xt_w, 512, 8), c, 2, [mw[5]] + xt_w)
            x_w = xg
            xt_w = norm_mod(3, 4, [], [o2, mw[7]])
            ht = {}
            fw = {}
            f_free = [[], []]

            def mlp_turn(c):
                for hf in range(2):
                    b, bw = take()
                    for q in range(4):
                        kt, t = hf * 2 + q // 2, q % 2
                        op = Q.add("pe", M.transpose, fw[c] + bw + t_pe, b[:, q * 128:q * 128 + 128],
                                   FB[c % 2][:, t, kt * 128:kt * 128 + 128], ident)
                    cp = s(A.activation, [op], T[:, 4 * c + 2 * hf:4 * c + 2 * hf + 2, :],
                           b[:, :].rearrange("p (n q) -> p n q", n=2), ACT.Square)
                    give(b, [cp])
                    ht[4 * c + 2 * hf] = ht[4 * c + 2 * hf + 1] = cp
                f_free[c % 2] = [op]

            FB = [GB[:, :, 0:512], GB[:, :, 512:1024]]
            for c in range(8):
                r = linear("mlp_w1_2", xt, xt_w, 512, 8)
                fw[c] = []
                for t in range(2):
                    o = v(V.tensor_scalar, [r[t][1]] + f_free[c % 2] + t_pe, FB[c % 2][:, t, :], r[t][0][:, :], 0.0, None, ALU.max)
                    give(r[t][0], [o])
                    fw[c].append(o)
                if c:
                    mlp_turn(c - 1)
            mlp_turn(7)
            r = linear_long("mlp_w2_2", lambda kt, t: T[:, kt, t * 128:t * 128 + 128], lambda kt: [ht[kt]], 32)
            t_pe = [r[1][1][1]]
            xg = [[], []]
            for c in range(2):
                gated([r[0][c], r[1][c]], c, 5, [mw[11]] + xt_w)
            x_w = xg
            mod_rd = x_w[0] + x_w[1]
            mix_rd = x_w[0] + x_w[1]
        for t in range(2):
            Q.stores.append(Q.dma("sp", f"out{t}", Y.dma_start, x_w[t], out[0, t * 128:t * 128 + 128, :], X[:, t, :]))

        Q.finish()
        block = ctx.enter_context(nc.Block())

        @block.sync
        def _(eng):
            Q.emit("sp", eng)

        @block.gpsimd
        def _(eng):
            Q.emit("pool", eng)

        @block.scalar
        def _(eng):
            Q.emit("act", eng)

        @block.vector
        def _(eng):
            Q.emit("dve", eng)

        @block.tensor
        def _(eng):
            Q.emit("pe", eng)


def constants():
    c = np.zeros((128, C_END), np.float32)
    q, k = np.arange(128)[:, None], np.arange(128)[None, :]
    c[:, C_ID:C_ID + 128] = np.eye(128)
    c[:, C_CM:C_CM + 128] = np.where(k // 64 <= q // 64, 0.0, -BIG)
    c[:, C_TRI:C_TRI + 128] = q <= k
    c[:, C_INV:C_INV + 8] = np.float32(500000.0) ** (np.float32(-2.0) * np.arange(8, dtype=np.float32) / np.float32(16))
    c[:, C_INV + 8:C_INV + 40] = np.float32(10000.0) ** (-np.arange(32, dtype=np.float32) / np.float32(32))
    c[:, C_HPI] = math.pi / 2
    c[:, C_MH] = -0.5
    b = np.zeros((128, 7, 128), np.float32)
    b[:, B_ID] = np.eye(128)
    for n, ok in ((B_TRI, k <= q), (B_UP, k >= q), (B_TRI4, (k <= q) & ((q - k) % 4 == 0)), (B_M4, (q - k) % 4 == 0),
                  (B_TRI16, (k <= q) & ((q - k) % 16 == 0)), (B_M16, (q - k) % 16 == 0)):
        b[:, n] = np.where(ok, 0.0, -BIG)
    return c, b.reshape(128, -1)


def kernel(**inputs):
    import concourse.bacc as _bacc
    from concourse.bass_utils import run_bass_kernel_spmd as _run

    a = {n: np.asarray(x) for n, x in inputs.items()}
    parts = []
    for name, i, k, cols in plan():
        w = a[name][i]
        if name == "sgu_w":
            w = w.transpose(2, 0, 1)
        w = w.reshape(k, -1)
        w = np.concatenate([w[:, c0:c1] for c0, c1 in cols], axis=1)
        w = w.reshape(k // 128, 128, -1).transpose(1, 0, 2)
        for k0, n in pieces(k, w.shape[2]):
            parts.append(w[:, k0:k0 + n, :].reshape(-1))
    cst, cstb = constants()
    x = a["x"]
    arrays = {
        "W": np.concatenate(parts),
        "xd": x,
        "xTd": np.ascontiguousarray(x[0].T.reshape(8, 128, S).transpose(1, 0, 2).reshape(128, -1)),
        "pTd": np.ascontiguousarray(a["p"][:, 0].transpose(0, 2, 1).reshape(2, 2, 128, S).transpose(0, 2, 1, 3)
                                    .reshape(2, 128, -1)),
        "posd": np.ascontiguousarray(a["positions"].reshape(2, 128).T),
        "pos2d": np.ascontiguousarray(a["positions_2"].reshape(2, 128).T),
        "cTd": np.ascontiguousarray(a["c_2"][0].reshape(8, 128).T),
        "cstd": cst,
        "cstbd": cstb,
        "vecd": np.concatenate([a[n][i] for i in range(2) for n in
                                ("ln1_g", "ln1_b", "ln2_g", "ln2_b", "sgu_ln_g", "sgu_ln_b")]),
        "sgbd": np.ascontiguousarray(a["sgu_b"].transpose(2, 0, 1).reshape(128, 16)),
        "nrmd": np.concatenate([a[n][i] for i in range(2) for n in ("norm_mix_2", "norm_mlp_2")]),
        "adabd": a["ada_b_2"].reshape(-1),
        "smalld": np.concatenate([a[n].reshape(-1) for n, _ in SMALL]),
    }
    nc = _bacc.Bacc("TRN2", target_bir_lowering=False, num_devices=1)
    args = [nc.dram_tensor(n, x_.shape, mybir.dt.from_np(x_.dtype), kind="ExternalInput").ap()
            for n, x_ in arrays.items()]
    args.append(nc.dram_tensor("out", (1, S, D), F32, kind="ExternalOutput").ap())
    program(nc, *args)
    r = _run(nc, [arrays], core_ids=[0])
    return r.results[0]["out"]
```

```python
import math
from contextlib import ExitStack

import numpy as np

import concourse.bass as bass
from concourse import mybir

F32 = mybir.dt.float32
BF16 = mybir.dt.bfloat16
I32 = mybir.dt.int32
ALU = mybir.AluOpType
ACT = mybir.ActivationFunctionType
X_ = mybir.AxisListType.X

F32R = mybir.dt.float32r

S, D = 256, 1024
SLOT = 2048
NRAW = 3
NPAIR = 3
DFF = 2816
ALPHA = 4 ** 0.25
BIG = 1e30
LAM = 0.8 - 0.6 * math.exp(-0.3)

C_ID, C_CM, C_TRI, C_INV, C_HPI, C_MH, C_ONE, C_END = 0, 128, 256, 384, 424, 425, 426, 554
B_ID, B_TRI, B_UP, B_TRI4, B_M4, B_TRI16, B_M16 = range(7)
K_ADAB, K_NRM, K_C, K_SGB, K_END = 0, 96, 128, 136, 152
SMALL = [("mla_q_lat_norm_2", 384), ("mla_kv_lat_norm_2", 256), ("mla_q_norm_2", 96), ("mla_k_norm_2", 96),
         ("dil_q_norm_2", 64), ("dil_k_norm_2", 64), ("diff_q_norm_2", 64), ("diff_k_norm_2", 64),
         ("diff_subln_2", 128), ("moba_q_norm_2", 64), ("moba_k_norm_2", 64), ("diff_lambda_2", 256)]
NSMALL = sum(n for _, n in SMALL)


def plan():
    out = []

    def all_rows(name, i, k, *cuts):
        for cols in cuts:
            out.append((name, i, (0, k), cols if isinstance(cols, list) else [cols]))

    def ada(i, *cs):
        for c in cs:
            out.append(("ada_w_2", i, (0, 1024), [(c * 512, c * 512 + 512)]))

    halves = ((0, 512), (512, 1024))
    for i in range(2):
        all_rows("w_in", i, 1024, (0, 364), (364, 728), (728, 1092), (1092, 1604), (1604, 2116))
        all_rows("w_o", i, 1024, *halves)
        for h in halves:
            all_rows("w_ple_gate", i, 1024, h)
            all_rows("w_ple", i, 256, h)
        for c in range(12):
            if c < 11:
                all_rows("w_ffn_in", i, 1024, [(c * 256, c * 256 + 256), (DFF + c * 256, DFF + c * 256 + 256)])
            if c in (2, 4, 6, 8):
                ada(0, (0, 1, 2, 3, 6, 7, 8, 9)[i * 4 + c // 2 - 1])
            if c:
                out.append(("w_ffn_out", i, (c * 256 - 256, c * 256), [(0, 1024)]))
    for i in range(2):
        if i == 0:
            all_rows("even_w_in_2", 0, 1024, (0, 384), (384, 672))
            all_rows("mla_w_uq_2", 0, 384, (0, 384), (384, 768))
            all_rows("mla_w_ukv_2", 0, 256, [(h * 128, h * 128 + 64) for h in range(8)],
                     [(h * 128 + 64, h * 128 + 128) for h in range(8)])
            ada(0, 4)
            all_rows("even_w_in_2", 0, 1024, (672, 1056), (1056, 1440), (1440, 1824))
            ada(0, 5)
            all_rows("even_w_in_2", 0, 1024, (1824, 2208), (2208, 2592), (2592, 2976))
            all_rows("even_w_out_2", 0, 768, *halves)
        else:
            all_rows("odd_w_in_2", 0, 1024, (0, 512), (512, 1024), (1024, 1536))
            ada(1, 4)
            all_rows("odd_w_in_2", 0, 1024, (1536, 2048), (2048, 2560))
            ada(1, 5)
            all_rows("odd_w_in_2", 0, 1024, (2560, 3072))
            all_rows("odd_w_out_2", 0, 1024, *halves)
        for c in range(9):
            if c < 8:
                all_rows("mlp_w1_2", i, 1024, (c * 512, c * 512 + 512))
            for la, ca in ((((0, 10),), ((0, 11),), ((1, 1),), ((1, 3),), ((1, 7),), ((1, 8),), (), (), ())
                           if i == 0 else (((1, 10),), (), ((1, 11),), (), (), (), (), (), ()))[c]:
                ada(la, ca)
            if c:
                out.append(("mlp_w2_2", i, (c * 512 - 512, c * 512), [(0, 1024)]))
                for la, ca in (((1, 0),), ((1, 2),), ((1, 6),), (), ((1, 9),), (), (), ())[c - 1] if i == 0 else ():
                    ada(la, ca)
    return out


def pieces(k, w):
    per = SLOT // w
    kt = k // 128
    return [(a, min(per, kt - a)) for a in range(0, kt, per)]


def width(cols):
    return sum(b - a for a, b in cols)


def total():
    return sum((r1 - r0) * width(cols) for _, _, (r0, r1), cols in plan())


class Op:
    def __init__(self, eng, f, waits, a, k):
        self.eng, self.f, self.waits, self.a, self.k = eng, f, waits, a, k
        self.used, self.sem, self.val = False, None, 0


class Queue:

    def __init__(self, nc, sem):
        self.nc, self.sem = nc, sem
        self.q = {"pe": [], "dve": [], "act": [], "pool": [], "sp": []}
        self.esem = {e: sem("s_" + e) for e in self.q}
        self.dcount = {}
        self.stores = []

    def add(self, eng, f, waits, *a, **k):
        flat = []
        for w in waits:
            flat.extend(w if isinstance(w, (list, tuple)) else [w])
        op = Op(eng, f, flat, a, k)
        for w in flat:
            w.used = True
        self.q[eng].append(op)
        return op

    def dma(self, eng, name, f, waits, dst, src):
        op = self.add(eng, f, waits, dst, src)
        if name not in self.dcount:
            self.dcount[name] = [self.sem("d_" + name), 0]
        c = self.dcount[name]
        c[1] += 16
        op.sem, op.val = c[0], c[1]
        return op

    def finish(self):
        for e, ops in self.q.items():
            n = 0
            for op in ops:
                if op.sem is None and op.used:
                    n += 1
                    op.val = n

    def emit(self, e, eng):
        seen = {}
        for op in self.q[e]:
            need = {}
            for w in op.waits:
                s = w.sem if w.sem is not None else self.esem[w.eng]
                need[id(s)] = (s, max(w.val, need.get(id(s), (s, 0))[1]))
            for i, (s, v) in need.items():
                if seen.get(i, 0) < v:
                    eng.wait_ge(s, v)
                    seen[i] = v
            ins = op.f(*op.a, **op.k)
            if op.sem is not None:
                ins.then_inc(op.sem, 16)
            elif op.used:
                ins.then_inc(self.esem[e], 1)
        for op in self.stores:
            if op.eng == e:
                eng.wait_ge(op.sem, op.val)


def program(nc, W, xd, xTd, pTd, posd, pos2d, colvd, cstd, cstbd, vecd, sgwd, adagd, smalld, out):
    with ExitStack() as ctx:
        def sb(name, shape, dt=F32):
            return ctx.enter_context(nc.sbuf_tensor(name, shape, dt))

        def sem(name):
            return ctx.enter_context(nc.semaphore(name))

        Q = Queue(nc, sem)
        V, A, G, M, Y = nc.vector, nc.scalar, nc.gpsimd, nc.tensor, nc.sync

        def v(f, waits, *a, **k):
            return Q.add("dve", f, waits, *a, **k)

        def s(f, waits, *a, **k):
            return Q.add("act", f, waits, *a, **k)

        def g(f, waits, *a, **k):
            return Q.add("pool", f, waits, *a, **k)

        def m(waits, *a, **k):
            return Q.add("pe", M.matmul, waits, *a, **k)

        RAW = sb("RAW", [128, NRAW, SLOT])
        WH = sb("WH", [128, NPAIR, SLOT], F32R)
        WL = sb("WL", [128, NPAIR, SLOT], F32R)
        X = sb("X", [128, 2, 1024])
        XTH = sb("XTH", [128, 8, 256], F32R)
        XTL = sb("XTL", [128, 8, 256], F32R)
        MIX = sb("MIX", [128, 2, 1024])
        H = sb("H", [128, 2, 3072])
        GB = sb("GB", [128, 2, 1024])
        VEC = sb("VEC", [128, 3072])
        VG = VEC[:, 0:2048].rearrange("p (a n) -> p a n", a=2)
        MV = VEC[:, 2048:3072].rearrange("p (t n) -> p t n", t=2)
        E = sb("E", [128, 2, 1024])
        PET = sb("PET", [128, 2, 768])
        SCR = sb("SCR", [128, 1024])
        ACC = sb("ACC", [128, 2, 512])
        PTH = sb("PTH", [128, 2, 256], F32R)
        PTL = sb("PTL", [128, 2, 256], F32R)
        cst = sb("cst", [128, C_END])
        cstb = sb("cstb", [128, 7 * 128], BF16)
        selb = sb("selb", [128, 2, 256], BF16)
        small = sb("small", [128, NSMALL])
        colv = sb("colv", [128, K_END])
        modc = sb("modc", [128, 2, 48])
        posi = sb("posi", [128, 4], I32)
        posf = sb("posf", [128, 4])
        trig = sb("trig", [128, 4, 2, 40])
        COS = sb("COS", [128, 2, 40])
        SIN = sb("SIN", [128, 2, 40])
        st = sb("st", [128, 256])
        lam = sb("lam", [128, 2])
        with nc.sbuf_tensor("T", [128, 16, 256], F32) as T:
            pass
        HTH = sb("HTH", [128, 8, 256], F32R)
        HTL = sb("HTL", [128, 8, 256], F32R)
        banks = [ctx.enter_context(nc.psum_tensor(f"ps{i}", [128, 512], F32)) for i in range(8)]

        free = [(b, []) for b in banks]

        def take():
            return free.pop(0)

        def give(bank, ops):
            free.append((bank, list(ops)))

        chunks = plan()
        seq, later = [], []
        off = 0
        for n, (name, i, (r0, r1), cols) in enumerate(chunks):
            w = width(cols)
            for a, c in pieces(r1 - r0, w):
                it = dict(name=name, layer=i, chunk=n, a=a, n=c, w=w, off=off, col=cols[0][0])
                off += 128 * c * w
                if name == "ada_w_2":
                    later.append(it)
                else:
                    seq.append(it)
                    if later:
                        seq.append(later.pop(0))
        cur = {"chunk": 0, "item": 0, "made": 0, "used": 0}
        raw_left = [[] for _ in range(NRAW)]
        pair_left = [[] for _ in range(NPAIR)]

        def load(n):
            if n >= len(seq):
                return
            it = seq[n]
            dst = RAW[:, n % NRAW, 0:it["n"] * it["w"]]
            src = W[it["off"]:it["off"] + 128 * it["n"] * it["w"]].rearrange("(p w) -> p w", p=128)
            it["load"] = Q.dma("sp", f"w{n % NRAW}", Y.dma_start, raw_left[n % NRAW], dst, src)

        def advance():
            while cur["item"] < len(seq):
                n = cur["item"]
                it = seq[n]
                if it["name"] == "ada_w_2":
                    raw_left[n % NRAW] = ada_slot(it, RAW[:, n % NRAW, :].rearrange("p (k w) -> p k w", k=4))
                else:
                    if cur["made"] - cur["used"] >= NPAIR:
                        return
                    p = cur["made"] % NPAIR
                    cur["made"] += 1
                    w = it["n"] * it["w"]
                    hi = s(A.activation, [it["load"]] + pair_left[p], WH[:, p, 0:w], RAW[:, n % NRAW, 0:w], ACT.Copy)
                    lo = v(V.tensor_tensor, [hi], WL[:, p, 0:w], RAW[:, n % NRAW, 0:w], WH[:, p, 0:w].bitcast(F32),
                           ALU.subtract)
                    it["pair"], it["ready"] = p, lo
                    raw_left[n % NRAW] = [lo]
                cur["item"] += 1
                load(n + NRAW)

        def chunk_items(name):
            while chunks[cur["chunk"]][0] == "ada_w_2":
                cur["chunk"] += 1
            assert chunks[cur["chunk"]][0] == name, (chunks[cur["chunk"]], name)
            its = [it for it in seq if it["chunk"] == cur["chunk"]]
            cur["chunk"] += 1
            return its

        def halves(it):
            p, w, n = it["pair"], it["w"], it["n"]
            return [b[:, p, 0:n * w].rearrange("p (k w) -> p k w", k=n) for b in (WH, WL)]

        def drop(it, op):
            pair_left[it["pair"]] = [op]
            cur["used"] += 1

        def mm3(waits, out_, lhs, hi, lo, start, stop):
            m(waits, out_, lhs[0], hi, start=start, stop=False)
            m([], out_, lhs[0], lo, start=False, stop=False)
            return m([], out_, lhs[1], hi, start=False, stop=stop)

        def linear(name, lhs, deps, evac, touter=False, mid=None):
            its = chunk_items(name)
            w, kts = its[0]["w"], its[-1]["a"] + its[-1]["n"]
            ps = [take(), None]
            if touter:
                assert len(its) <= NPAIR
                advance()
                for t in range(2):
                    if t:
                        if mid:
                            mid()
                        ps[1] = take()
                    for it in its:
                        hi, lo = halves(it)
                        for j in range(it["n"]):
                            kt = it["a"] + j
                            op = mm3([it["ready"]] + (deps[t] + ps[t][1] if kt == 0 else []), ps[t][0][:, 0:w],
                                     lhs(kt, t), hi[:, j, :], lo[:, j, :], kt == 0, kt == kts - 1)
                        if t:
                            drop(it, op)
                            advance()
                            yield
                    give(ps[t][0], evac(t, ps[t][0], op))
                flush()
                return
            ps[1] = take()
            for it in its:
                advance()
                hi, lo = halves(it)
                for t in range(2):
                    for j in range(it["n"]):
                        kt = it["a"] + j
                        op = mm3([it["ready"]] + (deps[t] + ps[t][1] if kt == 0 else []), ps[t][0][:, 0:w],
                                 lhs(kt, t), hi[:, j, :], lo[:, j, :], kt == 0, kt == kts - 1)
                    if it is its[-1] and t == 0:
                        op0 = op
                drop(it, op)
                if it is not its[-1]:
                    yield
            give(ps[0][0], evac(0, ps[0][0], op0))
            give(ps[1][0], evac(1, ps[1][0], op))
            flush()
            yield

        def run(gen):
            for _ in gen:
                pass

        def partial(name, lhs, deps, ps, first, last):
            its = chunk_items(name)
            ops = [[None, None], [None, None]]
            for it in its:
                advance()
                hi, lo = halves(it)
                for t in range(2):
                    for c in range(2):
                        for j in range(it["n"]):
                            kt = it["a"] + j
                            f = first and it is its[0] and j == 0
                            ops[t][c] = mm3([it["ready"]] + deps + (ps[t][c][1] if f else []), ps[t][c][0][:, :],
                                            lhs(kt, t), hi[:, j, c * 512:c * 512 + 512],
                                            lo[:, j, c * 512:c * 512 + 512], f,
                                            last and it is its[-1] and j == it["n"] - 1)
                drop(it, ops[1][1])
            flush()
            return ops

        acc_left = [[], []]
        vg = {"left": [[], []], "w": [[], []], "pending": [], "ld": [None, None]}
        mod_w = {}
        state = {"acc": 0, "prev": None}

        def ada_slot(it, view):
            a = state["acc"] % 2
            for j in range(4):
                kt = it["a"] + j
                cs = cond[:, kt:kt + 1]
                if kt == 0:
                    o = v(V.tensor_scalar, [it["load"], w_cond] + acc_left[a], ACC[:, a, :], view[:, j, :], cs, None,
                          ALU.mult)
                else:
                    o = v(V.scalar_tensor_tensor, [it["load"], state["prev"]], out=ACC[:, a, :], in0=view[:, j, :],
                          scalar=cs, in1=ACC[:, a, :], op0=ALU.mult, op1=ALU.add)
                state["prev"] = o
            if it["a"]:
                acc_left[a] = None
                vg["pending"].append((a, it["layer"], it["col"] // 512, o, cur["chunk"]))
                state["acc"] += 1
                if state["acc"] >= 2 and acc_left[state["acc"] % 2] is None:
                    flush(0)
            return [o]

        def flush(age=1):
            while vg["pending"] and cur["chunk"] >= vg["pending"][0][4] + age:
                a, layer, c, o, _ = vg["pending"].pop(0)
                b, bw = take()
                if c // 2 in (2, 5):
                    k = 0 if c < 6 else 1
                    if c % 2 == 0:
                        vg["ld"][k] = pld(f"adag{k}", VG[:, k, :], bc(adagd[layer * 2048 + k * 1024:
                                                                            layer * 2048 + k * 1024 + 1024]),
                                          vg["left"][k])
                        vg["w"][k] = []
                    op = m([o, l_cst] + bw, b[:, :], ones, ACC[:, a, :], start=True, stop=True)
                    gs = VG[:, k, (c % 2) * 512:(c % 2) * 512 + 512]
                    r = v(V.tensor_tensor, [op, vg["ld"][k]], gs, gs, b[:, :], ALU.add)
                    vg["w"][k].append(r)
                else:
                    for q in range(4):
                        op = m(([o, l_cst] + bw) if q == 0 else [], b[:, q:q + 1], ACC[:, a, q * 128:q * 128 + 128],
                               ones[:, 0:1], start=True, stop=True)
                    r = v(V.tensor_tensor, [op, l_colv], modc[:, layer, c * 4:c * 4 + 4],
                          b[:, 0:4], colv[:, K_ADAB + layer * 48 + c * 4:K_ADAB + layer * 48 + c * 4 + 4], ALU.add)
                    mod_w.setdefault((layer, c // 2), []).append(r)
                acc_left[a] = [op]
                give(b, [r])

        ident = cst[:, C_ID:C_ID + 128]
        identb = cstb[:, 0:128]

        def maskb(b):
            return cstb[:, b * 128:b * 128 + 128]

        def pld(name, dst, src, waits=()):
            return Q.dma("pool", name, G.dma_start, list(waits), dst, src)

        l_cst = pld("cst", cst[:, :], cstd[:, :])
        l_pos = pld("pos", posi[:, 0:2], posd)
        l_pos2 = pld("pos2", posi[:, 2:4], pos2d)
        GBT = GB[:, :, :].rearrange("p t n -> p (t n)").rearrange("p (k n) -> p k n", k=8)
        l_xT = Q.dma("act", "xT", A.dma_start, [], GBT, xTd.rearrange("p (k n) -> p k n", k=8))
        l_cb = pld("cstb", SCR[:, 0:896], cstbd[:, :])
        l_cstb = v(V.tensor_copy, [l_cb], cstb[:, :], SCR[:, 0:896])
        def bc(src):
            return src.rearrange("(a n) -> a n", a=1).to_broadcast([128, src.shape[0]])

        l_small = pld("small", small[:, :], bc(smalld))
        l_colv = pld("colv", colv[:, :], colvd[:, :])
        ones = cst[:, C_ONE:C_ONE + 128]
        cond = colv[:, K_C:K_C + 8]
        for n in range(NRAW):
            load(n)
        l_x = Q.dma("sp", "x", Y.dma_start, [], X[:, :, :], xd[0].rearrange("(t p) d -> p t d", p=128))
        w_cond = s(A.activation, [l_colv], cond, cond, ACT.Silu)
        sm = {}
        at = 0
        for nm, n in SMALL:
            sm[nm] = small[:, at:at + n]
            at += n

        w_pf = v(V.tensor_copy, [l_pos, l_pos2], posf[:, :], posi[:, :])
        ang, kk, rr, ab = (trig[:, n, :, :] for n in range(4))
        for t in range(2):
            v(V.tensor_scalar, [w_pf, l_cst], ang[:, t, 0:8], cst[:, C_INV:C_INV + 8], posf[:, t:t + 1], None, ALU.mult)
            w_a = v(V.tensor_scalar, [w_pf], ang[:, t, 8:40], cst[:, C_INV + 8:C_INV + 40], posf[:, 2 + t:3 + t], None,
                    ALU.mult)
        MAGIC = 12582912.0
        C1 = 6.28125
        c2 = 2 * math.pi - C1
        C2 = round(c2 * 2 ** 20) / 2.0 ** 20
        C3 = 2 * math.pi - C1 - C2
        o = v(V.tensor_scalar, [w_a], kk, ang, 1 / (2 * math.pi), MAGIC, ALU.mult, ALU.add)
        o = v(V.tensor_scalar, [o], kk, kk, -MAGIC, None, ALU.add)
        o = v(V.scalar_tensor_tensor, [o], out=rr, in0=kk, scalar=-C1, in1=ang, op0=ALU.mult, op1=ALU.add)
        o = v(V.scalar_tensor_tensor, [o], out=ab, in0=kk, scalar=-C2, in1=rr, op0=ALU.mult, op1=ALU.add)
        o = v(V.scalar_tensor_tensor, [o], out=rr, in0=kk, scalar=-C3, in1=ab, op0=ALU.mult, op1=ALU.add)
        PI = 3.1415925
        w_r = v(V.tensor_scalar, [o], rr, rr, PI, -PI, ALU.min, ALU.max)
        w_ab = v(V.scalar_tensor_tensor, [w_r], out=ab, in0=rr, scalar=-1.0, in1=rr, op0=ALU.mult, op1=ALU.max)
        s(A.activation, [w_r], SIN[:, :, :], rr, ACT.Sin)
        w_trig = s(A.activation, [w_ab], COS[:, :, :], ab, ACT.Sin, bias=cst[:, C_HPI:C_HPI + 1], scale=-1.0)

        def copy(eng, waits, dst, src):
            if eng == "act":
                return s(A.activation, waits, dst, src, ACT.Copy)
            if eng == "dve":
                return v(V.tensor_copy, waits, dst, src)
            return g(G.tensor_copy, waits, dst, src)

        flip = {"n": 0}

        def alt():
            flip["n"] += 1
            return "act" if flip["n"] % 2 else "dve"

        def turn(srcs, deps, dst, rows=128, eng=None):
            out_ops = []
            for a in range(0, len(srcs), 4):
                part = srcs[a:a + 4]
                b, bw = take()
                for j, src in enumerate(part):
                    op = Q.add("pe", M.transpose, (deps + bw) if j == 0 else [],
                               b[0:rows, j * 128:j * 128 + 128], src, ident)
                cp = copy(eng or alt(), [op], dst(a, len(part)),
                          b[0:rows, 0:128 * len(part)].rearrange("p (n q) -> p n q", n=len(part)))
                give(b, [cp])
                out_ops.append(cp)
            return out_ops

        def split(ps, dh, dl, op):
            hi = s(A.activation, op, dh, ps, ACT.Copy)
            return hi, v(V.tensor_tensor, [hi], dl, ps, dh.bitcast(F32), ALU.subtract)

        def turn_halves(srcs, deps, dh, dl, t):
            outs = []
            for a in range(0, len(srcs), 4):
                part = srcs[a:a + 4]
                b, bw = take()
                for j, src in enumerate(part):
                    op = Q.add("pe", M.transpose, (deps + bw) if j == 0 else [], b[:, j * 128:j * 128 + 128], src, ident)
                n = len(part)
                _, lo = split(b[:, 0:128 * n].rearrange("p (n q) -> p n q", n=n),
                              dh[:, a:a + n, t * 128:t * 128 + 128], dl[:, a:a + n, t * 128:t * 128 + 128], [op])
                give(b, [lo])
                outs.append(lo)
            return outs

        def to_XT(src, n, deps, t):
            return turn_halves([src[:, t, k * 128:k * 128 + 128] for k in range(n)], deps, XTH, XTL, t)

        def xt(kt, t):
            return XTH[:, kt, t * 128:t * 128 + 128], XTL[:, kt, t * 128:t * 128 + 128]

        tick = {"n": 0}

        def col(n):
            if tick["n"] + n > 256:
                tick["n"] = 0
            c = tick["n"]
            tick["n"] += n
            return st[:, c:c + n]

        MH = cst[:, C_MH:C_MH + 1]

        def rsqrt(src, waits, scale, eps):
            o1 = g(G.tensor_scalar, waits + [l_cst], src, src, scale, eps, ALU.mult, ALU.add)
            return g(G.tensor_tensor, [o1], src, src, MH.to_broadcast([128, src.shape[1]]), ALU.pow)

        def layer_norm(src, dst, n, gam, bet, waits, vw):
            c = n // 512
            sts = col(6 * c)
            mv = col(2)
            for j in range(c):
                o = v(V.bn_stats, waits, sts[:, 6 * j:6 * j + 6], src[:, j * 512:j * 512 + 512])
            o = v(V.bn_aggr, [o], mv, sts.rearrange("p (c k) -> p c k", k=6))
            r = rsqrt(mv[:, 1:2], [o], 1.0, 1e-5)
            o = v(V.scalar_tensor_tensor, [r] + vw, out=dst, in0=src, scalar=mv[:, 0:1], in1=gam,
                  op0=ALU.subtract, op1=ALU.mult)
            return v(V.scalar_tensor_tensor, [o], out=dst, in0=dst, scalar=mv[:, 1:2], in1=bet,
                     op0=ALU.mult, op1=ALU.add)

        scr_rd = []

        def rope(x, cos, sin, nh, hf, waits, tmp_deps):
            x4 = x.rearrange("p h (a f) -> p h a f", a=2)
            cb = cos.unsqueeze(1).unsqueeze(1).broadcast_to([128, nh, 2, hf])
            sb_ = sin.unsqueeze(1).unsqueeze(1).broadcast_to([128, nh, 2, hf])
            n = nh * 2 * hf
            P4 = SCR[:, 0:n].rearrange("p (h a f) -> p h a f", h=nh, a=2)
            Q4 = SCR[:, 512:512 + n].rearrange("p (h a f) -> p h a f", h=nh, a=2) if n <= 512 else None
            if n > 512:
                raise ValueError("rope too wide")
            o1 = v(V.tensor_tensor, waits + tmp_deps + [w_trig], P4, x4, cb, ALU.mult)
            o2 = v(V.tensor_tensor, [], Q4, x4, sb_, ALU.mult)
            o3 = v(V.tensor_tensor, [o1, o2], x4[:, :, 0, :], P4[:, :, 0, :], Q4[:, :, 1, :], ALU.subtract)
            return v(V.tensor_tensor, [], x4[:, :, 1, :], P4[:, :, 1, :], Q4[:, :, 0, :], ALU.add)

        scr = {"last": [l_cstb]}

        def rope_at(x, cos, sin, nh, hf, waits):
            o = rope(x, cos, sin, nh, hf, waits, scr["last"])
            scr["last"] = [o]
            return o

        def head_rms(x, nh, hd, w, waits, engw="dve"):
            n = nh * hd
            o = s(A.activation, waits + scr["last"], SCR[:, 0:n], x, ACT.Square)
            r = col(nh)
            o = v(V.tensor_reduce, [o], r, SCR[:, 0:n].rearrange("p (h d) -> p h d", h=nh), X_, ALU.add)
            scr["last"] = [o]
            rq = rsqrt(r, [o], 1.0 / hd, 1e-6)
            x3 = x.rearrange("p (h d) -> p h d", h=nh)
            o = v(V.tensor_tensor, [rq], x3, x3, r.unsqueeze(2).broadcast_to([128, nh, hd]), ALU.mult)
            return v(V.tensor_tensor, [o, l_small], x3, x3, w.unsqueeze(1).broadcast_to([128, nh, hd]), ALU.mult)

        buf = {"n": 0}
        e_free = [[], []]
        p_free = [[], []]

        def attention(units, scale, filler=None, steps=1):
            n = len(units)

            def scores(u):
                u["ps"] = []
                u["off"] = []
                off = 0
                for segs in u["banks"]:
                    b, bw = take()
                    c = 0
                    cols = []
                    first = True
                    for lhsT, rhs, nk, masks in segs:
                        op = m((u["deps"] + bw) if first else [], b[:, c:c + nk], lhsT, rhs,
                               start=True, stop=True)
                        first = False
                        for j, (c0, w, mk) in enumerate(masks):
                            op = m([l_cstb] + u.get("mdeps", []), b[:, c + c0:c + c0 + w], identb, mk, start=False,
                                   stop=True, skip_group_check=True)
                        cols.append((c, nk, off))
                        c += nk
                        off += nk
                    u["ps"].append((b, cols, op))

            def maxes(u):
                nseg = sum(len(c) for _, c, _ in u["ps"])
                mx = col(nseg)
                k = 0
                for b, cols, op in u["ps"]:
                    nk = cols[0][1]
                    o = v(V.tensor_reduce, [op], mx[:, k:k + len(cols)],
                          b[:, 0:nk * len(cols)].rearrange("p (n k) -> p n k", k=nk), X_, ALU.max)
                    k += len(cols)
                if u["joint"] and nseg > 1:
                    m1 = col(1)
                    o = v(V.tensor_reduce, [o], m1, mx, X_, ALU.max)
                    mx = m1
                nb = col(mx.shape[1])
                o = v(V.tensor_scalar, [o], nb, mx, -scale, None, ALU.mult)
                i = buf["n"] % 2
                buf["n"] += 1
                u["i"] = i
                k = 0
                if u["joint"]:
                    sums = col(nseg)
                else:
                    sums = u["sums"]
                for b, cols, op in u["ps"]:
                    for c, nk, off in cols:
                        bi = nb[:, 0:1] if u["joint"] else nb[:, k:k + 1]
                        so = sums[:, k:k + 1] if u["joint"] else sums[k]
                        x = s(A.activation, [o] + (e_free[i] if k == 0 else []), E[:, i, off:off + nk],
                              b[:, c:c + nk], ACT.Exp, bias=bi, scale=scale, accum_out=so)
                        k += 1
                    give(b, [x])
                u["x"] = x
                if u["joint"]:
                    u["x2"] = v(V.tensor_reduce, [x], u["sums"][0], sums, X_, ALU.add)
                if u["diff"]:
                    u["diff"](u)

            def turns(u):
                i = u["i"]
                tb = u["blocks"]
                ops = turn([E[:, i, c:c + 128] for c in tb], [u["x"]] + p_free[i],
                           lambda a, c: PET[:, i, a * 128:(a + c) * 128].rearrange("p (n q) -> p n q", n=c))
                u["t"] = ops
                e_free[i] = [ops[-1]]

            def values(u):
                i = u["i"]
                for okey, c0, dv, lst in u["outs"]:
                    ob, ow = okey["bank"]
                    for j, (blk, vap) in enumerate(lst):
                        op = m(u["t"] + ow + u["vdeps"], ob[:, c0:c0 + dv], PET[:, i, blk * 128:blk * 128 + 128], vap,
                               start=(j == 0), stop=(j == len(lst) - 1))
                    okey["op"] = op
                    okey["left"] -= 1
                    if okey["left"] == 0:
                        okey["done"]()
                p_free[i] = [op]

            for k in range(n + 2):
                if k < n:
                    for okey, *_ in units[k]["outs"]:
                        if "bank" not in okey:
                            okey["bank"] = take()
                    scores(units[k])
                    maxes(units[k])
                if filler is not None:
                    for _ in range(steps):
                        next(filler, None)
                if 1 <= k <= n:
                    turns(units[k - 1])
                if k >= 2:
                    values(units[k - 2])

        def okey(n, done):
            return {"left": n, "done": done}

        def normalise(ob, dst, sums, nh, dv, key):
            def done():
                r = col(nh)
                sdeps = key["sdeps"]() if "sdeps" in key else []
                o = v(V.reciprocal, [key["op"]] + sdeps, r, sums)
                o = v(V.tensor_tensor, [o], dst, key["bank"][0][:, 0:nh * dv].rearrange("p (h d) -> p h d", h=nh),
                      r.unsqueeze(2).broadcast_to([128, nh, dv]), ALU.mult)
                give(key["bank"][0], [o])
                key["out"] = o
            return done

        def residual(b, c, t, waits):
            xs = X[:, t, c * 512:c * 512 + 512]
            return v(V.scalar_tensor_tensor, waits, out=xs, in0=xs, scalar=ALPHA, in1=b[:, :],
                     op0=ALU.mult, op1=ALU.add)

        def chain(*gens):
            for ge in gens:
                yield from ge

        vec_left = [[], [], []]
        x_w = [[l_x], [l_x]]
        hi0 = s(A.activation, [l_xT], XTH[:, :, :], GBT, ACT.Copy)
        lo0 = v(V.tensor_tensor, [hi0], XTL[:, :, :], GBT, XTH[:, :, :].bitcast(F32), ALU.subtract)
        xt_w = [[lo0], [lo0]]
        mid_in = None
        gb_free = [lo0]
        sel_left, pt_left, mix_left = [], [], [[], []]

        def ln_pair(waits, gam, bet, vw):
            mvs, rs = [], []
            for t in range(2):
                sts, mv = col(12), col(2)
                for j in range(2):
                    o = v(V.bn_stats, waits[t], sts[:, 6 * j:6 * j + 6], X[:, t, j * 512:j * 512 + 512])
                o = v(V.bn_aggr, [o], mv, sts.rearrange("p (c k) -> p c k", k=6))
                mvs.append(mv)
                rs.append(rsqrt(mv[:, 1:2], [o], 1.0, 1e-5))
            res = []
            for t in range(2):
                xs, mv = X[:, t, :], mvs[t]
                o = v(V.scalar_tensor_tensor, [rs[t]] + vw, out=xs, in0=xs, scalar=mv[:, 0:1], in1=gam,
                      op0=ALU.subtract, op1=ALU.mult)
                res.append([v(V.scalar_tensor_tensor, [o], out=xs, in0=xs, scalar=mv[:, 1:2], in1=bet,
                              op0=ALU.mult, op1=ALU.add)])
            return res

        t_pe = []
        for i in range(2):
            vb = i * 5120
            l_vs = pld("vec2", VEC[:, 2048:3072], bc(vecd[vb + 4096:vb + 5120]), vec_left[2])
            l_v1 = [pld("vec0", VEC[:, 0:1024], bc(vecd[vb:vb + 1024]), vec_left[0]),
                    pld("vec1", VEC[:, 1024:2048], bc(vecd[vb + 1024:vb + 2048]), vec_left[1])]
            SGW = T[:, 9:13, :].rearrange("p a b -> p (a b)").rearrange("p (g t) -> p g t", g=8)
            l_sgw = pld("sgw", SGW, sgwd[i].rearrange("p (g t) -> p g t", g=8), t_pe)
            PR = T[:, 13:15, :]
            l_pT = pld("pT", PR, pTd[i].rearrange("p (k n) -> p k n", k=2), t_pe)
            hw = [[], []]
            cuts = ((0, 364), (364, 728), (728, 1092))
            for c, (a, b) in enumerate(cuts):
                def put(t, bk, op, a=a, b=b):
                    o = copy("act", [op], H[:, t, a:b], bk[:, 0:b - a])
                    hw[t].append(o)
                    return [o]
                run(linear("w_in", xt, xt_w, put, touter=(c == 0), mid=mid_in if c == 0 else None))
            kd = [None, None]
            KD = MIX[:, :, 0:384].rearrange("p t (a b d) -> p t a b d", a=3, b=2)
            gw = [[], []]

            def gelus():
                for c in range(2):
                    def put(t, bk, op, c=c):
                        o = s(A.activation, [op] + gb_free, GB[:, t, c * 512:c * 512 + 512], bk[:, :],
                              ACT.Gelu_apprx_tanh)
                        gw[t].append(o)
                        return [o]
                    yield from linear("w_in", xt, xt_w, put)

            fill = gelus()
            kx = [None, None]
            for t in range(2):
                cs, sn = COS[:, t, 0:8], SIN[:, t, 0:8]
                o2 = rope_at(H[:, t, 768:1088].rearrange("p (h d) -> p h d", d=64)[:, :, 0:16], cs, sn, 5, 8, hw[t])
                k2 = v(V.tensor_copy, [o2] + mix_left[t], KD[:, t, 2, :, :], H[:, t, 1024:1088].unsqueeze(1)
                       .broadcast_to([128, 2, 64]))
                wi = H[:, t, 1088:1092]
                kd[t] = v(V.tensor_scalar, [o2], wi, wi, 1.0 / 16.0, None, ALU.mult)
                o1 = rope_at(H[:, t, 0:640].rearrange("p (h d) -> p h d", d=64)[:, :, 0:16], cs, sn, 10, 8, hw[t])
                k1 = v(V.tensor_copy, [o1], KD[:, t, 0:2, :, :], H[:, t, 512:640].rearrange("p (a d) -> p a d", a=2)
                       .unsqueeze(2).broadcast_to([128, 2, 2, 64]))
                kx[t] = [k1, k2]
            tw = []
            for t in range(2):
                src = ([H[:, t, j * 128:j * 128 + 128] for j in range(4)]
                       + [MIX[:, t, j * 128:j * 128 + 128] for j in range(2)]
                       + [H[:, t, 768 + j * 128:896 + j * 128] for j in range(2)] + [MIX[:, t, 256:384]])
                tw += turn(src, kx[t] + t_pe, lambda a, c, t=t: T[:, a:a + c, t * 128:t * 128 + 128])
                next(fill, None)

            sel_w = [None, None]
            SCs = [SCR[:, 0:128], SCR[:, 256:512]]
            last = [None, None]
            for t in range(2):
                nk = 128 * (t + 1)
                SC = SCs[t]
                o = v(V.tensor_copy, scr["last"] + [l_cst], SC[:, nk - 128:nk], cst[:, C_CM:C_CM + 128])
                acc = [o]
                if t:
                    acc.append(v(V.memset, scr["last"], SC[:, 0:128], 0.0))
                for par in range(2):
                    b, bw = take()
                    for n_, h in enumerate((par, par + 2)):
                        mm = m(tw + bw, b[:, n_ * nk:n_ * nk + nk],
                               T[64 * par:64 * par + 64, 6 + h // 2, t * 128:t * 128 + 128],
                               T[64 * par:64 * par + 64, 8, 0:nk], start=True, stop=True)
                    rl = s(A.activation, [mm] + e_free[par], E[:, par, 0:2 * nk], b[:, 0:2 * nk], ACT.Relu)
                    give(b, [rl])
                    for n_, h in enumerate((par, par + 2)):
                        o = v(V.scalar_tensor_tensor, [rl, kd[t]] + acc, out=SC, in0=E[:, par, n_ * nk:n_ * nk + nk],
                              scalar=H[:, t, 1088 + h:1089 + h], in1=SC, op0=ALU.mult, op1=ALU.add)
                        acc = [o]
                    e_free[par] = [o]
                last[t] = o
            WK = [[SCR[:, 128:256], SCR[:, 0:128]], [SCR[:, 512:768], SCR[:, 256:512]]]
            src = list(SCs)
            for rnd in range(8):
                mx8 = [col(8), col(8)]
                for t in range(2):
                    last[t] = v(V.max, [last[t]], mx8[t], src[t])
                for t in range(2):
                    d_ = WK[t][rnd % 2]
                    last[t] = v(V.match_replace, [last[t]], d_, mx8[t], src[t], -3e38)
                    src[t] = d_
                if rnd % 2:
                    next(fill, None)
            for t in range(2):
                nk = 128 * (t + 1)
                sel_w[t] = v(V.tensor_scalar, [last[t]] + sel_left, selb[:, t, 0:nk], src[t], -2e38, -BIG, ALU.is_gt,
                             ALU.mult)
            scr["last"] = list(sel_w)
            run(fill)
            sp_ = split(PR, PTH[:, :, :], PTL[:, :, :], [l_pT] + pt_left)

            SM = [col(8), col(8)]
            keys_, units = [], []
            for t in range(2):
                nk = 128 * (t + 1)
                ok = okey(8, None)
                ok["done"] = normalise(None, MIX[:, t, 0:512].rearrange("p (h d) -> p h d", h=8), SM[t], 8, 64, ok)
                keys_.append(ok)
                per = 4 // (t + 1)
                for par in range(2):
                    hs = [par + 2 * j for j in range(4)]
                    for a in range(0, 4, per):
                        hh = hs[a:a + per]
                        segs = [(T[64 * par:64 * par + 64, h // 2, t * 128:t * 128 + 128],
                                 T[64 * par:64 * par + 64, 4 + h // 4, 0:nk], nk, [(0, nk, selb[:, t, 0:nk])])
                                for h in hh]
                        outs = [(ok, h * 64, 64, [(n_ * (t + 1) + kb, H[:, kb, 640 + (h // 4) * 64:704 + (h // 4) * 64])
                                                  for kb in range(t + 1)]) for n_, h in enumerate(hh)]
                        units.append(dict(banks=[segs], joint=False, diff=None, deps=tw, mdeps=[sel_w[t]],
                                          vdeps=hw[0] + hw[1],
                                          sums=[SM[t][:, h:h + 1] for h in hh], outs=outs,
                                          blocks=[c * 128 for c in range(per * (t + 1))]))

            sgo = []

            def gating():
                vsw = [layer_norm(GB[:, t, 512:1024], GB[:, t, 512:1024], 512, VEC[:, 2048:2560], VEC[:, 2560:3072],
                                  gw[t], [l_vs]) for t in range(2)]
                vec_left[2] = list(vsw)
                yield
                wm = v(V.tensor_tensor, [l_sgw, l_cst], SGW, SGW,
                       cst[:, C_TRI:C_TRI + 128].unsqueeze(1).broadcast_to([128, 8, 128]), ALU.mult)
                for gh in range(2):
                    b, bw = take()
                    for gg in range(4):
                        gr = gh * 4 + gg
                        mm = m([wm] + vsw + bw, b[:, gg * 128:gg * 128 + 128], SGW[:, gr, :],
                               GB[:, :, 512 + gr * 64:576 + gr * 64], start=True, stop=True)
                    for gg in range(4):
                        gr = gh * 4 + gg
                        o = v(V.scalar_tensor_tensor, [mm, l_colv], out=MIX[:, :, 512 + gr * 64:576 + gr * 64],
                              in0=b[:, gg * 128:gg * 128 + 128].rearrange("p (t d) -> p t d", t=2),
                              scalar=colv[:, K_SGB + i * 8 + gr:K_SGB + i * 8 + gr + 1],
                              in1=GB[:, :, gr * 64:gr * 64 + 64], op0=ALU.add, op1=ALU.mult)
                    give(b, [o])
                    sgo.append(o)
                    yield
            fill = gating()
            attention(units, 0.125, fill)
            run(fill)
            o = sgo[-1]
            t_pe = [keys_[1]["op"]]
            sel_left = [keys_[1]["op"]]

            mo = [to_XT(MIX, 8, [keys_[t]["out"], o], t) for t in range(2)]
            rw = [[], []]
            for c in range(2):
                def put(t, bk, op, c=c):
                    r_ = residual(bk, c, t, [op] + x_w[t])
                    rw[t].append(r_)
                    return [r_]
                run(linear("w_o", xt, mo, put, touter=True))
            x_w = ln_pair(rw, VEC[:, 0:1024], VEC[:, 1024:2048], l_v1)
            vec_left[0] = vec_left[1] = x_w[0] + x_w[1]
            l_v2 = [pld("vec0", VEC[:, 0:1024], bc(vecd[vb + 2048:vb + 3072]), vec_left[0]),
                    pld("vec1", VEC[:, 1024:2048], bc(vecd[vb + 3072:vb + 4096]), vec_left[1])]
            xt_w = [to_XT(X, 8, x_w[0], 0), []]

            def mid1():
                xt_w[1][:] = to_XT(X, 8, x_w[1], 1)

            x_w2 = [[], []]
            for c in range(2):
                sg = [None, None]

                def put(t, bk, op, c=c, sg=sg):
                    sg[t] = s(A.activation, [op], MIX[:, t, c * 512:c * 512 + 512], bk[:, :], ACT.Sigmoid)
                    return [sg[t]]

                def put2(t, bk, op, c=c, sg=sg):
                    ms = MIX[:, t, c * 512:c * 512 + 512]
                    o1 = v(V.tensor_tensor, [op, sg[t]], ms, ms, bk[:, :], ALU.mult)
                    xs = X[:, t, c * 512:c * 512 + 512]
                    o2 = v(V.scalar_tensor_tensor, [o1] + x_w[t] + xt_w[t], out=xs, in0=xs, scalar=ALPHA, in1=ms,
                           op0=ALU.mult, op1=ALU.add)
                    x_w2[t].append(o2)
                    return [o1]

                run(linear("w_ple_gate", xt, xt_w, put, touter=(c == 0), mid=mid1 if c == 0 else None))
                run(linear("w_ple", lambda kt, t: (PTH[:, kt, t * 128:t * 128 + 128], PTL[:, kt, t * 128:t * 128 + 128]),
                           [[sp_[1]], [sp_[1]]], put2))
            x_w = x_w2
            mix_left = [list(x_w[0]), list(x_w[1])]
            f_left = [list(x_w[0]) + list(x_w[1]) + [o]] * 2
            ht_left = [list(t_pe), list(t_pe)]
            acc4 = None
            fw = {}
            for c in range(12):
                if c < 11:
                    fw[c] = []

                    def put(t, bk, op, c=c):
                        gs = GB[:, t, 512 + (c % 2) * 256:768 + (c % 2) * 256]
                        fs = GB[:, t, (c % 2) * 256:(c % 2) * 256 + 256]
                        a1 = s(A.activation, [op] + f_left[c % 2], gs, bk[:, 0:256], ACT.Silu)
                        a2 = v(V.tensor_tensor, [a1], fs, gs, bk[:, 256:512], ALU.mult)
                        fw[c].append(a2)
                        return [a2]
                    gen = linear("w_ffn_in", xt, xt_w, put)
                    next(gen)
                if c:
                    d = c - 1
                    b, bw = take()
                    for q in range(4):
                        kt, t = q // 2, q % 2
                        op = Q.add("pe", M.transpose, (fw[d] + bw) if q == 0 else [], b[:, q * 128:q * 128 + 128],
                                   GB[:, t, (d % 2) * 256 + kt * 128:(d % 2) * 256 + kt * 128 + 128], ident)
                    r2 = 2 * (d % 4)
                    _, lo = split(b[:, :].rearrange("p (n q) -> p n q", n=2), HTH[:, r2:r2 + 2, :],
                                  HTL[:, r2:r2 + 2, :], [op] + ht_left[d % 2])
                    give(b, [lo])
                    f_left[d % 2] = [op] + fw[d]
                if c < 11:
                    run(gen)
                if c:
                    if acc4 is None:
                        acc4 = [[take(), take()], [take(), take()]]
                    ops = partial("w_ffn_out", lambda kt, t, r2=r2: (HTH[:, r2 + kt, t * 128:t * 128 + 128],
                                                                     HTL[:, r2 + kt, t * 128:t * 128 + 128]),
                                  [lo], acc4, d == 0, d == 10)
                    ht_left[d % 2] = [ops[1][1]]
            t_pe = [ops[1][1]]
            gb_free = [op] + fw[10]
            pt_left = list(t_pe)
            rw = [[], []]
            for t in range(2):
                for c in range(2):
                    xs = X[:, t, c * 512:c * 512 + 512]
                    o = v(V.tensor_tensor, [ops[t][c]] + x_w[t], xs, xs, acc4[t][c][0][:, :], ALU.add)
                    give(acc4[t][c][0], [o])
                    rw[t].append(o)
            x_w = ln_pair(rw, VEC[:, 0:1024], VEC[:, 1024:2048], l_v2)
            vec_left[0] = vec_left[1] = x_w[0] + x_w[1]
            vg["left"] = [list(vec_left[0]), list(vec_left[0])]
            if i == 0:
                xt_w = [to_XT(X, 8, x_w[0], 0), []]

                def mid_in():
                    xt_w[1][:] = to_XT(X, 8, x_w[1], 1)

        lv = sm["diff_lambda_2"].rearrange("p (a b d) -> p a b d", a=2, b=2)
        lt = col(2)
        o = v(V.tensor_tensor, [l_small] + scr["last"], SCR[:, 0:128].rearrange("p (a d) -> p a d", a=2), lv[:, :, 0, :],
              lv[:, :, 1, :], ALU.mult)
        o = v(V.tensor_reduce, [o], lt, SCR[:, 0:128].rearrange("p (a d) -> p a d", a=2), X_, ALU.add)
        scr["last"] = [o]
        o = s(A.activation, [o], lt, lt, ACT.Exp)
        o = v(V.tensor_tensor, [o], lam[:, 0:1], lt[:, 0:1], lt[:, 1:2], ALU.subtract)
        w_lam = v(V.tensor_scalar, [o], lam[:, 1:2], lam[:, 0:1], LAM, -1.0, ALU.add, ALU.mult)
        subl = sm["diff_subln_2"]
        w_sub = v(V.tensor_scalar, [l_small], subl, subl, 1.0 - LAM, None, ALU.mult)

        def norm_mod(layer, k, waits):
            ncol = colv[:, K_NRM + layer * 16 + k * 8:K_NRM + layer * 16 + k * 8 + 8]
            scl = modc[:, layer, 24 * k + 8:24 * k + 16]
            shf = modc[:, layer, 24 * k:24 * k + 8]
            wa = v(V.scalar_tensor_tensor, mod_w[(layer, 3 * k + 1)], out=scl, in0=scl, scalar=1.0, in1=ncol,
                   op0=ALU.add, op1=ALU.mult)
            sw = [wa] + mod_w[(layer, 3 * k)] + (t_pe if k else [])
            HM = H[:, :, :].rearrange("p t n -> p (t n)")[:, 0:2048].rearrange("p (k n) -> p k n", k=8) if k else GBT
            hw_ = []
            for t in range(2):
                ss = col(1)
                o = s(A.activation, x_w[t] + waits, MIX[:, t, :], X[:, t, :], ACT.Square, accum_out=ss)
                o = rsqrt(ss, [o], 1.0 / D, 1e-6)
                hw_.append([v(V.tensor_scalar, [o], MIX[:, t, :], X[:, t, :], ss, None, ALU.mult)])
            res = [[], []]

            def go(t):
                last = []
                for a in (0, 4):
                    b, bw = take()
                    for j in range(4):
                        op = Q.add("pe", M.transpose, (hw_[t] + bw) if j == 0 else [], b[:, j * 128:j * 128 + 128],
                                   MIX[:, t, (a + j) * 128:(a + j) * 128 + 128], ident)
                    ls = []
                    for j in range(4):
                        kt = a + j
                        dst = HM[:, kt, t * 128:t * 128 + 128]
                        src = b[:, j * 128:j * 128 + 128]
                        if a == 0:
                            ls.append(s(A.activation, [op] + sw + gb_free, dst, src, ACT.Identity,
                                        bias=shf[:, kt:kt + 1], scale=scl[:, kt:kt + 1]))
                        else:
                            ls.append(v(V.tensor_scalar, [op] + sw + gb_free, dst, src, scl[:, kt:kt + 1],
                                        shf[:, kt:kt + 1], ALU.mult, ALU.add))
                    give(b, ls)
                    _, lo = split(HM[:, a:a + 4, t * 128:t * 128 + 128], XTH[:, a:a + 4, t * 128:t * 128 + 128],
                                  XTL[:, a:a + 4, t * 128:t * 128 + 128], ls)
                    last.append(lo)
                res[t][:] = last

            go(0)
            return res, lambda: go(1)

        def gated_put(c, k, xg):
            def put(t, bk, op):
                ms = MIX[:, t, c * 512:c * 512 + 512]
                o1 = v(V.tensor_tensor, [op] + vg["w"][k] + xt_w[0] + xt_w[1], ms, bk[:, :],
                       VG[:, k, c * 512:c * 512 + 512], ALU.mult)
                vg["left"][k] = [o1]
                xs = X[:, t, c * 512:c * 512 + 512]
                xg[t].append(v(V.tensor_tensor, [o1] + x_w[t], xs, xs, ms, ALU.add))
                return [o1]
            return put

        def put_H(a, b, lst, waits=()):
            def put(t, bk, op):
                o = copy("act", [op] + list(waits), H[:, t, a:b], bk[:, 0:b - a])
                lst[t].append(o)
                return [o]
            return put

        flush(0)
        gb_free = gb_free + x_w[0] + x_w[1]
        mix_rd = []
        for i in range(2):
            xt_w, mid = norm_mod(i, 0, mix_rd)
            gb_x = xt_w
            if i == 0:
                MQ = H[:, :, 2304:3072]
                MK = GB[:, :, 0:768]
                lw = [[], []]
                for n, (a, b) in enumerate(((0, 384), (384, 672))):
                    def put(t, bk, op, a=a, b=b):
                        o = copy("act", [op] + xt_w[0] + xt_w[1], MIX[:, t, a:b], bk[:, 0:b - a])
                        lw[t].append(o)
                        return [o]
                    if n == 0:
                        def put(t, bk, op, a=a, b=b):
                            o = copy("act", [op] + xt_w[t], MIX[:, t, a:b], bk[:, 0:b - a])
                            lw[t].append(o)
                            return [o]
                    run(linear("even_w_in_2", xt, xt_w, put, touter=(n == 0), mid=mid if n == 0 else None))
                lnw = [[], []]
                for t in range(2):
                    for a, n_, nm in ((0, 384, "mla_q_lat_norm_2"), (384, 256, "mla_kv_lat_norm_2")):
                        xs = MIX[:, t, a:a + n_]
                        ss = col(1)
                        o = s(A.activation, lw[t] + scr["last"], SCR[:, 0:n_], xs, ACT.Square, accum_out=ss)
                        scr["last"] = [o]
                        o = rsqrt(ss, [o], 1.0 / n_, 1e-6)
                        lnw[t].append(v(V.scalar_tensor_tensor, [o, l_small], out=xs, in0=xs, scalar=ss, in1=sm[nm],
                                        op0=ALU.mult, op1=ALU.mult))
                ltw = [turn_halves([MIX[:, t, k * 128:k * 128 + 128] for k in range(5)], lnw[t] + t_pe, HTH, HTL, t)
                       for t in range(2)]

                def lat(k0):
                    return lambda kt, t: (HTH[:, k0 + kt, t * 128:t * 128 + 128], HTL[:, k0 + kt, t * 128:t * 128 + 128])

                qw = [[], []]
                for c in range(2):
                    run(linear("mla_w_uq_2", lat(0), ltw, put_H(2304 + c * 384, 2688 + c * 384, qw)))
                kw = [[], []]
                gbr = gb_x[0] + gb_x[1]

                def put(t, bk, op):
                    k3 = MK[:, t, :].rearrange("p (h d) -> p h d", h=8)
                    o = copy("act", [op] + gbr, k3[:, :, 0:64], bk[:, :].rearrange("p (h d) -> p h d", h=8))
                    o3 = copy("dve", lw[t] + gbr, k3[:, :, 64:96],
                              MIX[:, t, 640:672].unsqueeze(1).broadcast_to([128, 8, 32]))
                    kw[t] = [o, o3]
                    return [o]
                run(linear("mla_w_ukv_2", lat(3), ltw, put))
                mvw = []

                def put(t, bk, op):
                    o = copy("act", [op] + vec_left[2], MV[:, t, :], bk[:, :])
                    mvw.append(o)
                    return [o]
                run(linear("mla_w_ukv_2", lat(3), ltw, put))
                dw = [[[], []] for _ in range(3)]

                def dils():
                    for c in range(6):
                        yield from linear("even_w_in_2", xt, xt_w, put_H(c * 384, c * 384 + 384, dw[c // 2]))
                        if c < 4:
                            for t in range(2):
                                xs = H[:, t, c * 384:c * 384 + 384]
                                o_ = head_rms(xs, 6, 64, sm["dil_q_norm_2" if c < 2 else "dil_k_norm_2"],
                                              [dw[c // 2][t][c % 2]])
                                yield
                                qkr[t].append(rope_at(xs.rearrange("p (h d) -> p h d", h=6), COS[:, t, 8:40],
                                                      SIN[:, t, 8:40], 6, 32, [o_]))
                                yield

                qkr = [[], []]
                fill = dils()
                tw = []
                for t in range(2):
                    cs, sn = COS[:, t, 8:40:2], SIN[:, t, 8:40:2]
                    for x_, ww, nm, base in ((MQ, qw, "mla_q_norm_2", 0), (MK, kw, "mla_k_norm_2", 8)):
                        o = head_rms(x_[:, t, :], 8, 96, sm[nm], ww[t])
                        o = rope_at(x_[:, t, :].rearrange("p (h d) -> p h d", h=8)[:, :, 64:96], cs, sn, 8, 16, [o])
                        next(fill, None)
                        tw += turn([x_[:, t, h * 96:h * 96 + 96] for h in range(8)], [o] + t_pe,
                                   lambda a, c, t=t, base=base: T[0:96, base + a:base + a + c, t * 128:t * 128 + 128],
                                   rows=96)
                SMm = [col(8), col(8)]
                keys_, units = [], []
                mla_scale = 96 ** -0.5
                for t in range(2):
                    nk = 128 * (t + 1)
                    ok = okey(8, None)
                    ok["done"] = normalise(None, MIX[:, t, 0:512].rearrange("p (h d) -> p h d", h=8), SMm[t], 8, 64, ok)
                    keys_.append(ok)
                    per = 4 // (t + 1)
                    for a in range(0, 8, per):
                        hh = list(range(a, a + per))
                        segs = [(T[0:96, h, t * 128:t * 128 + 128], T[0:96, 8 + h, 0:nk], nk,
                                 [(nk - 128, 128, maskb(B_TRI))]) for h in hh]
                        outs = [(ok, h * 64, 64, [(n_ * (t + 1) + kb, MV[:, kb, h * 64:h * 64 + 64])
                                                  for kb in range(t + 1)]) for n_, h in enumerate(hh)]
                        units.append(dict(banks=[segs], joint=False, diff=None, deps=tw,
                                          vdeps=mvw, sums=[SMm[t][:, h:h + 1] for h in hh], outs=outs,
                                          blocks=[c * 128 for c in range(per * (t + 1))]))
                attention(units, mla_scale, fill, 3)
                run(fill)
                t_pe = [keys_[1]["op"]]
                tw2 = []
                for t in range(2):
                    for x0, base in ((0, 0), (768, 6)):
                        tw2 += turn([H[:, t, x0 + h * 128:x0 + h * 128 + 128] for h in range(6)], qkr[t] + t_pe,
                                    lambda a, c, t=t, base=base: T[:, base + a:base + a + c, t * 128:t * 128 + 128])
                SMd = [col(4), col(4)]
                units = []
                for t in range(2):
                    nk = 128 * (t + 1)
                    ok = okey(4, None)
                    ok["done"] = normalise(None, MIX[:, t, 512:768].rearrange("p (h d) -> p h d", h=4), SMd[t], 4, 64, ok)
                    keys_.append(ok)
                    for h in range(4):
                        segs = []
                        for gp in range(3):
                            hd = gp * 4 + h
                            bs = 64 * (hd % 2)
                            mk = [(nk - 128, 128, maskb((B_TRI, B_TRI4, B_TRI16)[gp]))]
                            if t:
                                mk.append((0, 128, maskb((B_UP, B_M4, B_M16)[gp])))
                            segs.append((T[bs:bs + 64, hd // 2, t * 128:t * 128 + 128],
                                         T[bs:bs + 64, 6 + hd // 2, 0:nk], nk, mk))
                        outs = [(ok, h * 64, 64, [(gp * (t + 1) + kb,
                                                   H[:, kb, 1536 + (gp * 4 + h) * 64:1600 + (gp * 4 + h) * 64])
                                                  for gp in range(3) for kb in range(t + 1)])]
                        units.append(dict(banks=[segs[0:2], segs[2:3]], joint=True, diff=None, deps=tw2,
                                          vdeps=dw[2][0] + dw[2][1], sums=[SMd[t][:, h:h + 1]], outs=outs,
                                          blocks=[c * 128 for c in range(3 * (t + 1))]))
                attention(units, 0.125)
                t_pe = [keys_[3]["op"]]
                ao_w = [[keys_[0]["out"], keys_[2]["out"]], [keys_[1]["out"], keys_[3]["out"]]]
                n_out, nm_out = 6, "even_w_out_2"
            else:
                dw = [[[], []] for _ in range(6)]

                def part(cs_):
                    for c in cs_:
                        yield from linear("odd_w_in_2", xt, xt_w, put_H(c * 512, c * 512 + 512, dw[c]),
                                          touter=(c == 0), mid=mid if c == 0 else None)

                run(part(range(3)))
                def qk(c, nm, base, fl=None):
                    ops_ = []
                    for t in range(2):
                        xs = H[:, t, c * 512:c * 512 + 512]
                        o = head_rms(xs, 8, 64, sm[nm], dw[c][t])
                        o = rope_at(xs.rearrange("p (h d) -> p h d", h=8), COS[:, t, 8:40], SIN[:, t, 8:40], 8, 32, [o])
                        if fl is not None:
                            next(fl, None)
                        ops_ += turn([xs[:, h * 128:h * 128 + 128] for h in range(4)], [o] + t_pe,
                                     lambda a, c, t=t: T[:, base + a:base + a + c, t * 128:t * 128 + 128])
                    return ops_

                def qk_steps(c, nm, base):
                    for t in range(2):
                        xs = H[:, t, c * 512:c * 512 + 512]
                        o = head_rms(xs, 8, 64, sm[nm], [dw[c][t]])
                        yield
                        o = rope_at(xs.rearrange("p (h d) -> p h d", h=8), COS[:, t, 8:40], SIN[:, t, 8:40], 8, 32, [o])
                        yield
                        twm.extend(turn([xs[:, h * 128:h * 128 + 128] for h in range(4)], [o] + t_pe,
                                        lambda a, c, t=t: T[:, base + a:base + a + c, t * 128:t * 128 + 128]))
                        yield

                twm = []
                fill = chain(part((3,)), qk_steps(3, "moba_q_norm_2", 8), part((4,)), qk_steps(4, "moba_k_norm_2", 12),
                             part((5,)))
                tw = qk(0, "diff_q_norm_2", 0, fill) + qk(1, "diff_k_norm_2", 4, fill)
                units, keys_ = [], []

                def differ(u):
                    i_, t, nk = u["i"], u["tt"], u["nk"]
                    r4 = col(4)
                    o = v(V.reciprocal, [u["x"]], r4, u["s4"])
                    c2_ = col(2)
                    o = v(V.tensor_scalar, [o, w_lam], c2_, r4[:, 2:4], lam[:, 1:2], None, ALU.mult)
                    for n_ in range(2):
                        e1 = E[:, i_, (2 + n_) * nk:(3 + n_) * nk]
                        o1 = v(V.tensor_scalar, [o], e1, e1, c2_[:, n_:n_ + 1], None, ALU.mult)
                    for n_ in range(2):
                        e0 = E[:, i_, n_ * nk:n_ * nk + nk]
                        e1 = E[:, i_, (2 + n_) * nk:(3 + n_) * nk]
                        o1 = v(V.scalar_tensor_tensor, [o1], out=e0, in0=e0, scalar=r4[:, n_:n_ + 1], in1=e1,
                               op0=ALU.mult, op1=ALU.add)
                    u["x"] = o1

                def diff_done(t, ok):
                    def done():
                        dst = MIX[:, t, 0:512]
                        b = ok["bank"][0]
                        o = s(A.activation, [ok["op"]], dst, b[:, :], ACT.Copy)
                        give(b, [o])
                        ok["out"] = head_rms(dst, 4, 128, subl, [o, w_sub])
                    return done

                for t in range(2):
                    nk = 128 * (t + 1)
                    ok = okey(4, None)
                    ok["done"] = diff_done(t, ok)
                    keys_.append(ok)
                    for a in (0, 2):
                        bks = []
                        for mp in range(2):
                            bks.append([(T[64 * mp:64 * mp + 64, h, t * 128:t * 128 + 128],
                                         T[64 * mp:64 * mp + 64, 4 + h, 0:nk], nk, [(nk - 128, 128, maskb(B_TRI))])
                                        for h in (a, a + 1)])
                        s4 = col(4)
                        outs = [(ok, h * 128, 128, [(n_ * (t + 1) + kb, H[:, kb, 1024 + h * 128:1152 + h * 128])
                                                    for kb in range(t + 1)]) for n_, h in enumerate((a, a + 1))]
                        units.append(dict(banks=bks, joint=False, diff=differ, deps=tw, vdeps=dw[2][0] + dw[2][1], s4=s4, tt=t, nk=nk,
                                          sums=[s4[:, j:j + 1] for j in range(4)], outs=outs,
                                          blocks=[c * 128 for c in range(2 * (t + 1))]))
                attention(units, 0.125, fill, 3)
                run(fill)
                tw = twm
                SMb = [col(8), col(8)]
                units = []
                for t in range(2):
                    nk = 128 * (t + 1)
                    ok = okey(8, None)
                    ok["done"] = normalise(None, MIX[:, t, 512:1024].rearrange("p (h d) -> p h d", h=8), SMb[t], 8, 64,
                                           ok)
                    keys_.append(ok)
                    per = 4 // (t + 1)
                    for par in range(2):
                        hs = [par + 2 * j for j in range(4)]
                        for a in range(0, 4, per):
                            hh = hs[a:a + per]
                            segs = [(T[64 * par:64 * par + 64, 8 + h // 2, t * 128:t * 128 + 128],
                                     T[64 * par:64 * par + 64, 12 + h // 2, 0:nk], nk,
                                     [(nk - 128, 128, maskb(B_TRI))]) for h in hh]
                            outs = [(ok, h * 64, 64, [(n_ * (t + 1) + kb, H[:, kb, 2560 + h * 64:2624 + h * 64])
                                                      for kb in range(t + 1)]) for n_, h in enumerate(hh)]
                            units.append(dict(banks=[segs], joint=False, diff=None, deps=tw, vdeps=dw[5][0] + dw[5][1],
                                              sums=[SMb[t][:, h:h + 1] for h in hh], outs=outs,
                                              blocks=[c * 128 for c in range(per * (t + 1))]))
                attention(units, 0.125)
                t_pe = [keys_[3]["op"]]
                ao_w = [[keys_[0]["out"], keys_[2]["out"]], [keys_[1]["out"], keys_[3]["out"]]]
                n_out, nm_out = 8, "odd_w_out_2"
            t_pe = [keys_[3]["op"]]
            xt_w = [to_XT(MIX, n_out, ao_w[t], t) for t in range(2)]
            xg = [[], []]
            for c in range(2):
                run(linear(nm_out, xt, xt_w, gated_put(c, 0, xg), touter=True))
            x_w = xg
            gb_free = list(t_pe)
            xt_w, mid = norm_mod(i, 1, [])
            f_left = [gb_free, gb_free]
            ht_left = [list(t_pe), list(t_pe)]
            acc4 = None
            fw = {}
            FB = [GB[:, :, 0:512], GB[:, :, 512:1024]]
            for c in range(9):
                if c < 8:
                    fw[c] = []

                    def put(t, bk, op, c=c):
                        fs = FB[c % 2][:, t, :]
                        a1 = s(A.activation, [op] + f_left[c % 2], fs, bk[:, :], ACT.Relu)
                        fw[c].append(s(A.activation, [a1], fs, fs, ACT.Square))
                        return [a1]
                    gen = linear("mlp_w1_2", xt, xt_w, put, touter=(c == 0), mid=mid if c == 0 else None)
                    next(gen)
                if c:
                    d = c - 1
                    los = []
                    for hf in range(2):
                        b, bw = take()
                        for q in range(4):
                            kt, t = hf * 2 + q // 2, q % 2
                            op = Q.add("pe", M.transpose, (fw[d] + bw) if q == 0 else [], b[:, q * 128:q * 128 + 128],
                                       FB[d % 2][:, t, kt * 128:kt * 128 + 128], ident)
                        r2 = 4 * (d % 2) + 2 * hf
                        _, lo = split(b[:, :].rearrange("p (n q) -> p n q", n=2), HTH[:, r2:r2 + 2, :],
                                      HTL[:, r2:r2 + 2, :], [op] + ht_left[d % 2])
                        give(b, [lo])
                        los.append(lo)
                    f_left[d % 2] = [op]
                if c < 8:
                    run(gen)
                if c:
                    if acc4 is None:
                        acc4 = [[take(), take()], [take(), take()]]
                    r2 = 4 * (d % 2)
                    ops = partial("mlp_w2_2", lambda kt, t, r2=r2: (HTH[:, r2 + kt, t * 128:t * 128 + 128],
                                                                    HTL[:, r2 + kt, t * 128:t * 128 + 128]),
                                  los, acc4, d == 0, d == 7)
                    ht_left[d % 2] = [ops[1][1]]
            t_pe = [ops[1][1]]
            xg = [[], []]
            for t in range(2):
                for c in range(2):
                    give(acc4[t][c][0], gated_put(c, 1, xg)(t, acc4[t][c][0], ops[t][c]))
            x_w = xg
            gb_free = list(t_pe)
            mix_rd = []
        for t in range(2):
            Q.stores.append(Q.dma("sp", f"out{t}", Y.dma_start, x_w[t], out[0, t * 128:t * 128 + 128, :], X[:, t, :]))

        Q.finish()
        block = ctx.enter_context(nc.Block())

        @block.sync
        def _(eng):
            Q.emit("sp", eng)

        @block.gpsimd
        def _(eng):
            Q.emit("pool", eng)

        @block.scalar
        def _(eng):
            Q.emit("act", eng)

        @block.vector
        def _(eng):
            Q.emit("dve", eng)

        @block.tensor
        def _(eng):
            Q.emit("pe", eng)


def constants():
    c = np.zeros((128, C_END), np.float32)
    q, k = np.arange(128)[:, None], np.arange(128)[None, :]
    c[:, C_ID:C_ID + 128] = np.eye(128)
    c[:, C_CM:C_CM + 128] = np.where(k // 64 <= q // 64, 0.0, -BIG)
    c[:, C_TRI:C_TRI + 128] = q <= k
    c[:, C_INV:C_INV + 8] = np.float32(500000.0) ** (np.float32(-2.0) * np.arange(8, dtype=np.float32) / np.float32(16))
    c[:, C_INV + 8:C_INV + 40] = np.float32(10000.0) ** (-np.arange(32, dtype=np.float32) / np.float32(32))
    c[:, C_HPI] = math.pi / 2
    c[:, C_MH] = -0.5
    c[:, C_ONE:C_ONE + 128] = 1.0
    b = np.zeros((128, 7, 128), np.float32)
    b[:, B_ID] = np.eye(128)
    for n, ok in ((B_TRI, k <= q), (B_UP, k >= q), (B_TRI4, (k <= q) & ((q - k) % 4 == 0)), (B_M4, (q - k) % 4 == 0),
                  (B_TRI16, (k <= q) & ((q - k) % 16 == 0)), (B_M16, (q - k) % 16 == 0)):
        b[:, n] = np.where(ok, 0.0, -BIG)
    return c, b.reshape(128, -1)


def kernel(**inputs):
    import concourse.bacc as _bacc
    from concourse.bass_utils import run_bass_kernel_spmd as _run

    a = {n: np.asarray(x) for n, x in inputs.items()}
    parts = []
    for name, i, (r0, r1), cols in plan():
        w = a[name][i]
        w = w.reshape(w.shape[0], -1)[r0:r1]
        k = r1 - r0
        w = np.concatenate([w[:, c0:c1] for c0, c1 in cols], axis=1)
        w = w.reshape(k // 128, 128, -1).transpose(1, 0, 2)
        for k0, n in pieces(k, w.shape[2]):
            parts.append(w[:, k0:k0 + n, :].reshape(-1))
    cst, cstb = constants()
    x = a["x"]
    arrays = {
        "W": np.concatenate(parts),
        "xd": x,
        "xTd": np.ascontiguousarray(x[0].T.reshape(8, 128, S).transpose(1, 0, 2).reshape(128, -1)),
        "pTd": np.ascontiguousarray(a["p"][:, 0].transpose(0, 2, 1).reshape(2, 2, 128, S).transpose(0, 2, 1, 3)
                                    .reshape(2, 128, -1)),
        "posd": np.ascontiguousarray(a["positions"].reshape(2, 128).T),
        "pos2d": np.ascontiguousarray(a["positions_2"].reshape(2, 128).T),
        "colvd": np.ascontiguousarray(np.concatenate(
            [a["ada_b_2"].reshape(96, 128), np.stack([a["norm_mix_2"], a["norm_mlp_2"]], 1).reshape(32, 128),
             a["c_2"].reshape(8, 128), a["sgu_b"].reshape(16, 128)]).T),
        "cstd": cst,
        "cstbd": cstb,
        "vecd": np.concatenate([a[n][i] for i in range(2) for n in
                                ("ln1_g", "ln1_b", "ln2_g", "ln2_b", "sgu_ln_g", "sgu_ln_b")]),
        "sgwd": np.ascontiguousarray(a["sgu_w"].transpose(0, 3, 1, 2).reshape(2, 128, 1024)),
        "adagd": np.ascontiguousarray(a["ada_b_2"].reshape(2, 6, 1024)[:, [2, 5]].reshape(-1)),
        "smalld": np.concatenate([a[n].reshape(-1) for n, _ in SMALL]),
    }
    nc = _bacc.Bacc("TRN2", target_bir_lowering=False, num_devices=1)
    args = [nc.dram_tensor(n, x_.shape, mybir.dt.from_np(x_.dtype), kind="ExternalInput").ap()
            for n, x_ in arrays.items()]
    args.append(nc.dram_tensor("out", (1, S, D), F32, kind="ExternalOutput").ap())
    program(nc, *args)
    r = _run(nc, [arrays], core_ids=[0])
    return r.results[0]["out"]
```

```python
import math
from contextlib import ExitStack

import numpy as np

import concourse.bass as bass
from concourse import mybir

F32 = mybir.dt.float32
BF16 = mybir.dt.bfloat16
I32 = mybir.dt.int32
ALU = mybir.AluOpType
ACT = mybir.ActivationFunctionType
X_ = mybir.AxisListType.X

F32R = mybir.dt.float32r

S, D = 256, 1024
SLOT = 2048
NRAW = 3
NPAIR = 3
DFF = 2816
ALPHA = 4 ** 0.25
BIG = 1e30
LAM = 0.8 - 0.6 * math.exp(-0.3)

C_ID, C_CM, C_TRI, C_INV, C_HPI, C_MH, C_ONE, C_END = 0, 128, 256, 384, 424, 425, 426, 554
B_ID, B_TRI, B_UP, B_TRI4, B_M4, B_TRI16, B_M16 = range(7)
K_ADAB, K_NRM, K_C, K_SGB, K_END = 0, 96, 128, 136, 152
SMALL = [("mla_q_lat_norm_2", 384), ("mla_kv_lat_norm_2", 256), ("mla_q_norm_2", 96), ("mla_k_norm_2", 96),
         ("dil_q_norm_2", 64), ("dil_k_norm_2", 64), ("diff_q_norm_2", 64), ("diff_k_norm_2", 64),
         ("diff_subln_2", 128), ("moba_q_norm_2", 64), ("moba_k_norm_2", 64), ("diff_lambda_2", 256)]
NSMALL = sum(n for _, n in SMALL)


ADA = [(0, c) for c in (0, 1, 2, 3, 6, 7, 8, 9, 4, 5, 10, 11)] + [(1, c) for c in (0, 1, 2, 3, 6, 7, 8, 9, 4, 5, 10, 11)]


def plan():
    out = []

    def all_rows(name, i, k, *cuts):
        for cols in cuts:
            out.append((name, i, (0, k), cols if isinstance(cols, list) else [cols]))

    def ada(i, *cs):
        for c in cs:
            out.append(("ada_w_2", i, (0, 1024), [(c * 512, c * 512 + 512)]))

    halves = ((0, 512), (512, 1024))
    for i in range(2):
        all_rows("w_in", i, 1024, (0, 364), (364, 728), (728, 1092), (1092, 1604), (1604, 2116))
        all_rows("w_o", i, 1024, *halves)
        all_rows("w_ple", i, 256, *halves)
        all_rows("w_ple_gate", i, 1024, *halves)
        for c in range(12):
            if c < 11:
                all_rows("w_ffn_in", i, 1024, [(c * 256, c * 256 + 256), (DFF + c * 256, DFF + c * 256 + 256)])
            if 1 <= c <= 8:
                ada(*ADA[i * 8 + c - 1])
            if c:
                out.append(("w_ffn_out", i, (c * 256 - 256, c * 256), [(0, 1024)]))
    for i in range(2):
        if i == 0:
            all_rows("even_w_in_2", 0, 1024, (0, 384), (384, 672))
            all_rows("mla_w_uq_2", 0, 384, (0, 384), (384, 768))
            all_rows("mla_w_ukv_2", 0, 256, [(h * 128, h * 128 + 64) for h in range(8)],
                     [(h * 128 + 64, h * 128 + 128) for h in range(8)])
            all_rows("even_w_in_2", 0, 1024, (2208, 2592), (2592, 2976), (672, 1056))
            all_rows("even_w_in_2", 0, 1024, (1056, 1440), (1440, 1824), (1824, 2208))
            all_rows("even_w_out_2", 0, 768, *halves)
        else:
            all_rows("odd_w_in_2", 0, 1024, (0, 512), (512, 1024), (1024, 1536))
            all_rows("odd_w_in_2", 0, 1024, (1536, 2048), (2048, 2560))
            all_rows("odd_w_in_2", 0, 1024, (2560, 3072))
            all_rows("odd_w_out_2", 0, 1024, *halves)
        for c in range(9):
            if c < 8:
                all_rows("mlp_w1_2", i, 1024, (c * 512, c * 512 + 512))
            if i == 0 and c < 8:
                ada(*ADA[16 + c])
            if c:
                out.append(("mlp_w2_2", i, (c * 512 - 512, c * 512), [(0, 1024)]))
    return out


def pieces(k, w):
    per = SLOT // w
    kt = k // 128
    return [(a, min(per, kt - a)) for a in range(0, kt, per)]


def width(cols):
    return sum(b - a for a, b in cols)


def total():
    return sum((r1 - r0) * width(cols) for _, _, (r0, r1), cols in plan())


class Op:
    def __init__(self, eng, f, waits, a, k):
        self.eng, self.f, self.waits, self.a, self.k = eng, f, waits, a, k
        self.used, self.sem, self.val = False, None, 0


class Queue:

    def __init__(self, nc, sem):
        self.nc, self.sem = nc, sem
        self.q = {"pe": [], "dve": [], "act": [], "pool": [], "sp": []}
        self.esem = {e: sem("s_" + e) for e in self.q}
        self.dcount = {}
        self.stores = []

    def add(self, eng, f, waits, *a, **k):
        flat = []
        for w in waits:
            flat.extend(w if isinstance(w, (list, tuple)) else [w])
        op = Op(eng, f, flat, a, k)
        for w in flat:
            w.used = True
        self.q[eng].append(op)
        return op

    def dma(self, eng, name, f, waits, dst, src):
        op = self.add(eng, f, waits, dst, src)
        if name not in self.dcount:
            self.dcount[name] = [self.sem("d_" + name), 0]
        c = self.dcount[name]
        c[1] += 16
        op.sem, op.val = c[0], c[1]
        return op

    def finish(self):
        for e, ops in self.q.items():
            n = 0
            for op in ops:
                if op.sem is None and op.used:
                    n += 1
                    op.val = n

    def emit(self, e, eng):
        seen = {}
        for op in self.q[e]:
            need = {}
            for w in op.waits:
                s = w.sem if w.sem is not None else self.esem[w.eng]
                need[id(s)] = (s, max(w.val, need.get(id(s), (s, 0))[1]))
            for i, (s, v) in need.items():
                if seen.get(i, 0) < v:
                    eng.wait_ge(s, v)
                    seen[i] = v
            ins = op.f(*op.a, **op.k)
            if op.sem is not None:
                ins.then_inc(op.sem, 16)
            elif op.used:
                ins.then_inc(self.esem[e], 1)
        for op in self.stores:
            if op.eng == e:
                eng.wait_ge(op.sem, op.val)


def program(nc, W, xd, xTd, pTd, posd, pos2d, colvd, cstd, cstbd, vecd, sgwd, smalld, out):
    with ExitStack() as ctx:
        def sb(name, shape, dt=F32):
            return ctx.enter_context(nc.sbuf_tensor(name, shape, dt))

        def sem(name):
            return ctx.enter_context(nc.semaphore(name))

        Q = Queue(nc, sem)
        V, A, G, M, Y = nc.vector, nc.scalar, nc.gpsimd, nc.tensor, nc.sync

        def v(f, waits, *a, **k):
            return Q.add("dve", f, waits, *a, **k)

        def s(f, waits, *a, **k):
            return Q.add("act", f, waits, *a, **k)

        def g(f, waits, *a, **k):
            return Q.add("pool", f, waits, *a, **k)

        def m(waits, *a, **k):
            return Q.add("pe", M.matmul, waits, *a, **k)

        RAW = sb("RAW", [128, NRAW, SLOT])
        WH = sb("WH", [128, NPAIR, SLOT], F32R)
        WL = sb("WL", [128, NPAIR, SLOT], F32R)
        X = sb("X", [128, 2, 1024])
        XTH = sb("XTH", [128, 8, 256], F32R)
        XTL = sb("XTL", [128, 8, 256], F32R)
        MIX = sb("MIX", [128, 2, 1024])
        H = sb("H", [128, 2, 3072])
        GB = sb("GB", [128, 2, 1024])
        VEC = sb("VEC", [128, 3072])
        VG = VEC[:, 0:2048].rearrange("p (a n) -> p a n", a=2)
        MV = VEC[:, 2048:3072].rearrange("p (t n) -> p t n", t=2)
        E = sb("E", [128, 2, 1024])
        PET = sb("PET", [128, 2, 768])
        SCR = sb("SCR", [128, 1024])
        SQ = sb("SQ", [128, 512])
        ACC = sb("ACC", [128, 2, 512])
        with nc.sbuf_tensor("TB", [128, 4, 2, 2, 64], F32) as TB:
            pass
        PTH = sb("PTH", [128, 2, 256], F32R)
        PTL = sb("PTL", [128, 2, 256], F32R)
        cst = sb("cst", [128, C_END])
        cstb = sb("cstb", [128, 7 * 128], BF16)
        selb = sb("selb", [128, 2, 256], BF16)
        small = sb("small", [128, NSMALL])
        colv = sb("colv", [128, K_END])
        modc = sb("modc", [128, 2, 48])
        posi = sb("posi", [128, 4], I32)
        posf = sb("posf", [128, 4])
        trig = sb("trig", [128, 4, 2, 40])
        COS = sb("COS", [128, 2, 40])
        SIN = sb("SIN", [128, 2, 40])
        st = sb("st", [128, 256])
        lam = sb("lam", [128, 2])
        with nc.sbuf_tensor("T", [128, 16, 256], F32) as T:
            pass
        HTH = sb("HTH", [128, 8, 256], F32R)
        HTL = sb("HTL", [128, 8, 256], F32R)
        banks = [ctx.enter_context(nc.psum_tensor(f"ps{i}", [128, 512], F32)) for i in range(8)]

        free = [(b, []) for b in banks]

        def take():
            return free.pop(0)

        def give(bank, ops):
            free.append((bank, list(ops)))

        chunks = plan()
        seq, later = [], []
        off = 0
        for n, (name, i, (r0, r1), cols) in enumerate(chunks):
            w = width(cols)
            for a, c in pieces(r1 - r0, w):
                it = dict(name=name, layer=i, chunk=n, a=a, n=c, w=w, off=off, col=cols[0][0])
                off += 128 * c * w
                if name == "ada_w_2":
                    later.append(it)
                else:
                    seq.append(it)
                    if later:
                        seq.append(later.pop(0))
        cur = {"chunk": 0, "item": 0, "made": 0, "used": 0}
        raw_left = [[] for _ in range(NRAW)]
        pair_left = [[] for _ in range(NPAIR)]

        def load(n):
            if n >= len(seq):
                return
            it = seq[n]
            dst = RAW[:, n % NRAW, 0:it["n"] * it["w"]]
            src = W[it["off"]:it["off"] + 128 * it["n"] * it["w"]].rearrange("(p w) -> p w", p=128)
            it["load"] = Q.dma("sp", f"w{n % NRAW}", Y.dma_start, raw_left[n % NRAW], dst, src)

        def advance(most=NPAIR):
            while cur["item"] < len(seq) and most:
                n = cur["item"]
                it = seq[n]
                if it["name"] == "ada_w_2":
                    raw_left[n % NRAW] = ada_slot(it, RAW[:, n % NRAW, :].rearrange("p (k w) -> p k w", k=4))
                else:
                    if cur["made"] - cur["used"] >= NPAIR:
                        return
                    most -= 1
                    p = cur["made"] % NPAIR
                    cur["made"] += 1
                    w = it["n"] * it["w"]
                    hi = s(A.activation, [it["load"]] + pair_left[p], WH[:, p, 0:w], RAW[:, n % NRAW, 0:w], ACT.Copy)
                    lo = v(V.tensor_tensor, [hi], WL[:, p, 0:w], RAW[:, n % NRAW, 0:w], WH[:, p, 0:w].bitcast(F32),
                           ALU.subtract)
                    it["pair"], it["ready"] = p, lo
                    raw_left[n % NRAW] = [lo]
                cur["item"] += 1
                load(n + NRAW)

        def chunk_items(name):
            while chunks[cur["chunk"]][0] == "ada_w_2":
                cur["chunk"] += 1
            assert chunks[cur["chunk"]][0] == name, (chunks[cur["chunk"]], name)
            its = [it for it in seq if it["chunk"] == cur["chunk"]]
            cur["chunk"] += 1
            return its

        def halves(it):
            p, w, n = it["pair"], it["w"], it["n"]
            return [b[:, p, 0:n * w].rearrange("p (k w) -> p k w", k=n) for b in (WH, WL)]

        def drop(it, op):
            pair_left[it["pair"]] = [op]
            cur["used"] += 1

        def mm3(waits, out_, lhs, hi, lo, start, stop):
            m(waits, out_, lhs[0], hi, start=start, stop=False)
            m([], out_, lhs[0], lo, start=False, stop=False)
            return m([], out_, lhs[1], hi, start=False, stop=stop)

        def linear(name, lhs, deps, evac, touter=False, mid=None, guard=None):
            its = chunk_items(name)
            w, kts = its[0]["w"], its[-1]["a"] + its[-1]["n"]
            ps = [take(), None]
            if touter:
                assert len(its) <= NPAIR
                advance()
                for t in range(2):
                    if t:
                        while guard is not None and not guard():
                            yield
                        if mid:
                            mid()
                        ps[1] = take()
                    for it in its:
                        hi, lo = halves(it)
                        for j in range(it["n"]):
                            kt = it["a"] + j
                            op = mm3([it["ready"]] + (deps[t] + ps[t][1] if kt == 0 else []), ps[t][0][:, 0:w],
                                     lhs(kt, t), hi[:, j, :], lo[:, j, :], kt == 0, kt == kts - 1)
                        if t:
                            drop(it, op)
                            if it is its[0]:
                                advance(1)
                        if it is not its[-1]:
                            yield
                    give(ps[t][0], evac(t, ps[t][0], op))
                advance()
                flush()
                yield
                return
            ps[1] = take()
            for it in its:
                advance()
                hi, lo = halves(it)
                for t in range(2):
                    for j in range(it["n"]):
                        kt = it["a"] + j
                        op = mm3([it["ready"]] + (deps[t] + ps[t][1] if kt == 0 else []), ps[t][0][:, 0:w],
                                 lhs(kt, t), hi[:, j, :], lo[:, j, :], kt == 0, kt == kts - 1)
                    if it is its[-1] and t == 0:
                        op0 = op
                drop(it, op)
                if it is not its[-1]:
                    yield
            give(ps[0][0], evac(0, ps[0][0], op0))
            give(ps[1][0], evac(1, ps[1][0], op))
            flush()
            yield

        def linear2(name, lhs, deps, evacs, mid):
            ia, ib = chunk_items(name), chunk_items(name)
            assert len(ia) == 2 and len(ib) == 2
            advance()
            ps = [[take(), None], [take(), None]]

            def slot(it, c, t, kts):
                hi, lo = halves(it)
                w = it["w"]
                for j in range(it["n"]):
                    kt = it["a"] + j
                    op = mm3([it["ready"]] + (deps[t] + ps[c][t][1] if kt == 0 else []), ps[c][t][0][:, 0:w],
                             lhs(kt, t), hi[:, j, :], lo[:, j, :], kt == 0, kt == kts - 1)
                return op

            na, nb_ = (i_[-1]["a"] + i_[-1]["n"] for i_ in (ia, ib))
            for t in range(2):
                if t:
                    ps[0][1], ps[1][1] = take(), take()
                for it in ia:
                    op = slot(it, 0, t, na)
                    if t:
                        drop(it, op)
                        if it is ia[0]:
                            advance(1)
                    elif it is ia[0]:
                        mid()
                give(ps[0][t][0], evacs[0](t, ps[0][t][0], op))
                if t:
                    advance(1)
                op = slot(ib[0], 1, t, nb_)
            drop(ib[0], op)
            yield
            advance()
            ops = [slot(ib[1], 1, t, nb_) for t in range(2)]
            drop(ib[1], ops[1])
            for t in range(2):
                give(ps[1][t][0], evacs[1](t, ps[1][t][0], ops[t]))
            flush()
            yield

        def run(gen):
            for _ in gen:
                pass

        def partial(name, parts, ps, first, last, evac=None):
            ops = [[None, None], [None, None]]
            its = []
            for lhs, deps in parts:
                its += [(it, lhs, deps) for it in chunk_items(name)]

            def one(n, t):
                it, lhs, deps = its[n]
                hi, lo = halves(it)
                for c in range(2):
                    for j in range(it["n"]):
                        kt = it["a"] + j
                        f = first and n == 0 and j == 0
                        ops[t][c] = mm3([it["ready"]] + deps + (ps[t][c][1] if f else []), ps[t][c][0][:, :],
                                        lhs(kt, t), hi[:, j, c * 512:c * 512 + 512], lo[:, j, c * 512:c * 512 + 512],
                                        f, last and n == len(its) - 1 and j == it["n"] - 1)

            if evac is None:
                for n in range(len(its)):
                    advance()
                    one(n, 0)
                    one(n, 1)
                    drop(its[n][0], ops[1][1])
            else:
                assert len(its) <= NPAIR
                advance()
                for t in range(2):
                    for n in range(len(its)):
                        one(n, t)
                        if t:
                            drop(its[n][0], ops[1][1])
                    evac(t, ops[t])
                advance()
            flush()
            return ops

        acc_left = [[], []]
        vg = {"left": [[], []], "w": [[], []], "pending": []}
        mod_w = {}
        state = {"acc": 0, "prev": None}

        def ada_slot(it, view):
            a = state["acc"] % 2
            for j in range(4):
                kt = it["a"] + j
                cs = cond[:, kt:kt + 1]
                if kt == 0:
                    o = v(V.tensor_scalar, [it["load"], w_cond] + acc_left[a], ACC[:, a, :], view[:, j, :], cs, None,
                          ALU.mult)
                else:
                    o = v(V.scalar_tensor_tensor, [it["load"], state["prev"]], out=ACC[:, a, :], in0=view[:, j, :],
                          scalar=cs, in1=ACC[:, a, :], op0=ALU.mult, op1=ALU.add)
                state["prev"] = o
            if it["a"]:
                acc_left[a] = None
                vg["pending"].append((a, it["layer"], it["col"] // 512, o, cur["chunk"]))
                state["acc"] += 1
                if state["acc"] >= 2 and acc_left[state["acc"] % 2] is None:
                    flush(0, 1)
            return [o]

        def flush(age=1, most=9):
            while most and vg["pending"] and cur["chunk"] >= vg["pending"][0][4] + age:
                most -= 1
                a, layer, c, o, _ = vg["pending"].pop(0)
                b, bw = take()
                for q in range(4):
                    op = m(([o, l_cst] + bw) if q == 0 else [], b[:, q:q + 1], ACC[:, a, q * 128:q * 128 + 128],
                           ones[:, 0:1], start=True, stop=True)
                r = v(V.tensor_tensor, [op, l_colv], modc[:, layer, c * 4:c * 4 + 4],
                      b[:, 0:4], colv[:, K_ADAB + layer * 48 + c * 4:K_ADAB + layer * 48 + c * 4 + 4], ALU.add)
                mod_w.setdefault((layer, c // 2), []).append(r)
                acc_left[a] = [op]
                give(b, [r])

        ident = cst[:, C_ID:C_ID + 128]
        identb = cstb[:, 0:128]

        def maskb(b):
            return cstb[:, b * 128:b * 128 + 128]

        def pld(name, dst, src, waits=()):
            return Q.dma("pool", name, G.dma_start, list(waits), dst, src)

        l_cst = pld("cst", cst[:, :], cstd[:, :])
        l_pos = pld("pos", posi[:, 0:2], posd)
        l_pos2 = pld("pos2", posi[:, 2:4], pos2d)
        GBT = GB[:, :, :].rearrange("p t n -> p (t n)").rearrange("p (k n) -> p k n", k=8)
        l_xT = Q.dma("act", "xT", A.dma_start, [], GBT, xTd.rearrange("p (k n) -> p k n", k=8))
        l_cb = pld("cstb", SCR[:, 0:896], cstbd[:, :])
        def bc(src):
            return src.rearrange("(a n) -> a n", a=1).to_broadcast([128, src.shape[0]])

        l_small = pld("small", small[:, :], bc(smalld))
        l_colv = pld("colv", colv[:, :], colvd[:, :])
        ones = cst[:, C_ONE:C_ONE + 128]
        cond = colv[:, K_C:K_C + 8]
        for n in range(NRAW):
            load(n)
        l_x = Q.dma("sp", "x", Y.dma_start, [], X[:, :, :], xd[0].rearrange("(t p) d -> p t d", p=128))
        xt_w = []
        advance(1)
        for t in range(2):
            dh, dl = (b[:, :, t * 128:t * 128 + 128] for b in (XTH, XTL))
            src = GBT[:, :, t * 128:t * 128 + 128]
            hi0 = s(A.activation, [l_xT], dh, src, ACT.Copy)
            xt_w.append([v(V.tensor_tensor, [hi0], dl, src, dh.bitcast(F32), ALU.subtract)])
            if t == 0:
                advance()
        l_cstb = v(V.tensor_copy, [l_cb], cstb[:, :], SCR[:, 0:896])
        w_cond = s(A.activation, [l_colv], cond, cond, ACT.Silu)
        sm = {}
        at = 0
        for nm, n in SMALL:
            sm[nm] = small[:, at:at + n]
            at += n

        w_pf = v(V.tensor_copy, [l_pos, l_pos2], posf[:, :], posi[:, :])
        ang, kk, rr, ab = (trig[:, n, :, :] for n in range(4))
        for t in range(2):
            v(V.tensor_scalar, [w_pf, l_cst], ang[:, t, 0:8], cst[:, C_INV:C_INV + 8], posf[:, t:t + 1], None, ALU.mult)
            w_a = v(V.tensor_scalar, [w_pf], ang[:, t, 8:40], cst[:, C_INV + 8:C_INV + 40], posf[:, 2 + t:3 + t], None,
                    ALU.mult)
        MAGIC = 12582912.0
        C1 = 6.28125
        c2 = 2 * math.pi - C1
        C2 = round(c2 * 2 ** 20) / 2.0 ** 20
        C3 = 2 * math.pi - C1 - C2
        o = v(V.tensor_scalar, [w_a], kk, ang, 1 / (2 * math.pi), MAGIC, ALU.mult, ALU.add)
        o = v(V.tensor_scalar, [o], kk, kk, -MAGIC, None, ALU.add)
        o = v(V.scalar_tensor_tensor, [o], out=rr, in0=kk, scalar=-C1, in1=ang, op0=ALU.mult, op1=ALU.add)
        o = v(V.scalar_tensor_tensor, [o], out=ab, in0=kk, scalar=-C2, in1=rr, op0=ALU.mult, op1=ALU.add)
        o = v(V.scalar_tensor_tensor, [o], out=rr, in0=kk, scalar=-C3, in1=ab, op0=ALU.mult, op1=ALU.add)
        PI = 3.1415925
        w_r = v(V.tensor_scalar, [o], rr, rr, PI, -PI, ALU.min, ALU.max)
        w_ab = v(V.scalar_tensor_tensor, [w_r], out=ab, in0=rr, scalar=-1.0, in1=rr, op0=ALU.mult, op1=ALU.max)
        s(A.activation, [w_r], SIN[:, :, :], rr, ACT.Sin)
        w_trig = s(A.activation, [w_ab], COS[:, :, :], ab, ACT.Sin, bias=cst[:, C_HPI:C_HPI + 1], scale=-1.0)

        def copy(eng, waits, dst, src):
            if eng == "act":
                return s(A.activation, waits, dst, src, ACT.Copy)
            if eng == "dve":
                return v(V.tensor_copy, waits, dst, src)
            return g(G.tensor_copy, waits, dst, src)

        flip = {"n": 0}

        def alt():
            flip["n"] += 1
            return "act" if flip["n"] % 3 else "dve"

        def turn(srcs, deps, dst, rows=128, eng=None):
            out_ops = []
            for a in range(0, len(srcs), 4):
                part = srcs[a:a + 4]
                b, bw = take()
                for j, src in enumerate(part):
                    op = Q.add("pe", M.transpose, (deps + bw) if j == 0 else [],
                               b[0:rows, j * 128:j * 128 + 128], src, ident)
                cp = copy(eng or alt(), [op], dst(a, len(part)),
                          b[0:rows, 0:128 * len(part)].rearrange("p (n q) -> p n q", n=len(part)))
                give(b, [cp])
                out_ops.append(cp)
            return out_ops

        def split(ps, dh, dl, op):
            hi = s(A.activation, op, dh, ps, ACT.Copy)
            return hi, v(V.tensor_tensor, [hi], dl, ps, dh.bitcast(F32), ALU.subtract)

        def turn_halves(srcs, deps, dh, dl, t):
            outs = []
            for a in range(0, len(srcs), 4):
                part = srcs[a:a + 4]
                b, bw = take()
                for j, src in enumerate(part):
                    op = Q.add("pe", M.transpose, (deps + bw) if j == 0 else [], b[:, j * 128:j * 128 + 128], src, ident)
                n = len(part)
                _, lo = split(b[:, 0:128 * n].rearrange("p (n q) -> p n q", n=n),
                              dh[:, a:a + n, t * 128:t * 128 + 128], dl[:, a:a + n, t * 128:t * 128 + 128], [op])
                give(b, [lo])
                outs.append(lo)
            return outs

        def to_XT(src, n, deps, t):
            return turn_halves([src[:, t, k * 128:k * 128 + 128] for k in range(n)], deps, XTH, XTL, t)

        def xt(kt, t):
            return XTH[:, kt, t * 128:t * 128 + 128], XTL[:, kt, t * 128:t * 128 + 128]

        tick = {"n": 0}

        def col(n):
            if tick["n"] + n > 256:
                tick["n"] = 0
            c = tick["n"]
            tick["n"] += n
            return st[:, c:c + n]

        MH = cst[:, C_MH:C_MH + 1]

        def rsqrt(src, waits, scale, eps):
            o1 = g(G.tensor_scalar, waits + [l_cst], src, src, scale, eps, ALU.mult, ALU.add)
            return g(G.tensor_tensor, [o1], src, src, MH.to_broadcast([128, src.shape[1]]), ALU.pow)

        sq_left = [[]]

        def layer_norms(xs, n, gam, bet, waits, vw):
            mean, ss, nb = ([col(1) for _ in xs] for _ in range(3))
            o = [None] * len(xs)
            for j, x in enumerate(xs):
                o[j] = s(A.activation, [waits[j]] + sq_left[0], SQ[:, 0:n], x, ACT.Copy, accum_out=mean[j])
                sq_left[0] = [o[j]]
            for j, x in enumerate(xs):
                o[j] = g(G.tensor_scalar, [o[j]], mean[j], mean[j], -1.0 / n, None, ALU.mult)
            for j, x in enumerate(xs):
                o[j] = s(A.activation, [o[j]] + sq_left[0], SQ[:, 0:n], x, ACT.Square, bias=mean[j], accum_out=ss[j])
                sq_left[0] = [o[j]]
            for j, x in enumerate(xs):
                o[j] = rsqrt(ss[j], [o[j]], 1.0 / n, 1e-5)
                o[j] = g(G.tensor_tensor, [o[j]], nb[j], mean[j], ss[j], ALU.mult)
            for j, x in enumerate(xs):
                o[j] = s(A.activation, [o[j]], x, x, ACT.Identity, bias=nb[j], scale=ss[j])
            for j, x in enumerate(xs):
                o[j] = g(G.tensor_tensor, [o[j]] + vw, x, x, gam, ALU.mult)
            for j, x in enumerate(xs):
                o[j] = g(G.tensor_tensor, [o[j]], x, x, bet, ALU.add)
            return o

        def rope(x, cos, sin, nh, hf, waits, tmp_deps, tw_):
            x4 = x.rearrange("p h (a f) -> p h a f", a=2)
            if len(cos.shape) == 2:
                cos, sin = (a.unsqueeze(1).broadcast_to([128, 2, hf]) for a in (cos, sin))
            cb = cos.unsqueeze(1).broadcast_to([128, nh, 2, hf])
            sb_ = sin.unsqueeze(1).broadcast_to([128, nh, 2, hf])
            n = nh * 2 * hf
            P4 = SCR[:, 0:n].rearrange("p (h a f) -> p h a f", h=nh, a=2)
            Q4 = SCR[:, 512:512 + n].rearrange("p (h a f) -> p h a f", h=nh, a=2) if n <= 512 else None
            if n > 512:
                raise ValueError("rope too wide")
            o1 = v(V.tensor_tensor, waits + tmp_deps + [w_trig] + tw_, P4, x4, cb, ALU.mult)
            o2 = v(V.tensor_tensor, [], Q4, x4, sb_, ALU.mult)
            o3 = v(V.tensor_tensor, [o1, o2], x4[:, :, 0, :], P4[:, :, 0, :], Q4[:, :, 1, :], ALU.subtract)
            return v(V.tensor_tensor, [], x4[:, :, 1, :], P4[:, :, 1, :], Q4[:, :, 0, :], ALU.add)

        scr = {"last": [l_cstb]}

        def rope_at(x, cos, sin, nh, hf, waits, tw_=()):
            o = rope(x, cos, sin, nh, hf, waits, scr["last"], list(tw_))
            scr["last"] = [o]
            return o

        def head_rms(x, nh, hd, w, waits, engw="dve"):
            n = nh * hd
            o = s(A.activation, waits + scr["last"], SCR[:, 0:n], x, ACT.Square)
            r = col(nh)
            o = v(V.tensor_reduce, [o], r, SCR[:, 0:n].rearrange("p (h d) -> p h d", h=nh), X_, ALU.add)
            scr["last"] = [o]
            rq = rsqrt(r, [o], 1.0 / hd, 1e-6)
            x3 = x.rearrange("p (h d) -> p h d", h=nh)
            o = v(V.tensor_tensor, [rq], x3, x3, r.unsqueeze(2).broadcast_to([128, nh, hd]), ALU.mult)
            return v(V.tensor_tensor, [o, l_small], x3, x3, w.unsqueeze(1).broadcast_to([128, nh, hd]), ALU.mult)

        def qk_pair(x, nh, hd, hf, r0, cos, sin, w, deps, sq, left, out_):
            n = nh * hd
            st_ = {}

            def first():
                o = s(A.activation, [deps] + left[0], sq[:, 0:n], x, ACT.Square)
                st_["r"] = col(nh)
                o = v(V.tensor_reduce, [o], st_["r"], sq[:, 0:n].rearrange("p (h d) -> p h d", h=nh), X_, ALU.add)
                left[0] = [o]
                st_["o"] = rsqrt(st_["r"], [o], 1.0 / hd, 1e-6)

            def second():
                x3 = x.rearrange("p (h d) -> p h d", h=nh)
                o = v(V.tensor_tensor, [st_["o"]], x3, x3, st_["r"].unsqueeze(2).broadcast_to([128, nh, hd]), ALU.mult)
                if w is not None:
                    o = v(V.tensor_tensor, [o, l_small], x3, x3, w.unsqueeze(1).broadcast_to([128, nh, hd]), ALU.mult)
                o = rope_at(x3[:, :, r0:r0 + 2 * hf], cos, sin, nh, hf, [o], tb_w if w is None else ())
                if w is None:
                    tb_left.append(o)
                out_.append(o)

            return first, second

        def weave(gen, steps):
            steps = list(steps)
            for _ in gen:
                yield
                if steps:
                    for f in steps.pop(0):
                        f()
                    yield
            for fs in steps:
                for f in fs:
                    f()
                yield

        buf = {"n": 0}
        e_free = [[], []]
        p_free = [[], []]

        def attention(units, scale, filler=None, steps=1):
            n = len(units)

            def scores(u):
                u["ps"] = []
                u["off"] = []
                off = 0
                for segs in u["banks"]:
                    b, bw = take()
                    c = 0
                    cols = []
                    first = True
                    for lhsT, rhs, nk, masks in segs:
                        op = m((u["deps"] + bw) if first else [], b[:, c:c + nk], lhsT, rhs,
                               start=True, stop=True)
                        first = False
                        for j, (c0, w, mk) in enumerate(masks):
                            op = m([l_cstb] + u.get("mdeps", []), b[:, c + c0:c + c0 + w], identb, mk, start=False,
                                   stop=True, skip_group_check=True)
                        cols.append((c, nk, off))
                        c += nk
                        off += nk
                    u["ps"].append((b, cols, op))

            def maxes(u):
                nseg = sum(len(c) for _, c, _ in u["ps"])
                mx = col(nseg)
                k = 0
                for b, cols, op in u["ps"]:
                    nk = cols[0][1]
                    o = v(V.tensor_reduce, [op], mx[:, k:k + len(cols)],
                          b[:, 0:nk * len(cols)].rearrange("p (n k) -> p n k", k=nk), X_, ALU.max)
                    k += len(cols)
                if u["joint"] and nseg > 1:
                    m1 = col(1)
                    o = v(V.tensor_reduce, [o], m1, mx, X_, ALU.max)
                    mx = m1
                nb = col(mx.shape[1])
                o = v(V.tensor_scalar, [o], nb, mx, -scale, None, ALU.mult)
                i = buf["n"] % 2
                buf["n"] += 1
                u["i"] = i
                k = 0
                if u["joint"]:
                    sums = col(nseg)
                else:
                    sums = u["sums"]
                for b, cols, op in u["ps"]:
                    for c, nk, off in cols:
                        bi = nb[:, 0:1] if u["joint"] else nb[:, k:k + 1]
                        so = sums[:, k:k + 1] if u["joint"] else sums[k]
                        x = s(A.activation, [o] + (e_free[i] if k == 0 else []), E[:, i, off:off + nk],
                              b[:, c:c + nk], ACT.Exp, bias=bi, scale=scale, accum_out=so)
                        k += 1
                    give(b, [x])
                u["x"] = x
                if u["joint"]:
                    u["x2"] = v(V.tensor_reduce, [x], u["sums"][0], sums, X_, ALU.add)
                if u["diff"]:
                    u["diff"](u)

            def turns(u):
                i = u["i"]
                tb = u["blocks"]
                ops = turn([E[:, i, c:c + 128] for c in tb], [u["x"]] + p_free[i],
                           lambda a, c: PET[:, i, a * 128:(a + c) * 128].rearrange("p (n q) -> p n q", n=c))
                u["t"] = ops
                e_free[i] = [ops[-1]]

            def values(u):
                i = u["i"]
                for okey, c0, dv, lst in u["outs"]:
                    ob, ow = okey["bank"]
                    for j, (blk, vap) in enumerate(lst):
                        op = m(u["t"] + ow + u["vdeps"], ob[:, c0:c0 + dv], PET[:, i, blk * 128:blk * 128 + 128], vap,
                               start=(j == 0), stop=(j == len(lst) - 1))
                    okey["op"] = op
                    okey["left"] -= 1
                    if okey["left"] == 0:
                        okey["done"]()
                p_free[i] = [op]

            for k in range(n + 2):
                if k < n:
                    for okey, *_ in units[k]["outs"]:
                        if "bank" not in okey:
                            okey["bank"] = take()
                    scores(units[k])
                    maxes(units[k])
                if 1 <= k <= n:
                    turns(units[k - 1])
                if filler is not None:
                    for _ in range(steps if isinstance(steps, int) else steps[k]):
                        next(filler, None)
                if k >= 2:
                    values(units[k - 2])

        def okey(n, done):
            return {"left": n, "done": done}

        def normalise(ob, dst, sums, nh, dv, key):
            def done():
                r = col(nh)
                sdeps = key["sdeps"]() if "sdeps" in key else []
                o = v(V.reciprocal, [key["op"]] + sdeps, r, sums)
                o = v(V.tensor_tensor, [o], dst, key["bank"][0][:, 0:nh * dv].rearrange("p (h d) -> p h d", h=nh),
                      r.unsqueeze(2).broadcast_to([128, nh, dv]), ALU.mult)
                give(key["bank"][0], [o])
                key["out"] = o
            return done

        def residual(b, c, t, waits):
            xs = X[:, t, c * 512:c * 512 + 512]
            return v(V.scalar_tensor_tensor, waits, out=xs, in0=xs, scalar=ALPHA, in1=b[:, :],
                     op0=ALU.mult, op1=ALU.add)

        def chain(*gens):
            for ge in gens:
                yield from ge

        vec_left = [[], [], []]
        x_w = [[l_x], [l_x]]
        mid_in = None
        gb_free = xt_w[0] + xt_w[1]
        sel_left, pt_left, mix_left, t_pe = [], [], [[], []], []

        def ln_tile(t, waits, gam, bet, vw, between=None):
            sts, mv = col(12), col(2)
            for j in range(2):
                o = v(V.bn_stats, waits, sts[:, 6 * j:6 * j + 6], X[:, t, j * 512:j * 512 + 512])
            o = v(V.bn_aggr, [o], mv, sts.rearrange("p (c k) -> p c k", k=6))
            r = rsqrt(mv[:, 1:2], [o], 1.0, 1e-5)
            if between:
                between()
            xs = X[:, t, :]
            o = v(V.scalar_tensor_tensor, [r] + vw, out=xs, in0=xs, scalar=mv[:, 0:1], in1=gam,
                  op0=ALU.subtract, op1=ALU.mult)
            return [v(V.scalar_tensor_tensor, [o], out=xs, in0=xs, scalar=mv[:, 1:2], in1=bet,
                      op0=ALU.mult, op1=ALU.add)]

        hn = [None, None]

        def norm_tile(t, waits):
            ss = col(1)
            o = s(A.activation, waits, MIX[:, t, :], X[:, t, :], ACT.Square, accum_out=ss)
            o = rsqrt(ss, [o], 1.0 / D, 1e-6)
            hn[t] = [v(V.tensor_scalar, [o], MIX[:, t, :], X[:, t, :], ss, None, ALU.mult)]

        def lambdas():
            lv = sm["diff_lambda_2"].rearrange("p (a b d) -> p a b d", a=2, b=2)
            lt = col(2)
            o = v(V.tensor_tensor, [l_small] + scr["last"], SCR[:, 0:128].rearrange("p (a d) -> p a d", a=2), lv[:, :, 0, :],
                  lv[:, :, 1, :], ALU.mult)
            o = v(V.tensor_reduce, [o], lt, SCR[:, 0:128].rearrange("p (a d) -> p a d", a=2), X_, ALU.add)
            scr["last"] = [o]
            o = s(A.activation, [o], lt, lt, ACT.Exp)
            o = v(V.tensor_tensor, [o], lam[:, 0:1], lt[:, 0:1], lt[:, 1:2], ALU.subtract)
            w_lam = v(V.tensor_scalar, [o], lam[:, 1:2], lam[:, 0:1], LAM, -1.0, ALU.add, ALU.mult)
            subl = sm["diff_subln_2"]
            w_sub = v(V.tensor_scalar, [l_small], subl, subl, 1.0 - LAM, None, ALU.mult)
            return w_lam, w_sub, subl

        def norm_mod(layer, k, left):
            ncol = colv[:, K_NRM + layer * 16 + k * 8:K_NRM + layer * 16 + k * 8 + 8]
            scl = modc[:, layer, 24 * k + 8:24 * k + 16]
            shf = modc[:, layer, 24 * k:24 * k + 8]
            assert len(mod_w[(layer, 3 * k)]) == 2 and len(mod_w[(layer, 3 * k + 1)]) == 2
            wa = v(V.scalar_tensor_tensor, mod_w[(layer, 3 * k + 1)], out=scl, in0=scl, scalar=1.0, in1=ncol,
                   op0=ALU.add, op1=ALU.mult)
            sw = [wa] + mod_w[(layer, 3 * k)] + left
            HM = H[:, :, :].rearrange("p t n -> p (t n)")[:, 0:2048].rearrange("p (k n) -> p k n", k=8) if k else GBT
            res = [[], []]

            def go(t):
                last = []
                for a in (0, 4):
                    b, bw = take()
                    for j in range(4):
                        op = Q.add("pe", M.transpose, (hn[t] + bw) if j == 0 else [], b[:, j * 128:j * 128 + 128],
                                   MIX[:, t, (a + j) * 128:(a + j) * 128 + 128], ident)
                    ls = []
                    for j in range(4):
                        kt = a + j
                        dst = HM[:, kt, t * 128:t * 128 + 128]
                        src = b[:, j * 128:j * 128 + 128]
                        if a == 0:
                            ls.append(s(A.activation, [op] + sw, dst, src, ACT.Identity,
                                        bias=shf[:, kt:kt + 1], scale=scl[:, kt:kt + 1]))
                        else:
                            ls.append(v(V.tensor_scalar, [op] + sw, dst, src, scl[:, kt:kt + 1],
                                        shf[:, kt:kt + 1], ALU.mult, ALU.add))
                    give(b, ls)
                    _, lo = split(HM[:, a:a + 4, t * 128:t * 128 + 128], XTH[:, a:a + 4, t * 128:t * 128 + 128],
                                  XTL[:, a:a + 4, t * 128:t * 128 + 128], ls)
                    last.append(lo)
                res[t][:] = last

            return res, go

        for i in range(2):
            vb = i * 5120
            SGW = T[:, 9:13, :].rearrange("p a b -> p (a b)").rearrange("p (g t) -> p g t", g=8)
            PR = T[:, 13:15, :]
            hw = [[], []]
            cuts = ((0, 364), (364, 728), (728, 1092))
            puts = []
            for a, b in cuts:
                def put(t, bk, op, a=a, b=b):
                    o = copy("act", [op], H[:, t, a:b], bk[:, 0:b - a])
                    hw[t].append(o)
                    return [o]
                puts.append(put)
            if i:
                run(linear2("w_in", xt, xt_w, puts[0:2], mid_in))
            else:
                run(linear("w_in", xt, xt_w, puts[0], touter=True))
                run(linear("w_in", xt, xt_w, puts[1]))
            run(linear("w_in", xt, xt_w, puts[2]))
            l_vs = pld("vec2", VEC[:, 2048:3072], bc(vecd[vb + 4096:vb + 5120]), vec_left[2] + hw[0][0:1])
            l_sgw = pld("sgw", SGW, sgwd[i].rearrange("p (g t) -> p g t", g=8), t_pe)
            l_pT = pld("pT", PR, pTd[i].rearrange("p (k n) -> p k n", k=2), t_pe)
            l_v1 = [pld("vec0", VEC[:, 0:1024], bc(vecd[vb:vb + 1024]), vec_left[0]),
                    pld("vec1", VEC[:, 1024:2048], bc(vecd[vb + 1024:vb + 2048]), vec_left[1])]
            kd = [None, None]
            KD = MIX[:, :, 0:384].rearrange("p t (a b d) -> p t a b d", a=3, b=2)
            gw = [[], []]

            def gelus():
                for c in range(2):
                    def put(t, bk, op, c=c):
                        o = s(A.activation, [op] + gb_free, GB[:, t, c * 512:c * 512 + 512], bk[:, :],
                              ACT.Gelu_apprx_tanh)
                        gw[t].append(o)
                        return [o]
                    yield from linear("w_in", xt, xt_w, put)

            fill = gelus()
            kx = [None, None]
            for t in range(2):
                cs, sn = COS[:, t, 0:8], SIN[:, t, 0:8]
                o2 = rope_at(H[:, t, 768:1088].rearrange("p (h d) -> p h d", d=64)[:, :, 0:16], cs, sn, 5, 8, hw[t])
                k2 = v(V.tensor_copy, [o2] + mix_left[t], KD[:, t, 2, :, :], H[:, t, 1024:1088].unsqueeze(1)
                       .broadcast_to([128, 2, 64]))
                wi = H[:, t, 1088:1092]
                kd[t] = v(V.tensor_scalar, [o2], wi, wi, 1.0 / 16.0, None, ALU.mult)
                o1 = rope_at(H[:, t, 0:640].rearrange("p (h d) -> p h d", d=64)[:, :, 0:16], cs, sn, 10, 8, hw[t])
                k1 = v(V.tensor_copy, [o1], KD[:, t, 0:2, :, :], H[:, t, 512:640].rearrange("p (a d) -> p a d", a=2)
                       .unsqueeze(2).broadcast_to([128, 2, 2, 64]))
                kx[t] = [k1, k2]
            next(fill, None)
            tw = []
            for t in range(2):
                src = ([H[:, t, j * 128:j * 128 + 128] for j in range(4)]
                       + [MIX[:, t, j * 128:j * 128 + 128] for j in range(2)]
                       + [H[:, t, 768 + j * 128:896 + j * 128] for j in range(2)] + [MIX[:, t, 256:384]])
                tw += turn(src, kx[t] + t_pe, lambda a, c, t=t: T[:, a:a + c, t * 128:t * 128 + 128])

            sel_w = [None, None]
            SCs = [SCR[:, 0:128], SCR[:, 256:512]]
            last = [None, None]
            for t in range(2):
                nk = 128 * (t + 1)
                SC = SCs[t]
                o = v(V.tensor_copy, scr["last"] + [l_cst], SC[:, nk - 128:nk], cst[:, C_CM:C_CM + 128])
                acc = [o]
                if t:
                    acc.append(v(V.memset, scr["last"], SC[:, 0:128], 0.0))
                for par in range(2):
                    b, bw = take()
                    for n_, h in enumerate((par, par + 2)):
                        mm = m(tw + bw, b[:, n_ * nk:n_ * nk + nk],
                               T[64 * par:64 * par + 64, 6 + h // 2, t * 128:t * 128 + 128],
                               T[64 * par:64 * par + 64, 8, 0:nk], start=True, stop=True)
                    rl = s(A.activation, [mm] + e_free[par], E[:, par, 0:2 * nk], b[:, 0:2 * nk], ACT.Relu)
                    give(b, [rl])
                    for n_, h in enumerate((par, par + 2)):
                        o = v(V.scalar_tensor_tensor, [rl, kd[t]] + acc, out=SC, in0=E[:, par, n_ * nk:n_ * nk + nk],
                              scalar=H[:, t, 1088 + h:1089 + h], in1=SC, op0=ALU.mult, op1=ALU.add)
                        acc = [o]
                    e_free[par] = [o]
                last[t] = o
            WK = [[SCR[:, 128:256], SCR[:, 0:128]], [SCR[:, 512:768], SCR[:, 256:512]]]
            src = list(SCs)
            for rnd in range(8):
                mx8 = [col(8), col(8)]
                for t in range(2):
                    last[t] = v(V.max, [last[t]], mx8[t], src[t])
                for t in range(2):
                    d_ = WK[t][rnd % 2]
                    last[t] = v(V.match_replace, [last[t]], d_, mx8[t], src[t], -3e38)
                    src[t] = d_
                if rnd % 2:
                    next(fill, None)
            for t in range(2):
                nk = 128 * (t + 1)
                sel_w[t] = v(V.tensor_scalar, [last[t]] + sel_left, selb[:, t, 0:nk], src[t], -2e38, -BIG, ALU.is_gt,
                             ALU.mult)
            scr["last"] = list(sel_w)
            run(fill)
            vsw = layer_norms([GB[:, t, 512:1024] for t in range(2)], 512, VEC[:, 2048:2560], VEC[:, 2560:3072], gw,
                              [l_vs])
            vec_left[2] = list(vsw)
            sp_ = split(PR, PTH[:, :, :], PTL[:, :, :], [l_pT] + pt_left)

            SM = [col(8), col(8)]
            keys_, units = [], []
            for t in range(2):
                nk = 128 * (t + 1)
                ok = okey(8, None)
                ok["done"] = normalise(None, MIX[:, t, 0:512].rearrange("p (h d) -> p h d", h=8), SM[t], 8, 64, ok)
                keys_.append(ok)
                per = 4 // (t + 1)
                for par in range(2):
                    hs = [par + 2 * j for j in range(4)]
                    for a in range(0, 4, per):
                        hh = hs[a:a + per]
                        segs = [(T[64 * par:64 * par + 64, h // 2, t * 128:t * 128 + 128],
                                 T[64 * par:64 * par + 64, 4 + h // 4, 0:nk], nk, [(0, nk, selb[:, t, 0:nk])])
                                for h in hh]
                        outs = [(ok, h * 64, 64, [(n_ * (t + 1) + kb, H[:, kb, 640 + (h // 4) * 64:704 + (h // 4) * 64])
                                                  for kb in range(t + 1)]) for n_, h in enumerate(hh)]
                        units.append(dict(banks=[segs], joint=False, diff=None, deps=tw, mdeps=[sel_w[t]],
                                          vdeps=hw[0] + hw[1],
                                          sums=[SM[t][:, h:h + 1] for h in hh], outs=outs,
                                          blocks=[c * 128 for c in range(per * (t + 1))]))

            sgo = []

            def gating():
                yield
                wm = v(V.tensor_tensor, [l_sgw, l_cst], SGW, SGW,
                       cst[:, C_TRI:C_TRI + 128].unsqueeze(1).broadcast_to([128, 8, 128]), ALU.mult)
                for gh in range(2):
                    b, bw = take()
                    for gg in range(4):
                        gr = gh * 4 + gg
                        mm = m([wm] + vsw + bw, b[:, gg * 128:gg * 128 + 128], SGW[:, gr, :],
                               GB[:, :, 512 + gr * 64:576 + gr * 64], start=True, stop=True)
                    for gg in range(4):
                        gr = gh * 4 + gg
                        o = v(V.scalar_tensor_tensor, [mm, l_colv], out=MIX[:, :, 512 + gr * 64:576 + gr * 64],
                              in0=b[:, gg * 128:gg * 128 + 128].rearrange("p (t d) -> p t d", t=2),
                              scalar=colv[:, K_SGB + i * 8 + gr:K_SGB + i * 8 + gr + 1],
                              in1=GB[:, :, gr * 64:gr * 64 + 64], op0=ALU.add, op1=ALU.mult)
                    give(b, [o])
                    sgo.append(o)
                    yield
            rw = [[], []]
            x_o, x_n = x_w, [None, None]
            mo = [[], []]
            tail = {"go": False}

            xt_n = [[], []]

            def put_o(c):
                def put(t, bk, op):
                    if c and t:
                        xt_n[0][:] = to_XT(X, 8, x_n[0], 0)
                    r_ = residual(bk, c, t, [op] + x_o[t])
                    rw[t].append(r_)
                    return [r_]
                return put

            def out_start():
                while "out" not in keys_[0]:
                    yield
                mo[0][:] = to_XT(MIX, 8, [keys_[0]["out"], sgo[-1]], 0)
                yield
                yield from linear("w_o", xt, mo, put_o(0), touter=True, guard=lambda: tail["go"],
                                  mid=lambda: mo[1].extend(to_XT(MIX, 8, [keys_[1]["out"], sgo[-1]], 1)))

            fill = chain(gating(), out_start())
            attention(units, 0.125, fill)
            tail["go"] = True
            run(fill)
            t_pe = [keys_[1]["op"]]
            sel_left = [keys_[1]["op"]]
            o = sgo[-1]

            run(linear("w_o", xt, mo, put_o(1), touter=True, mid=lambda: x_n.__setitem__(
                0, ln_tile(0, rw[0], VEC[:, 0:1024], VEC[:, 1024:2048], l_v1))))
            x_n[1] = ln_tile(1, rw[1], VEC[:, 0:1024], VEC[:, 1024:2048], l_v1)
            x_w = x_n
            vec_left[0] = vec_left[1] = x_w[0] + x_w[1]
            l_v2 = [pld("vec0", VEC[:, 0:1024], bc(vecd[vb + 2048:vb + 3072]), vec_left[0]),
                    pld("vec1", VEC[:, 1024:2048], bc(vecd[vb + 3072:vb + 4096]), vec_left[1])]
            xt_w = xt_n
            pw = [[], []]
            for c in range(2):
                def put(t, bk, op, c=c):
                    o1 = s(A.activation, [op, o], GB[:, t, c * 512:c * 512 + 512], bk[:, :], ACT.Copy)
                    pw[t].append(o1)
                    return [o1]
                run(linear("w_ple", lambda kt, t: (PTH[:, kt, t * 128:t * 128 + 128], PTL[:, kt, t * 128:t * 128 + 128]),
                           [[sp_[1]], [sp_[1]]], put))

            def mid1():
                xt_w[1][:] = to_XT(X, 8, x_w[1], 1)

            x_w2 = [[], []]
            def put_g(c):
                def put(t, bk, op):
                    ms = MIX[:, t, c * 512:c * 512 + 512]
                    o0 = s(A.activation, [op], ms, bk[:, :], ACT.Sigmoid)
                    o1 = v(V.tensor_tensor, [o0, pw[t][c]], ms, ms, GB[:, t, c * 512:c * 512 + 512], ALU.mult)
                    xs = X[:, t, c * 512:c * 512 + 512]
                    o2 = v(V.scalar_tensor_tensor, [o1] + x_w[t] + xt_w[t], out=xs, in0=xs, scalar=ALPHA, in1=ms,
                           op0=ALU.mult, op1=ALU.add)
                    x_w2[t].append(o2)
                    return [o0]
                return put

            run(linear2("w_ple_gate", xt, xt_w, [put_g(0), put_g(1)], mid1))
            x_w = x_w2
            mix_left = [list(x_w[0]), list(x_w[1])]
            f_left = [list(x_w[0]) + list(x_w[1]) + [o]] * 2
            ht_left = [list(t_pe), list(t_pe)]
            acc4 = None
            fw = {}
            for c in range(12):
                if c < 11:
                    fw[c] = []

                    def put(t, bk, op, c=c):
                        gs = GB[:, t, 512 + (c % 2) * 256:768 + (c % 2) * 256]
                        fs = GB[:, t, (c % 2) * 256:(c % 2) * 256 + 256]
                        a1 = s(A.activation, [op] + f_left[c % 2], gs, bk[:, 0:256], ACT.Silu)
                        a2 = v(V.tensor_tensor, [a1], fs, gs, bk[:, 256:512], ALU.mult)
                        fw[c].append(a2)
                        return [a2]
                    gen = linear("w_ffn_in", xt, xt_w, put)
                    next(gen)
                if c:
                    d = c - 1
                    b, bw = take()
                    for q in range(4):
                        kt, t = q // 2, q % 2
                        op = Q.add("pe", M.transpose, (fw[d] + bw) if q == 0 else [], b[:, q * 128:q * 128 + 128],
                                   GB[:, t, (d % 2) * 256 + kt * 128:(d % 2) * 256 + kt * 128 + 128], ident)
                    r2 = 2 * (d % 4)
                    _, lo = split(b[:, :].rearrange("p (n q) -> p n q", n=2), HTH[:, r2:r2 + 2, :],
                                  HTL[:, r2:r2 + 2, :], [op] + ht_left[d % 2])
                    give(b, [lo])
                    f_left[d % 2] = [op] + fw[d]
                if c < 11:
                    run(gen)
                if c:
                    if acc4 is None:
                        acc4 = [[take(), take()], [take(), take()]]
                    part_ = (lambda kt, t, r2=r2: (HTH[:, r2 + kt, t * 128:t * 128 + 128],
                                                   HTL[:, r2 + kt, t * 128:t * 128 + 128]), [lo])
                    if d < 9:
                        ops = partial("w_ffn_out", [part_], acc4, d == 0, False)
                        ht_left[d % 2] = [ops[1][1]]
                    elif d == 9:
                        part9 = part_
            x_o, x_n = x_w, [None, None]
            gb_free = [op] + fw[10]
            if i == 0:
                xt_w = [[], []]

                def mid_in():
                    xt_w[1][:] = to_XT(X, 8, x_w[1], 1)
            else:
                w_lam, w_sub, subl = lambdas()
                xt_w, go = norm_mod(0, 0, gb_free)

            def last(t, ops_):
                rw_ = []
                for c in range(2):
                    xs = X[:, t, c * 512:c * 512 + 512]
                    o_ = v(V.tensor_tensor, [ops_[c]] + x_o[t], xs, xs, acc4[t][c][0][:, :], ALU.add)
                    give(acc4[t][c][0], [o_])
                    rw_.append(o_)

                def between():
                    if t and i == 0:
                        xt_w[0][:] = to_XT(X, 8, x_n[0], 0)
                    elif t:
                        norm_tile(0, x_n[0])
                        go(0)

                x_n[t] = ln_tile(t, rw_, VEC[:, 0:1024], VEC[:, 1024:2048], l_v2, between)
                if t:
                    advance(1)
                if t and i == 1:
                    norm_tile(1, x_n[1])

            ops = partial("w_ffn_out", [part9, part_], acc4, False, True, last)
            t_pe = [ops[1][1]]
            pt_left = list(t_pe)
            x_w = x_n
            vec_left[0] = vec_left[1] = x_w[0] + x_w[1]
            vg["left"] = [list(vec_left[0]), list(vec_left[0])]
        def gain(layer, k, hf, buf, left):
            assert len(mod_w[(layer, 3 * k + 2)]) == 2
            if hf == 0:
                vg["w"][k] = []
            c0 = 24 * k + 16 + hf * 4
            o = v(V.tensor_tensor, [l_cst] + mod_w[(layer, 3 * k + 2)] + left[0],
                  buf.rearrange("p (a n) -> p a n", a=4), ident.unsqueeze(1).broadcast_to([128, 4, 128]),
                  modc[:, layer, c0:c0 + 4].unsqueeze(2).broadcast_to([128, 4, 128]), ALU.mult)
            b, bw = take()
            op = m([o] + bw, b[:, :], ones, buf, start=True, stop=True)
            left[0] = [op]
            r = s(A.activation, [op] + vg["left"][k], VG[:, k, hf * 512:hf * 512 + 512], b[:, :], ACT.Copy)
            give(b, [r])
            vg["w"][k].append(r)

        def gated_put(c, k, xg):
            def put(t, bk, op):
                ms = MIX[:, t, c * 512:c * 512 + 512]
                o1 = v(V.tensor_tensor, [op] + vg["w"][k] + (xo_w[t] if k == 0 else []), ms, bk[:, :],
                       VG[:, k, c * 512:c * 512 + 512], ALU.mult)
                vg["left"][k] = [o1]
                xs = X[:, t, c * 512:c * 512 + 512]
                xg[t].append(v(V.tensor_tensor, [o1] + x_w[t], xs, xs, ms, ALU.add))
                return [o1]
            return put

        def put_H(a, b, lst, waits=()):
            def put(t, bk, op):
                o = copy("act", [op] + list(waits), H[:, t, a:b], bk[:, 0:b - a])
                lst[t].append(o)
                return [o]
            return put

        table, tb_w, tb_left = {}, [], list(pt_left)

        def tables(names):
            del tb_w[:]
            for n, nm in enumerate(names):
                for t in range(2):
                    pair = []
                    for j, tr in enumerate((COS, SIN)):
                        dst = TB[:, n, t, j, :].rearrange("p (a f) -> p a f", a=2)
                        tb_w.append(g(G.tensor_tensor, [w_trig, l_small] + tb_left, dst,
                                      tr[:, t, 8:40].unsqueeze(1).broadcast_to([128, 2, 32]),
                                      sm[nm].rearrange("p (a f) -> p a f", a=2), ALU.mult))
                        pair.append(dst)
                    table[n, t] = pair

        for i in range(2):
            mid = (lambda go=go: go(1))
            gb_x = xt_w
            tables(("dil_q_norm_2", "dil_k_norm_2") if i == 0 else
                   ("diff_q_norm_2", "diff_k_norm_2", "moba_q_norm_2", "moba_k_norm_2"))
            if i == 0:
                MQ = H[:, :, 2304:3072]
                MK = GB[:, :, 0:768]
                lw = [[], []]
                puts = []
                for a, b in ((0, 384), (384, 672)):
                    def put(t, bk, op, a=a, b=b):
                        o = copy("act", [op] + xt_w[t], MIX[:, t, a:b], bk[:, 0:b - a])
                        lw[t].append(o)
                        return [o]
                    puts.append(put)
                run(linear2("even_w_in_2", xt, xt_w, puts, mid))
                lnw = [[], []]
                for t in range(2):
                    for a, n_, nm in ((0, 384, "mla_q_lat_norm_2"), (384, 256, "mla_kv_lat_norm_2")):
                        xs = MIX[:, t, a:a + n_]
                        ss = col(1)
                        o = s(A.activation, lw[t] + scr["last"], SCR[:, 0:n_], xs, ACT.Square, accum_out=ss)
                        scr["last"] = [o]
                        o = rsqrt(ss, [o], 1.0 / n_, 1e-6)
                        lnw[t].append(v(V.scalar_tensor_tensor, [o, l_small], out=xs, in0=xs, scalar=ss, in1=sm[nm],
                                        op0=ALU.mult, op1=ALU.mult))
                ltw = [turn_halves([MIX[:, t, k * 128:k * 128 + 128] for k in range(5)], lnw[t] + t_pe, HTH, HTL, t)
                       for t in range(2)]

                def lat(k0):
                    return lambda kt, t: (HTH[:, k0 + kt, t * 128:t * 128 + 128], HTL[:, k0 + kt, t * 128:t * 128 + 128])

                qw = [[], []]
                for c in range(2):
                    run(linear("mla_w_uq_2", lat(0), ltw, put_H(2304 + c * 384, 2688 + c * 384, qw)))
                kw = [[], []]
                gbr = gb_x[0] + gb_x[1]

                def put(t, bk, op):
                    k3 = MK[:, t, :].rearrange("p (h d) -> p h d", h=8)
                    o = copy("act", [op] + gbr, k3[:, :, 0:64], bk[:, :].rearrange("p (h d) -> p h d", h=8))
                    o3 = copy("dve", lw[t] + gbr, k3[:, :, 64:96],
                              MIX[:, t, 640:672].unsqueeze(1).broadcast_to([128, 8, 32]))
                    kw[t] = [o, o3]
                    return [o]
                run(linear("mla_w_ukv_2", lat(3), ltw, put))
                mvw = []

                def put(t, bk, op):
                    o = copy("act", [op] + vec_left[2], MV[:, t, :], bk[:, :])
                    mvw.append(o)
                    return [o]
                run(linear("mla_w_ukv_2", lat(3), ltw, put))
                dw = [[[], []] for _ in range(3)]

                def dils(*cs_):
                    for c in cs_:
                        yield from linear("even_w_in_2", xt, xt_w, put_H(c * 384, c * 384 + 384, dw[c // 2]))

                qkr = [[], []]
                ch = {}
                for c in range(4):
                    for t in range(2):
                        xs = H[:, t, c * 384:c * 384 + 384]
                        ch[c, t] = qk_pair(xs, 6, 64, 32, 0, *table[c // 2, t], None, dw[c // 2][t], SQ, sq_left, qkr[t])
                mch, mr = {}, {}
                el = [[e_free[0]], [e_free[1]]]
                for n, (x_, ww, nm) in enumerate(((MQ, qw, "mla_q_norm_2"), (MK, kw, "mla_k_norm_2"))):
                    for t in range(2):
                        mr[n, t] = []
                        mch[n, t] = qk_pair(x_[:, t, :], 8, 96, 16, 64, COS[:, t, 8:40:2], SIN[:, t, 8:40:2], sm[nm],
                                            ww[t], E[:, n, :], el[n], mr[n, t])
                gs = [lambda k=k, hf=hf: gain(i, k, hf, SQ[:, :], sq_left) for k in range(2) for hf in range(2)]
                run(weave(dils(4, 5, 0), [[mch[0, 0][0], mch[1, 0][0]], [gs[0], mch[0, 0][1], mch[0, 1][0]],
                                          [gs[1], mch[1, 0][1], mch[1, 1][0]], [gs[2], mch[0, 1][1]],
                                          [gs[3], mch[1, 1][1]]]))
                e_free[0], e_free[1] = el[0][0], el[1][0]
                tw = []
                for t in range(2):
                    for n, (x_, base) in enumerate(((MQ, 0), (MK, 8))):
                        tw += turn([x_[:, t, h * 96:h * 96 + 96] for h in range(8)], mr[n, t] + t_pe,
                                   lambda a, c, t=t, base=base: T[0:96, base + a:base + a + c, t * 128:t * 128 + 128],
                                   rows=96)
                fill = weave(dils(1, 2, 3), [[ch[0, 0][0]], [ch[0, 1][0], ch[0, 0][1]], [ch[0, 1][1], ch[1, 0][0]],
                                             [ch[1, 1][0], ch[1, 0][1]], [ch[1, 1][1], ch[2, 0][0]],
                                             [ch[2, 1][0], ch[2, 0][1]], [ch[2, 1][1], ch[3, 0][0]],
                                             [ch[3, 1][0], ch[3, 0][1]], [ch[3, 1][1]]])
                SMm = [col(8), col(8)]
                keys_, units = [], []
                mla_scale = 96 ** -0.5
                for t in range(2):
                    nk = 128 * (t + 1)
                    ok = okey(8, None)
                    ok["done"] = normalise(None, MIX[:, t, 0:512].rearrange("p (h d) -> p h d", h=8), SMm[t], 8, 64, ok)
                    keys_.append(ok)
                    per = 4 // (t + 1)
                    for a in range(0, 8, per):
                        hh = list(range(a, a + per))
                        segs = [(T[0:96, h, t * 128:t * 128 + 128], T[0:96, 8 + h, 0:nk], nk,
                                 [(nk - 128, 128, maskb(B_TRI))]) for h in hh]
                        outs = [(ok, h * 64, 64, [(n_ * (t + 1) + kb, MV[:, kb, h * 64:h * 64 + 64])
                                                  for kb in range(t + 1)]) for n_, h in enumerate(hh)]
                        units.append(dict(banks=[segs], joint=False, diff=None, deps=tw,
                                          vdeps=mvw, sums=[SMm[t][:, h:h + 1] for h in hh], outs=outs,
                                          blocks=[c * 128 for c in range(per * (t + 1))]))
                attention(units, mla_scale, fill, (3, 2, 2, 2, 2, 2, 1, 1))
                run(fill)
                t_pe = [keys_[1]["op"]]
                tw2 = []
                for t in range(2):
                    for x0, base in ((0, 0), (768, 6)):
                        tw2 += turn([H[:, t, x0 + h * 128:x0 + h * 128 + 128] for h in range(6)], qkr[t] + t_pe,
                                    lambda a, c, t=t, base=base: T[:, base + a:base + a + c, t * 128:t * 128 + 128])
                SMd = [col(4), col(4)]
                units = []
                xg, xo_w, tail = [[], []], [[], []], {"go": False}

                def out_start():
                    while "out" not in keys_[2]:
                        yield
                    xo_w[0][:] = to_XT(MIX, n_out, [keys_[0]["out"], keys_[2]["out"]], 0)
                    yield
                    yield from linear(nm_out, xt, xo_w, gated_put(0, 0, xg), touter=True, guard=lambda: tail["go"],
                                      mid=lambda: xo_w[1].extend(
                                          to_XT(MIX, n_out, [keys_[1]["out"], keys_[3]["out"]], 1)))

                n_out, nm_out = 6, "even_w_out_2"
                fill = out_start()
                for t in range(2):
                    nk = 128 * (t + 1)
                    ok = okey(4, None)
                    ok["done"] = normalise(None, MIX[:, t, 512:768].rearrange("p (h d) -> p h d", h=4), SMd[t], 4, 64, ok)
                    keys_.append(ok)
                    for h in range(4):
                        segs = []
                        for gp in range(3):
                            hd = gp * 4 + h
                            bs = 64 * (hd % 2)
                            mk = [(nk - 128, 128, maskb((B_TRI, B_TRI4, B_TRI16)[gp]))]
                            if t:
                                mk.append((0, 128, maskb((B_UP, B_M4, B_M16)[gp])))
                            segs.append((T[bs:bs + 64, hd // 2, t * 128:t * 128 + 128],
                                         T[bs:bs + 64, 6 + hd // 2, 0:nk], nk, mk))
                        outs = [(ok, h * 64, 64, [(gp * (t + 1) + kb,
                                                   H[:, kb, 1536 + (gp * 4 + h) * 64:1600 + (gp * 4 + h) * 64])
                                                  for gp in range(3) for kb in range(t + 1)])]
                        units.append(dict(banks=[segs[0:2], segs[2:3]], joint=True, diff=None, deps=tw2,
                                          vdeps=dw[2][0] + dw[2][1], sums=[SMd[t][:, h:h + 1]], outs=outs,
                                          blocks=[c * 128 for c in range(3 * (t + 1))]))
                attention(units, 0.125, fill)
                tail["go"] = True
                xt_w = xo_w
            else:
                dw = [[[], []] for _ in range(6)]

                def put(c):
                    return put_H(c * 512, c * 512 + 512, dw[c])

                def part(cs_):
                    for c in cs_:
                        yield from linear("odd_w_in_2", xt, xt_w, put(c))

                ch, cr = {}, {}
                for n, c in enumerate((0, 1, 3, 4)):
                    for t in range(2):
                        cr[c, t] = []
                        ch[c, t] = qk_pair(H[:, t, c * 512:c * 512 + 512], 8, 64, 32, 0, *table[n, t], None,
                                           dw[c][t], SQ, sq_left, cr[c, t])

                def turn_qk(c, t, base, lst):
                    lst.extend(turn([H[:, t, c * 512 + h * 128:c * 512 + h * 128 + 128] for h in range(4)],
                                    cr[c, t] + t_pe, lambda a, n: T[:, base + a:base + a + n, t * 128:t * 128 + 128]))

                el = [[e_free[0]], [e_free[1]]]
                gs = [lambda k=k, hf=hf: gain(i, k, hf, E[:, k, hf * 512:hf * 512 + 512], el[k])
                      for k in range(2) for hf in range(2)]
                run(weave(chain(linear2("odd_w_in_2", xt, xt_w, [put(0), put(1)], mid), part((2, 3))),
                          [[ch[0, 0][0]], [gs[0], ch[0, 1][0], ch[0, 0][1]], [gs[1], ch[0, 1][1], ch[1, 0][0]],
                           [gs[2], ch[1, 1][0], ch[1, 0][1]], [gs[3], ch[1, 1][1]]]))
                e_free[0], e_free[1] = el[0][0], el[1][0]
                tw, twm = [], []
                for c in range(2):
                    for t in range(2):
                        turn_qk(c, t, 4 * c, tw)
                fill = weave(part((4, 5)), [[ch[3, 0][0]], [ch[3, 1][0], ch[3, 0][1]], [ch[3, 1][1], ch[4, 0][0]],
                                            [ch[4, 1][0], ch[4, 0][1]], [ch[4, 1][1]]]
                             + [[lambda c=c, t=t: turn_qk(c, t, 4 * c - 4, twm)] for c in (3, 4) for t in range(2)])
                units, keys_ = [], []

                def differ(u):
                    i_, t, nk = u["i"], u["tt"], u["nk"]
                    r4 = col(4)
                    o = v(V.reciprocal, [u["x"]], r4, u["s4"])
                    c2_ = col(2)
                    o = v(V.tensor_scalar, [o, w_lam], c2_, r4[:, 2:4], lam[:, 1:2], None, ALU.mult)
                    for n_ in range(2):
                        e1 = E[:, i_, (2 + n_) * nk:(3 + n_) * nk]
                        o1 = v(V.tensor_scalar, [o], e1, e1, c2_[:, n_:n_ + 1], None, ALU.mult)
                    for n_ in range(2):
                        e0 = E[:, i_, n_ * nk:n_ * nk + nk]
                        e1 = E[:, i_, (2 + n_) * nk:(3 + n_) * nk]
                        o1 = v(V.scalar_tensor_tensor, [o1], out=e0, in0=e0, scalar=r4[:, n_:n_ + 1], in1=e1,
                               op0=ALU.mult, op1=ALU.add)
                    u["x"] = o1

                def diff_done(t, ok):
                    def done():
                        dst = MIX[:, t, 0:512]
                        b = ok["bank"][0]
                        o = s(A.activation, [ok["op"]], dst, b[:, :], ACT.Copy)
                        give(b, [o])
                        ok["out"] = head_rms(dst, 4, 128, subl, [o, w_sub])
                    return done

                for t in range(2):
                    nk = 128 * (t + 1)
                    ok = okey(4, None)
                    ok["done"] = diff_done(t, ok)
                    keys_.append(ok)
                    for a in (0, 2):
                        bks = []
                        for mp in range(2):
                            bks.append([(T[64 * mp:64 * mp + 64, h, t * 128:t * 128 + 128],
                                         T[64 * mp:64 * mp + 64, 4 + h, 0:nk], nk, [(nk - 128, 128, maskb(B_TRI))])
                                        for h in (a, a + 1)])
                        s4 = col(4)
                        outs = [(ok, h * 128, 128, [(n_ * (t + 1) + kb, H[:, kb, 1024 + h * 128:1152 + h * 128])
                                                    for kb in range(t + 1)]) for n_, h in enumerate((a, a + 1))]
                        units.append(dict(banks=bks, joint=False, diff=differ, deps=tw, vdeps=dw[2][0] + dw[2][1], s4=s4, tt=t, nk=nk,
                                          sums=[s4[:, j:j + 1] for j in range(4)], outs=outs,
                                          blocks=[c * 128 for c in range(2 * (t + 1))]))
                attention(units, 0.125, fill, (2, 3, 3, 3, 1, 1))
                run(fill)
                tw = twm
                SMb = [col(8), col(8)]
                units = []
                xg, xo_w, tail = [[], []], [[], []], {"go": False}
                n_out, nm_out = 8, "odd_w_out_2"
                fill = out_start()
                for t in range(2):
                    nk = 128 * (t + 1)
                    ok = okey(8, None)
                    ok["done"] = normalise(None, MIX[:, t, 512:1024].rearrange("p (h d) -> p h d", h=8), SMb[t], 8, 64,
                                           ok)
                    keys_.append(ok)
                    per = 4 // (t + 1)
                    for par in range(2):
                        hs = [par + 2 * j for j in range(4)]
                        for a in range(0, 4, per):
                            hh = hs[a:a + per]
                            segs = [(T[64 * par:64 * par + 64, 8 + h // 2, t * 128:t * 128 + 128],
                                     T[64 * par:64 * par + 64, 12 + h // 2, 0:nk], nk,
                                     [(nk - 128, 128, maskb(B_TRI))]) for h in hh]
                            outs = [(ok, h * 64, 64, [(n_ * (t + 1) + kb, H[:, kb, 2560 + h * 64:2624 + h * 64])
                                                      for kb in range(t + 1)]) for n_, h in enumerate(hh)]
                            units.append(dict(banks=[segs], joint=False, diff=None, deps=tw, vdeps=dw[5][0] + dw[5][1],
                                              sums=[SMb[t][:, h:h + 1] for h in hh], outs=outs,
                                              blocks=[c * 128 for c in range(per * (t + 1))]))
                attention(units, 0.125, fill)
                tail["go"] = True
                xt_w = xo_w
            t_pe = [keys_[3]["op"]]
            run(fill)
            x_o = x_w
            mod, go = norm_mod(i, 1, t_pe)
            gput = gated_put(1, 0, xg)

            def put(t, bk, op):
                if t:
                    go(0)
                r = gput(t, bk, op)
                if t:
                    advance(1)
                    norm_tile(1, xg[1])
                return r
            run(linear(nm_out, xt, xt_w, put, touter=True, mid=lambda: norm_tile(0, xg[0])))
            x_w = xg
            xt_w = mod
            mid = (lambda go=go: go(1))
            gb_free = list(t_pe)
            f_left = [gb_free, gb_free]
            ht_left = [list(t_pe), list(t_pe)]
            acc4 = None
            fw = {}
            FB = [GB[:, :, 0:512], GB[:, :, 512:1024]]

            def put_f(c):
                fw[c] = []

                def put(t, bk, op):
                    fs = FB[c % 2][:, t, :]
                    a1 = s(A.activation, [op] + f_left[c % 2], fs, bk[:, :], ACT.Relu)
                    fw[c].append(s(A.activation, [a1], fs, fs, ACT.Square))
                    return [a1]
                return put

            for c in range(9):
                if c == 0:
                    gen = linear2("mlp_w1_2", xt, xt_w, [put_f(0), put_f(1)], mid)
                    next(gen)
                    continue
                if 2 <= c < 8:
                    gen = linear("mlp_w1_2", xt, xt_w, put_f(c))
                    next(gen)
                if c:
                    d = c - 1
                    los = []
                    for hf in range(2):
                        b, bw = take()
                        for q in range(4):
                            kt, t = hf * 2 + q // 2, q % 2
                            op = Q.add("pe", M.transpose, (fw[d] + bw) if q == 0 else [], b[:, q * 128:q * 128 + 128],
                                       FB[d % 2][:, t, kt * 128:kt * 128 + 128], ident)
                        r2 = 4 * (d % 2) + 2 * hf
                        _, lo = split(b[:, :].rearrange("p (n q) -> p n q", n=2), HTH[:, r2:r2 + 2, :],
                                      HTL[:, r2:r2 + 2, :], [op] + ht_left[d % 2])
                        give(b, [lo])
                        los.append(lo)
                    f_left[d % 2] = [op]
                if c < 8:
                    run(gen)
                if c:
                    if acc4 is None:
                        acc4 = [[take(), take()], [take(), take()]]
                    r2 = 4 * (d % 2)
                    part_ = (lambda kt, t, r2=r2: (HTH[:, r2 + kt, t * 128:t * 128 + 128],
                                                   HTL[:, r2 + kt, t * 128:t * 128 + 128]), los)
                    if d < 7:
                        ops = partial("mlp_w2_2", [part_], acc4, d == 0, False)
                        ht_left[d % 2] = [ops[1][1]]
            xg = [[], []]

            if i == 0:
                mod, go = norm_mod(1, 0, [op] + fw[7])

            def last(t, ops_):
                if t and i == 0:
                    go(0)
                for c in range(2):
                    give(acc4[t][c][0], gated_put(c, 1, xg)(t, acc4[t][c][0], ops_[c]))
                if t:
                    advance(1)
                if i == 0:
                    norm_tile(t, xg[t])
                else:
                    Q.stores.append(Q.dma("sp", f"out{t}", Y.dma_start, xg[t], out[0, t * 128:t * 128 + 128, :],
                                          X[:, t, :]))

            ops = partial("mlp_w2_2", [part_], acc4, False, True, last)
            t_pe = [ops[1][1]]
            x_w = xg
            xt_w = mod
            gb_free = list(t_pe)
        Q.finish()
        block = ctx.enter_context(nc.Block())

        @block.sync
        def _(eng):
            Q.emit("sp", eng)

        @block.gpsimd
        def _(eng):
            Q.emit("pool", eng)

        @block.scalar
        def _(eng):
            Q.emit("act", eng)

        @block.vector
        def _(eng):
            Q.emit("dve", eng)

        @block.tensor
        def _(eng):
            Q.emit("pe", eng)


def constants():
    c = np.zeros((128, C_END), np.float32)
    q, k = np.arange(128)[:, None], np.arange(128)[None, :]
    c[:, C_ID:C_ID + 128] = np.eye(128)
    c[:, C_CM:C_CM + 128] = np.where(k // 64 <= q // 64, 0.0, -BIG)
    c[:, C_TRI:C_TRI + 128] = q <= k
    c[:, C_INV:C_INV + 8] = np.float32(500000.0) ** (np.float32(-2.0) * np.arange(8, dtype=np.float32) / np.float32(16))
    c[:, C_INV + 8:C_INV + 40] = np.float32(10000.0) ** (-np.arange(32, dtype=np.float32) / np.float32(32))
    c[:, C_HPI] = math.pi / 2
    c[:, C_MH] = -0.5
    c[:, C_ONE:C_ONE + 128] = 1.0
    b = np.zeros((128, 7, 128), np.float32)
    b[:, B_ID] = np.eye(128)
    for n, ok in ((B_TRI, k <= q), (B_UP, k >= q), (B_TRI4, (k <= q) & ((q - k) % 4 == 0)), (B_M4, (q - k) % 4 == 0),
                  (B_TRI16, (k <= q) & ((q - k) % 16 == 0)), (B_M16, (q - k) % 16 == 0)):
        b[:, n] = np.where(ok, 0.0, -BIG)
    return c, b.reshape(128, -1)


def kernel(**inputs):
    import concourse.bacc as _bacc
    from concourse.bass_utils import run_bass_kernel_spmd as _run

    a = {n: np.asarray(x) for n, x in inputs.items()}
    parts = []
    for name, i, (r0, r1), cols in plan():
        w = a[name][i]
        w = w.reshape(w.shape[0], -1)[r0:r1]
        k = r1 - r0
        w = np.concatenate([w[:, c0:c1] for c0, c1 in cols], axis=1)
        w = w.reshape(k // 128, 128, -1).transpose(1, 0, 2)
        for k0, n in pieces(k, w.shape[2]):
            parts.append(w[:, k0:k0 + n, :].reshape(-1))
    cst, cstb = constants()
    x = a["x"]
    arrays = {
        "W": np.concatenate(parts),
        "xd": x,
        "xTd": np.ascontiguousarray(x[0].T.reshape(8, 128, S).transpose(1, 0, 2).reshape(128, -1)),
        "pTd": np.ascontiguousarray(a["p"][:, 0].transpose(0, 2, 1).reshape(2, 2, 128, S).transpose(0, 2, 1, 3)
                                    .reshape(2, 128, -1)),
        "posd": np.ascontiguousarray(a["positions"].reshape(2, 128).T),
        "pos2d": np.ascontiguousarray(a["positions_2"].reshape(2, 128).T),
        "colvd": np.ascontiguousarray(np.concatenate(
            [a["ada_b_2"].reshape(96, 128), np.stack([a["norm_mix_2"], a["norm_mlp_2"]], 1).reshape(32, 128),
             a["c_2"].reshape(8, 128), a["sgu_b"].reshape(16, 128)]).T),
        "cstd": cst,
        "cstbd": cstb,
        "vecd": np.concatenate([a[n][i] for i in range(2) for n in
                                ("ln1_g", "ln1_b", "ln2_g", "ln2_b", "sgu_ln_g", "sgu_ln_b")]),
        "sgwd": np.ascontiguousarray(a["sgu_w"].transpose(0, 3, 1, 2).reshape(2, 128, 1024)),
        "smalld": np.concatenate([a[n].reshape(-1) for n, _ in SMALL]),
    }
    nc = _bacc.Bacc("TRN2", target_bir_lowering=False, num_devices=1)
    args = [nc.dram_tensor(n, x_.shape, mybir.dt.from_np(x_.dtype), kind="ExternalInput").ap()
            for n, x_ in arrays.items()]
    args.append(nc.dram_tensor("out", (1, S, D), F32, kind="ExternalOutput").ap())
    program(nc, *args)
    r = _run(nc, [arrays], core_ids=[0])
    return r.results[0]["out"]
```
